# Optimizing a Trainium2 kernel written in Bass

```python
import jax, jax.numpy as jnp
from jax import lax
import numpy as np

D_MODEL = 1024
BATCH = 1
SEQ = 2048
DEPTH = 1

CHUNK = 64
MIX_WIDTH = D_MODEL
ATTN_WIDTH = MIX_WIDTH // 2
HEAD_DIM = 64
N_Q_HEADS = ATTN_WIDTH // HEAD_DIM
N_KV_HEADS = 2
GQA_GROUP = N_Q_HEADS // N_KV_HEADS
WINDOW = 128
WINDOW_CHUNKS = WINDOW // CHUNK
ROPE_DIM = HEAD_DIM // 4
ROPE_THETA = 500000.0
HGRN_WIDTH = MIX_WIDTH - ATTN_WIDTH
HGRN_EXPAND = 128
HGRN_HEADS = HGRN_WIDTH // HGRN_EXPAND
HGRN_DK = HGRN_EXPAND
HGRN_DV = HGRN_WIDTH // HGRN_HEADS
D_FF = -(-8 * D_MODEL // (3 * 256)) * 256
RMS_EPS = 1e-6
NEG_INF = -1e30
Q_A = N_Q_HEADS * HEAD_DIM
KV_A = N_KV_HEADS * HEAD_DIM
IN_WIDTH = Q_A + 2 * KV_A + 4 * HGRN_WIDTH
SPLIT_POINTS = (Q_A, Q_A + KV_A, Q_A + 2 * KV_A, Q_A + 2 * KV_A + HGRN_WIDTH, Q_A + 2 * KV_A + 2 * HGRN_WIDTH, Q_A + 2 * KV_A + 3 * HGRN_WIDTH)

kernel_name = 'hymba_swa_sink_hgrn2_block'

def _rmsnorm(t, w):
    t32 = t.astype(jnp.float32)
    y = t32 * lax.rsqrt(jnp.mean(t32 * t32, axis=-1, keepdims=True) + RMS_EPS)
    return (y * w.astype(jnp.float32)).astype(t.dtype)

def _partial_rope(t, pos):
    half = ROPE_DIM // 2
    inv_freq = jnp.float32(ROPE_THETA) ** (-jnp.arange(half, dtype=jnp.float32) * 2.0 / ROPE_DIM)
    ang = pos.astype(jnp.float32)[:, None] * inv_freq[None, :]
    cos = jnp.cos(ang)[None, :, None, :]
    sin = jnp.sin(ang)[None, :, None, :]
    t32 = t.astype(jnp.float32)
    x1 = t32[..., :half]
    x2 = t32[..., half:ROPE_DIM]
    out = jnp.concatenate([x1 * cos - x2 * sin, x2 * cos + x1 * sin, t32[..., ROPE_DIM:]], axis=-1)
    return out.astype(t.dtype)

def _shift_chunks(t, s):
    if s == 0:
        return t
    return jnp.concatenate([jnp.zeros_like(t[:, :s]), t[:, :-s]], axis=1)

def _swa_sink_attention(q, k, v, q_norm_w, k_norm_w, sinks):
    B, S = q.shape[0], q.shape[1]
    NC = S // CHUNK
    pos = jnp.arange(S)
    q = _partial_rope(_rmsnorm(q.reshape(B, S, N_Q_HEADS, HEAD_DIM), q_norm_w), pos)
    k = _partial_rope(_rmsnorm(k.reshape(B, S, N_KV_HEADS, HEAD_DIM), k_norm_w), pos)
    v = v.reshape(B, S, N_KV_HEADS, HEAD_DIM)
    qc = q.reshape(B, NC, CHUNK, N_KV_HEADS, GQA_GROUP, HEAD_DIM)
    kc = k.reshape(B, NC, CHUNK, N_KV_HEADS, HEAD_DIM)
    vc = v.reshape(B, NC, CHUNK, N_KV_HEADS, HEAD_DIM)
    kw = jnp.concatenate([_shift_chunks(kc, WINDOW_CHUNKS - 1 - w) for w in range(WINDOW_CHUNKS)], axis=2)
    vw = jnp.concatenate([_shift_chunks(vc, WINDOW_CHUNKS - 1 - w) for w in range(WINDOW_CHUNKS)], axis=2)
    scores = jnp.einsum('bnqhgd,bnkhd->bnhgqk', qc, kw, preferred_element_type=jnp.float32) * (HEAD_DIM ** -0.5)
    chunk_idx = jnp.arange(NC)[:, None]
    slot = jnp.arange(WINDOW_CHUNKS * CHUNK)[None, :] // CHUNK
    valid = (chunk_idx - (WINDOW_CHUNKS - 1 - slot)) >= 0
    scores = jnp.where(valid[None, :, None, None, None, :], scores, NEG_INF)
    sink = sinks.astype(jnp.float32).reshape(N_KV_HEADS, GQA_GROUP)[None, None, :, :, None, None]
    m = jnp.maximum(jnp.max(scores, axis=-1, keepdims=True), sink)
    p = jnp.exp(scores - m)
    denom = jnp.sum(p, axis=-1, keepdims=True) + jnp.exp(sink - m)
    probs = (p / denom).astype(v.dtype)
    out = jnp.einsum('bnhgqk,bnkhd->bnqhgd', probs, vw)
    return out.reshape(B, S, ATTN_WIDTH).astype(q.dtype)

def _hgrn2(q, f, i, g, lb, g_norm_w):
    B, S = q.shape[0], q.shape[1]
    NC = S // CHUNK
    out_dtype = q.dtype

    def heads(t, d):
        return t.reshape(B, NC, CHUNK, HGRN_HEADS, d).transpose(0, 3, 1, 2, 4).astype(jnp.float32)

    qh = heads(jax.nn.silu(q), HGRN_DK)
    lb_h = lb.astype(jnp.float32).reshape(HGRN_HEADS, 1, 1, HGRN_DK)
    fg = lb_h + (1.0 - lb_h) * jax.nn.sigmoid(heads(f, HGRN_DK))
    kh = 1.0 - fg
    vh = heads(i, HGRN_DV)
    b = jnp.cumsum(jnp.log(fg), axis=3)
    ref = b[:, :, :, CHUNK // 2:CHUNK // 2 + 1, :]
    att = jnp.einsum('bhntd,bhnsd->bhnts', qh * jnp.exp(b - ref), kh * jnp.exp(ref - b))
    causal = jnp.tril(jnp.ones((CHUNK, CHUNK), dtype=bool))
    att = jnp.where(causal, att, 0.0)
    o_intra = jnp.einsum('bhnts,bhnsv->bhntv', att, vh)
    b_last = b[:, :, :, -1:, :]
    d_state = jnp.einsum('bhnsd,bhnsv->nbhdv', kh * jnp.exp(b_last - b), vh)
    decay = jnp.exp(b_last[:, :, :, 0, :]).transpose(2, 0, 1, 3)

    def step(state, inp):
        dec, ds = inp
        return dec[..., None] * state + ds, state

    init = jnp.zeros((B, HGRN_HEADS, HGRN_DK, HGRN_DV), jnp.float32)
    _, s_start = lax.scan(step, init, (decay, d_state))
    o_inter = jnp.einsum('bhntd,nbhdv->bhntv', qh * jnp.exp(b), s_start)
    o = _rmsnorm(o_intra + o_inter, g_norm_w)
    o = o.transpose(0, 2, 3, 1, 4).reshape(B, S, HGRN_WIDTH)
    return (o * jax.nn.silu(g.astype(jnp.float32))).astype(out_dtype)

def setup_inputs(seed: int = 0) -> dict:
    key = jax.random.key(seed)
    ks = jax.random.split(key, 12)

    def nrm(k, shape, scale):
        return jax.random.normal(k, shape, jnp.float32) * scale

    return {
        'x': nrm(ks[0], (BATCH, SEQ, D_MODEL), 1.0),
        'w_in': nrm(ks[1], (DEPTH, D_MODEL, IN_WIDTH), D_MODEL ** -0.5),
        'w_out': nrm(ks[2], (DEPTH, MIX_WIDTH, D_MODEL), MIX_WIDTH ** -0.5),
        'norm1_w': 1.0 + nrm(ks[3], (DEPTH, D_MODEL), 0.02),
        'norm2_w': 1.0 + nrm(ks[4], (DEPTH, D_MODEL), 0.02),
        'q_norm_w': 1.0 + nrm(ks[5], (DEPTH, HEAD_DIM), 0.02),
        'k_norm_w': 1.0 + nrm(ks[6], (DEPTH, HEAD_DIM), 0.02),
        'attn_sinks': nrm(ks[7], (DEPTH, N_Q_HEADS), 0.5),
        'hgrn_lb_logits': nrm(ks[8], (DEPTH + 1, HGRN_WIDTH), 0.5),
        'hgrn_gnorm_w': 1.0 + nrm(ks[9], (DEPTH, HGRN_DV), 0.02),
        'w_gate_up': nrm(ks[10], (DEPTH, D_MODEL, 2 * D_FF), D_MODEL ** -0.5),
        'w_down': nrm(ks[11], (DEPTH, D_FF, D_MODEL), D_FF ** -0.5),
    }

def reference(x, w_in, w_out, norm1_w, norm2_w, q_norm_w, k_norm_w, attn_sinks, hgrn_lb_logits, hgrn_gnorm_w, w_gate_up, w_down):
    lower_bounds = jnp.cumsum(jax.nn.softmax(hgrn_lb_logits.astype(jnp.float32), axis=0), axis=0)
    for layer in range(DEPTH):
        h = _rmsnorm(x, norm1_w[layer])
        proj = h @ w_in[layer]
        qa, ka, va, qb, fb, ib, gb = jnp.split(proj, SPLIT_POINTS, axis=-1)
        ya = _swa_sink_attention(qa, ka, va, q_norm_w[layer], k_norm_w[layer], attn_sinks[layer])
        yb = _hgrn2(qb, fb, ib, gb, lower_bounds[layer], hgrn_gnorm_w[layer])
        x = x + (jnp.concatenate([ya, yb], axis=-1) @ w_out[layer]).astype(x.dtype)
        h = _rmsnorm(x, norm2_w[layer])
        gate, up = jnp.split(h @ w_gate_up[layer], 2, axis=-1)
        x = x + ((jax.nn.silu(gate) * up) @ w_down[layer]).astype(x.dtype)
    return x


_drawn_inputs = setup_inputs


def setup_inputs(seed=0):
    import zlib

    import numpy as np

    out = dict(_drawn_inputs(seed))
    spreads = {}
    factors = {'norm1_w': 4.594,
     'norm2_w': 12.67,
     'q_norm_w': 8.0,
     'k_norm_w': 8.0,
     'attn_sinks': 8.0,
     'hgrn_gnorm_w': 5.866}
    for name, (base, spread) in spreads.items():
        noise = np.random.default_rng([zlib.crc32(name.encode()), seed]).standard_normal(out[name].shape)
        drawn = base * np.exp(spread * noise) if base else spread * noise
        out[name] = __import__('jax').numpy.asarray(drawn.astype(out[name].dtype))
    for name, factor in factors.items():
        out[name] = (out[name] * factor).astype(out[name].dtype)
    return out
```

```python
from contextlib import ExitStack

import numpy as np

import concourse.bass as bass
from concourse import mybir

F32 = mybir.dt.float32
F32R = mybir.dt.float32r
BF16 = mybir.dt.bfloat16
U32 = mybir.dt.uint32
ALU = mybir.AluOpType
ACT = mybir.ActivationFunctionType
AX = mybir.AxisListType

P = 128
SEQ, D = 2048, 1024
KT = D // P
CHUNK = 64
HD = 64
N_Q, N_KV = 8, 2
SLOTS = N_Q + N_KV
ROPE = HD // 4
HG = 4
D_FF = 2816
FT = D_FF // P
EPS = 1e-6
NEG = -1e30

TB = 512
NB = SEQ // TB
TT = TB // P
NC = TB // CHUNK
WC = 256
TH = 1024
HT = TH // P

CHUNKS = [("KV", 512, 256), ("QA0", 0, 256), ("QA1", 256, 256), ("F0", 1280, 128), ("F1", 1408, 128),
          ("Q01", 768, 256), ("I01", 1792, 256), ("G01", 2304, 256), ("F23", 1536, 256), ("Q23", 1024, 256),
          ("I23", 2048, 256), ("G23", 2560, 256)]
NW = len(CHUNKS) + D // WC
FIRST_HEAD = {"F0": 0, "F1": 1, "F23": 2, "Q01": 0, "Q23": 2}
HALF_CHUNKS = [n for n, c in enumerate(CHUNKS) if c[2] < WC]
WHOLE_CHUNKS = [n for n in range(NW) if n not in HALF_CHUNKS]


def chunk_name(n):
    return CHUNKS[n][0] if n < len(CHUNKS) else f"WO{n - len(CHUNKS)}"


def chunk_groups(n):
    name = chunk_name(n)
    return CHUNKS[n][2] // P if name in FIRST_HEAD else TT


GROUPS_TO = [sum(chunk_groups(m) for m in range(n)) for n in range(NW + 1)]
N_GROUPS = GROUPS_TO[NW]
CHUNK_AT = {chunk_name(n): n for n in range(NW)}


def block_steps():
    at = {}

    def after(name, group, *steps):
        at.setdefault((name, group), []).extend(steps)

    after("KV", 3, ("vmix",))
    after("QA1", 0, ("qn1", 0))
    after("QA1", 1, ("qn1", 1))
    after("QA1", 2, ("qn1", 2), ("qn2", 0))
    after("QA1", 3, ("qn1", 3), ("qn2", 1))
    after("F0", 0, ("qn2", 2), ("qn2", 3))
    after("Q01", 0, ("qT", 0), ("qT", 1), ("qT", 2), ("qT", 3), ("kT",))
    after("Q01", 1, ("sc", 0), ("sm1", 0), ("sm1", 1))
    after("I01", 0, ("ha", 0))
    after("I01", 1, ("sm2", 0), ("sm2", 1), ("sc", 1))
    after("I01", 2, ("pt", 0), ("pt", 1), ("sm1", 2), ("sm1", 3), ("hb", 0))
    after("I01", 3, ("pv", 0), ("sm2", 2), ("sm2", 3), ("sc", 2))
    after("G01", 0, ("pt", 2), ("pt", 3), ("sm1", 4), ("sm1", 5), ("xload",), ("hc", 0), ("ha", 1))
    after("G01", 1, ("pv", 1), ("sm2", 4), ("sm2", 5), ("sc", 3))
    after("G01", 2, ("pt", 4), ("pt", 5), ("sm1", 6), ("sm1", 7), ("hb", 1), ("att", 0), ("kt", 0))
    after("G01", 3, ("ds", 0, 0), ("ds", 0, 1), ("pv", 2), ("sm2", 6), ("sm2", 7), ("hc", 1))
    after("F23", 0, ("pt", 6), ("pt", 7))
    after("F23", 1, ("pv", 3), ("o", 0), ("on1", 0), ("kt", 1), ("ha", 2))
    after("Q23", 0, ("on2", 0), ("on3", 0), ("ds", 1, 0), ("ds", 1, 1), ("hb", 2), ("att", 1))
    after("Q23", 1, ("yt", 0), ("o", 1), ("on1", 1))
    after("I23", 0, ("on2", 1), ("on3", 1), ("hc", 2), ("ha", 3))
    after("I23", 1, ("yt", 1), ("att", 2), ("kt", 2))
    after("I23", 2, ("hb", 3), ("n1a",))
    after("I23", 3, ("hc", 3))
    after("G23", 0, ("ds", 2, 0), ("ds", 2, 1), ("n1b",))
    after("G23", 1, ("o", 2), ("on1", 2), ("kt", 3))
    after("G23", 2, ("on2", 2), ("ds", 3, 0), ("ds", 3, 1), ("att", 3))
    after("G23", 3, ("on3", 2), ("o", 3), ("on1", 3), ("yt", 2), ("on2", 3), ("on3", 3))
    after("WO0", 0, ("xT", 0))
    after("WO0", 1, ("xT", 1))
    after("WO0", 2, ("xT", 2))
    after("WO1", 0, ("xT", 3))
    after("WO1", 2, ("xT", 4))
    after("WO2", 0, ("xT", 5))
    after("WO2", 2, ("xT", 6))
    after("WO3", 0, ("xT", 7))
    steps = []
    for n in range(NW):
        for g in range(chunk_groups(n)):
            if (chunk_name(n), g) == ("WO0", 0):
                steps.append(("yt", 3))
            if g == 0 and chunk_groups(n) == 1:
                steps.append(("split", n + 1))
            steps.append(("proj", n, g))
            steps += at.pop((chunk_name(n), g), [])
            if g == 0 and chunk_groups(n) > 1:
                steps.append(("split", n + 1))
    assert not at, at
    return steps


STEPS = block_steps()
TR_KINDS = ("qT", "pt", "kt", "ds", "yt", "xT")
TR_USES = [s for s in STEPS if s[0] in TR_KINDS]
assert len(TR_USES) % 2 == 0


class Signal:

    def __init__(self, nc, ctx, name, per_pass, ahead=0):
        self.sem = ctx.enter_context(nc.semaphore(name))
        self.per_pass, self.ahead = per_pass, ahead

    def upto(self, n_pass, k):
        return n_pass * self.per_pass + (k + self.ahead)


class Places:

    def __init__(self, nc):
        self.nc, self.at = nc, (nc.sbuf_base + 63) // 64 * 64

    def put(self, name, shape, dt, at=None):
        size = int(np.prod(shape[1:])) * (2 if dt == BF16 else 4)
        offset = self.at if at is None else at
        if at is None:
            self.at += (size + 31) // 32 * 32
            assert self.at <= self.nc.sbuf_usable_end, (name, self.at)
        return self.nc.alloc_sbuf_tensor_at(name, list(shape), dt, offset=offset)


def three_passes(pe, out, stationary, moving, before_last=None):
    for k in range(KT):
        if k == KT - 1 and before_last is not None:
            before_last()
        pe.matmul(out, stationary[0](k), moving[0](k), start=(k == 0), stop=False)
        pe.matmul(out, stationary[0](k), moving[1](k), start=False, stop=False)
        last = pe.matmul(out, stationary[1](k), moving[0](k), start=False, stop=(k == KT - 1))
    return last


def build_phase_a(nc, ctx, dram, x_mid):
    def sem(name):
        return ctx.enter_context(nc.semaphore(name))

    def signal(name, per_pass, ahead=0):
        return Signal(nc, ctx, name, per_pass, ahead)

    mem = Places(nc)
    put = mem.put
    ident = put("a_ident", [P, P], F32)
    causal = put("a_causal", [P, 1, P], U32)
    qk_weight = put("a_qk_weight", [P, 2, HD], F32)
    sink = put("a_sink", [P, N_KV, 4], F32)
    n1w = put("a_n1w", [P, KT], F32)
    gnw = put("a_gnw", [P, 1], F32)
    lb_in = put("a_lb_in", [P, 2, HG], F32)
    lb_e = put("a_lb_e", [P, 4, HG], F32)
    lb = put("a_lb", [P, HG], F32)
    one_less_lb = put("a_one_less_lb", [P, HG], F32)
    neg_half = put("a_neg_half", [P, SLOTS], F32)
    ones_row = put("a_ones_row", [1, P], F32)
    penalty = put("a_penalty", [1, P], F32)
    not_start = put("a_not_start", [P, TB], BF16)
    rope = put("a_rope", [P, TT, 4 * ROPE // 2], F32)
    w_stage = [put(f"a_w_stage{s}", [P, KT, WC], F32) for s in range(2)]
    w_hi = [put(f"a_w_hi{s}", [P, KT, WC], F32R) for s in range(2)]
    w_lo = [put(f"a_w_lo{s}", [P, KT, WC], F32R) for s in range(2)]
    hT_hi = put("a_hT_hi", [P, KT, TB], F32R)
    hT_lo = put("a_hT_lo", [P, KT, TB], F32R)
    yA_hi = put("a_yA_hi", [P, HG, TB], F32R)
    yA_lo = put("a_yA_lo", [P, HG, TB], F32R)
    arena = mem.at
    x_in = put("a_x_in", [P, TT, D], F32)
    qk = put("a_qk", [P, TT, SLOTS, HD], F32, at=arena)
    qk_sq = put("a_qk_sq", [P, SLOTS, HD], F32, at=arena + TT * SLOTS * HD * 4)
    rope_u = put("a_rope_u", [P, SLOTS, ROPE], F32, at=arena + TT * SLOTS * HD * 4)
    rope_v = put("a_rope_v", [P, SLOTS, ROPE], F32, at=arena + TT * SLOTS * HD * 4 + SLOTS * ROPE * 4)
    x_res = [put(f"a_x_res{s}", [P, TT, WC], F32) for s in range(2)]
    qT = put("a_qT", [P, NC, 4, CHUNK], F32)
    kT = put("a_kT", [P, TT, P], F32)
    kT_even = put("a_kT_even", [P, TT, P], F32)
    v_nat = put("a_v_nat", [P, TT, P], F32)
    v_even = put("a_v_even", [P, TT + 1, P], F32)
    i_nat = put("a_i_nat", [P, TT, HG * P], F32)
    g_nat = put("a_g_nat", [P, TT, HG * P], F32)
    f_at, f_gate, q_h, yH_hi, yH_lo = [], [], [], [], []
    for h in range(HG):
        f_at.append(mem.at)
        f_gate.append(put(f"a_f_gate{h}", [P, TB], F32))
        yH_hi.append(put(f"a_yH_hi{h}", [P, TB], F32R, at=f_at[h]))
        q_at = mem.at
        q_h.append(put(f"a_q_h{h}", [P, TB], F32))
        yH_lo.append(put(f"a_yH_lo{h}", [P, TB], F32R, at=q_at))
    q_in = [put(f"a_q_in{s}", [P, TB], F32) for s in range(2)]
    k_end = [put(f"a_k_end{s}", [P, TB], F32) for s in range(2)]
    t_a = put("a_t_a", [P, TB], F32)
    t_b = put("a_t_b", [P, TB], F32)
    decay = put("a_decay", [P, HG, NC], F32)
    prob_at = mem.at
    prob = [put(f"a_prob{s}", [P, 4, P], F32) for s in range(2)]
    probT = [put(f"a_probT{s}", [P, 4, P], F32) for s in range(2)]
    att_m = put("a_att_m", [P, TT, P], F32)
    k_nat = put("a_k_nat", [P, TT, P], F32)
    state = put("a_state", [P, NC, P], F32)
    carry = put("a_carry", [P, HG, P], F32)
    y_nat = put("a_y_nat", [P, TT, P], F32)
    junk = put("a_junk", [P, D], BF16, at=prob_at)
    o_sq = put("a_o_sq", [P, TT, P], BF16)
    ss = put("a_ss", [P, TT], F32)
    x_rs = put("a_x_rs", [P, TT], F32)
    q_ss = put("a_q_ss", [P, TT, SLOTS], F32)
    q_rs = put("a_q_rs", [P, TT, SLOTS], F32)
    o_ss = put("a_o_ss", [P, TT], F32)
    o_rs = put("a_o_rs", [P, TT], F32)
    top = put("a_top", [P, 2, 4], F32)
    neg_top = put("a_neg_top", [P, 2, 4], F32)
    sink_less = put("a_sink_less", [P, 2, 4], F32)
    sink_e = put("a_sink_e", [P, 2, 4], F32)
    denom = put("a_denom", [P, 2, 4], F32)

    def bank(name):
        return ctx.enter_context(nc.psum_tensor(name, [P, 512], F32))

    pj = [bank(f"a_pj{s}") for s in range(2)]
    tr = [bank(f"a_tr{s}") for s in range(2)]
    sc = [bank(f"a_sc{s}") for s in range(2)]
    pvb = bank("a_pv")
    hb = bank("a_hb")

    consts_in = sem("consts_in")
    w_loaded = [sem(f"w_loaded{s}") for s in range(2)]
    x_loaded, rope_loaded = sem("x_loaded"), sem("rope_loaded")
    xr_loaded = [sem(f"xr_loaded{s}") for s in range(2)]
    xr_stored = [sem(f"xr_stored{s}") for s in range(2)]
    w_hi_ready = signal("w_hi_ready", NW, 1)
    w_lo_ready = signal("w_lo_ready", NW, 1)
    pj_full = signal("pj_full", N_GROUPS, 1)
    tr_full = signal("tr_full", len(TR_USES), KT)
    ss_ready = signal("ss_ready", 1, 1)
    ms_ready = signal("ms_ready", 1, 1)
    x_rs_ready = signal("x_rs_ready", 1, 1)
    xn_ready = signal("xn_ready", 1, 1)
    h_hi_ready = signal("h_hi_ready", KT, KT)
    hT_ready = signal("hT_ready", KT, KT)
    f_ready = signal("f_ready", HG)
    q_ready = signal("q_ready", HG)
    g_ready = signal("g_ready", 2 * TT)
    kv_ready = signal("kv_ready", TT)
    qa_ready = signal("qa_ready", 2 * TT)
    i_ready = signal("i_ready", 2 * TT)
    v_even_ready = signal("v_even_ready", 1)
    q_ms_ready = signal("q_ms_ready", TT)
    q_rs_ready = signal("q_rs_ready", TT)
    qk_ready = signal("qk_ready", TT)
    kT_full = signal("kT_full", 1)
    qT_ready = signal("qT_ready", 4)
    kT_ready = signal("kT_ready", 1)
    sc_full = signal("sc_full", 8)
    sink_less_ready = signal("sink_less_ready", 8)
    exp_ready = signal("exp_ready", 8)
    prob_ready = signal("prob_ready", 8)
    probT_ready = signal("probT_ready", 8)
    pv_full = signal("pv_full", TT)
    yA_hi_ready = signal("yA_hi_ready", TT)
    yA_ready = signal("yA_ready", TT, 1)
    fg_ready = signal("fg_ready", HG)
    lf_ready = signal("lf_ready", HG)
    b_ready = signal("b_ready", HG)
    e_ready = signal("e_ready", HG)
    gates_ready = signal("gates_ready", HG, 1)
    att_full = signal("att_full", HG)
    att_ready = signal("att_ready", HG)
    k_nat_ready = signal("k_nat_ready", HG)
    state_ready = signal("state_ready", HG)
    o_full = signal("o_full", HG)
    o_sq_ready = signal("o_sq_ready", HG)
    o_ms_ready = signal("o_ms_ready", HG)
    o_rs_ready = signal("o_rs_ready", HG)
    hb_read = signal("hb_read", HG, 1)
    y_nat_ready = signal("y_nat_ready", HG)
    yH_hi_ready = signal("yH_hi_ready", HG)
    yH_ready = signal("yH_ready", HG)
    res_done = signal("res_done", 4 * TT, 1)
    pool_waited, dve_waited = sem("pool_waited"), sem("dve_waited")
    pool_set, dve_set, act_set = sem("pool_set"), sem("dve_set"), sem("act_set")

    tr_read = {"qT": (qT_ready, lambda s: s[1] + 1), "pt": (probT_ready, lambda s: s[1] + 1),
               "kt": (k_nat_ready, lambda s: s[1] + 1), "ds": (state_ready, lambda s: s[1] + 1),
               "yt": (yH_ready, lambda s: s[1] + 1), "xT": (hT_ready, lambda s: s[1] + 1)}
    pj_read = []
    counts = {}
    for n in range(NW):
        kind = chunk_name(n)[:2] if chunk_name(n)[:2] in ("KV", "QA", "WO") else chunk_name(n)[0]
        for g in range(chunk_groups(n)):
            counts[kind] = counts.get(kind, 0) + 1
            s = {"F": f_ready, "Q": q_ready, "G": g_ready, "KV": kv_ready, "QA": qa_ready, "I": i_ready,
                 "WO": res_done}[kind]
            pj_read.append((s, counts[kind]))

    blk = ctx.enter_context(nc.Block())

    @blk.sync
    def _(sp):
        def load(n):
            m = n % NW
            if m in HALF_CHUNKS:
                sp.dma_start(w_stage[n % 2][:, :, 0:P], dram["w_half"][HALF_CHUNKS.index(m)]).then_inc(w_loaded[n % 2], 16)
            else:
                sp.dma_start(w_stage[n % 2][:, :, :], dram["w_whole"][WHOLE_CHUNKS.index(m)]).then_inc(w_loaded[n % 2], 16)

        load(0)
        for name, tile in (("ident", ident), ("causal", causal), ("qk_weight", qk_weight), ("sink", sink),
                           ("n1w", n1w), ("gnw", gnw), ("lb", lb_in), ("not_start", None)):
            if tile is not None:
                sp.dma_start(tile[:], dram[name]).then_inc(consts_in, 16)
        with sp.Fori(0, NB) as b:
            for n in range(1, NW + 1):
                sp.wait_ge(w_lo_ready.sem, w_lo_ready.upto(b, max(n - 2, 0)))
                load(n)

    @blk.gpsimd
    def _(pool):
        def wait(sem, value):
            pool.wait_ge(sem, value)
            pool.sem_inc(pool_waited, 1)

        def load_block(b):
            pool.dma_start(x_in[:], dram["x_pad"][bass.ds(b, 1)].rearrange("o (t p) d -> p (o t) d", p=P)).then_inc(x_loaded, 16)
            pool.dma_start(rope[:], dram["rope"][bass.ds(b, 1)].rearrange("o p t c -> p (o t) c")).then_inc(rope_loaded, 16)

        load_block(0)
        pool.memset(neg_half[:], -0.5)
        pool.memset(ones_row[:], 1.0)
        pool.memset(penalty[:, 0:CHUNK], 0.0)
        pool.memset(penalty[:, CHUNK:P], NEG)
        pool.memset(kT[:], 0.0)
        pool.memset(v_even[:], 0.0)
        pool.memset(carry[:], 0.0)
        pool.memset(att_m[:], 0.0)
        pool.memset(not_start[:], 1.0)
        pool.drain()
        pool.memset(not_start[:].rearrange("p (c s) -> p c s", s=CHUNK)[:, :, 0:1], 0.0).then_inc(pool_set, 1)

        def power(out, in_, width, ready, done, value, shape=None):
            pool.drain()
            pool.wait_ge(ready.sem, value)
            pool.tensor_tensor(out, in_, neg_half[:, 0:width], ALU.pow).then_inc(done.sem, 1)

        pool.drain()
        power(x_rs[:], ss[:], TT, ms_ready, x_rs_ready, ms_ready.upto(-1, 1))
        x_cols = dram["x_pad"].rearrange("b (t p) (c n) -> b p t c n", p=P, n=WC)
        mid_cols = x_mid.rearrange("(b t p) (c n) -> b p t c n", b=NB, p=P, n=WC)
        with pool.Fori(0, NB) as b:
            def load_res(c, b=b):
                pool.dma_start(x_res[c % 2][:], x_cols[bass.ds(b, 1), :, :, c, :].rearrange("o p t n -> p (o t) n")).then_inc(xr_loaded[c % 2], 16)

            def store_res(c, b=b):
                wait(res_done.sem, res_done.upto(b, TT * (c + 1)))
                pool.dma_start(mid_cols[bass.ds(b, 1), :, :, c, :].rearrange("o p t n -> p (o t) n"), x_res[c % 2][:]).then_inc(xr_stored[c % 2], 16)

            for step in STEPS:
                kind = step[0]
                if kind == "vmix":
                    wait(kv_ready.sem, kv_ready.upto(b, TT))
                    pool.drain()
                    pool.tensor_copy(v_even[CHUNK:P, 0, :], v_even[CHUNK:P, TT, :])
                    pool.drain()
                    pool.tensor_copy(v_even[0:CHUNK, 0:TT, :], v_nat[0:CHUNK, :, :])
                    pool.drain()
                    pool.tensor_copy(v_even[CHUNK:P, 1:TT + 1, :], v_nat[CHUNK:P, :, :]).then_inc(v_even_ready.sem, 1)
                elif kind == "qn1":
                    t = step[1]
                    power(q_rs[:, t, :], q_ss[:, t, :], SLOTS, q_ms_ready, q_rs_ready, q_ms_ready.upto(b, t + 1))
                elif kind == "sc" and step[1] == 1:
                    wait(sc_full.sem, sc_full.upto(b, 2))
                    pool.drain()
                    pool.memset(penalty[:, CHUNK:P], 0.0)
                elif kind == "xload":
                    wait(kT_full.sem, kT_full.upto(b, 1))
                    load_block(b + 1)
                    load_res(0)
                    load_res(1)
                elif kind == "on1":
                    h = step[1]
                    power(o_rs[:], o_ss[:], TT, o_ms_ready, o_rs_ready, o_ms_ready.upto(b, h + 1))
                elif kind == "n1a":
                    power(x_rs[:], ss[:], TT, ms_ready, x_rs_ready, ms_ready.upto(b, 1))
                elif kind == "proj" and chunk_name(step[1]).startswith("WO") and step[2] == TT - 1:
                    c = step[1] - len(CHUNKS)
                    store_res(c)
                    wait(xr_stored[c % 2], b * 32 + 16 * (c // 2 + 1))
                    if c < 2:
                        load_res(c + 2)

    @blk.scalar
    def _(act):
        def split(b, n):
            s = n % 2
            loaded = b * (16 * NW // 2) + 16 * ((n + 1) // 2 + (1 - s))
            act.wait_ge(w_loaded[s], loaded)
            if n >= 1:
                act.wait_ge(pj_full.sem, pj_full.upto(b, GROUPS_TO[max(n - 1, 0)]))
            cols = P if n % NW in HALF_CHUNKS else WC
            act.activation(w_hi[s][:, :, 0:cols], w_stage[s][:, :, 0:cols], ACT.Copy).then_inc(w_hi_ready.sem, 1)

        def square_x(b):
            act.wait_ge(x_loaded, b * 16 + 32)
            for t in range(TT):
                last = act.activation(junk[:], x_in[:, t, :], ACT.Square, accum_out=ss[:, t:t + 1])
                if t < TT - 1:
                    act.drain()
            last.then_inc(ss_ready.sem, 1)

        def evacuate_x(b, k, use):
            act.wait_ge(tr_full.sem, tr_full.upto(b, use + 1))
            act.activation(hT_hi[:, k, :], tr[use % 2][:], ACT.Copy, scale=n1w[:, k:k + 1]).then_inc(h_hi_ready.sem, 1)

        act.wait_ge(consts_in, 7 * 16)
        act.wait_ge(dve_set, 1)
        act.activation(lb_e[:, 0:2, :], lb_e[:, 2:4, :], ACT.Exp).then_inc(act_set, 1)
        split(0, 0)
        square_x(-1)
        for k in range(KT):
            evacuate_x(-1, k, len(TR_USES) - KT + k)

        with act.Fori(0, NB) as b:
            use = 0
            table = [None]

            def use_exp_table():
                if table[0] != "exp":
                    act.preload_act_table_set("natural_log_exp_and_others")
                table[0] = "exp"

            for step in STEPS:
                kind = step[0]
                if kind == "proj" and chunk_name(step[1])[0] in "FQG" and chunk_name(step[1])[:2] != "QA":
                    table[0] = "other"
                if kind == "split":
                    split(b, step[1])
                elif kind == "proj":
                    n, g = step[1:]
                    name, ps = chunk_name(n), pj[(GROUPS_TO[n] + g) % 2]
                    if name.startswith("WO"):
                        continue
                    act.wait_ge(pj_full.sem, pj_full.upto(b, GROUPS_TO[n] + g + 1))
                    if name[0] == "F":
                        act.activation(f_gate[FIRST_HEAD[name] + g][:], ps[:], ACT.Sigmoid).then_inc(f_ready.sem, 1)
                    elif name in FIRST_HEAD:
                        act.activation(q_h[FIRST_HEAD[name] + g][:], ps[:], ACT.Silu).then_inc(q_ready.sem, 1)
                    elif name[0] == "G":
                        c0 = WC * (name == "G23")
                        act.activation(g_nat[:, g, c0:c0 + WC], ps[:, 0:WC], ACT.Silu).then_inc(g_ready.sem, 1)
                    elif name == "KV":
                        act.activation(qk[:, g, N_Q:SLOTS, :], ps[:, 0:P].rearrange("p (s d) -> p s d", d=HD), ACT.Copy)
                        act.activation(v_nat[:, g, :], ps[:, P:2 * P], ACT.Copy).then_inc(kv_ready.sem, 1)
                    elif name[:2] == "QA":
                        half = int(name[2])
                        act.activation(qk[:, g, half:N_Q:2, :], ps[:, 0:WC].rearrange("p (s d) -> p s d", d=HD), ACT.Copy).then_inc(qa_ready.sem, 1)
                    else:
                        c0 = WC * (name == "I23")
                        act.activation(i_nat[:, g, c0:c0 + WC], ps[:, 0:WC], ACT.Copy).then_inc(i_ready.sem, 1)
                elif kind == "ha":
                    h = step[1]
                    use_exp_table()
                    act.wait_ge(fg_ready.sem, fg_ready.upto(b, h + 1))
                    act.wait_ge(gates_ready.sem, gates_ready.upto(b, h))
                    act.activation(t_a[:], f_gate[h][:], ACT.Ln).then_inc(lf_ready.sem, 1)
                elif kind == "hb":
                    h, s = step[1], step[1] % 2
                    use_exp_table()
                    act.wait_ge(b_ready.sem, b_ready.upto(b, h + 1))
                    act.activation(q_in[s][:], t_a[:], ACT.Exp)
                    act.activation(k_end[s][:], k_end[s][:], ACT.Exp)
                    act.activation(decay[:, h, :], t_b[:].rearrange("p (c s) -> p c s", s=CHUNK)[:, :, CHUNK - 1], ACT.Exp)
                    act.drain()
                    act.activation(t_a[:], t_a[:], ACT.Exp, scale=-1.0)
                    act.activation(t_b[:], t_b[:], ACT.Exp).then_inc(e_ready.sem, 1)
                elif kind == "qT":
                    j = step[1]
                    act.wait_ge(tr_full.sem, tr_full.upto(b, use + 1))
                    act.activation(qT[:, :, j, :], tr[use % 2][:].rearrange("p (c q) -> p c q", q=CHUNK), ACT.Copy).then_inc(qT_ready.sem, 1)
                elif kind == "kT":
                    act.wait_ge(kT_full.sem, kT_full.upto(b, 1))
                    ps = sc[0][:].rearrange("p (t c) -> p t c", c=P)
                    act.activation(kT_even[:, 0, CHUNK:P], kT[:, TT - 1, CHUNK:P], ACT.Copy)
                    act.drain()
                    act.activation(kT[:], ps, ACT.Copy)
                    act.activation(kT_even[:, :, 0:CHUNK], ps[:, :, 0:CHUNK], ACT.Copy)
                    act.activation(kT_even[:, 1:TT, CHUNK:P], ps[:, 0:TT - 1, CHUNK:P], ACT.Copy).then_inc(kT_ready.sem, 1)
                elif kind == "sm1":
                    u, s, kv = step[1], step[1] % 2, step[1] % 2
                    use_exp_table()
                    act.wait_ge(sink_less_ready.sem, sink_less_ready.upto(b, u + 1))
                    act.activation(sink_e[:, s, :], sink_less[:, s, :], ACT.Exp)
                    for i in range(4):
                        last = act.activation(prob[s][:, i, :], sc[kv][:, i * P:(i + 1) * P], ACT.Exp,
                                              bias=neg_top[:, s, i:i + 1], scale=HD ** -0.5, accum_out=denom[:, s, i:i + 1])
                    last.then_inc(exp_ready.sem, 1)
                elif kind == "pt":
                    u = step[1]
                    act.wait_ge(tr_full.sem, tr_full.upto(b, use + 1))
                    act.activation(probT[u % 2][:].rearrange("p i c -> p (i c)"), tr[use % 2][:], ACT.Copy).then_inc(probT_ready.sem, 1)
                elif kind == "pv":
                    t = step[1]
                    act.wait_ge(pv_full.sem, pv_full.upto(b, t + 1))
                    act.activation(yA_hi[:, :, t * P:(t + 1) * P].rearrange("p j (c q) -> p j c q", c=2),
                                   pvb[:].rearrange("p (c j q) -> p j c q", c=2, j=4), ACT.Copy).then_inc(yA_hi_ready.sem, 1)
                elif kind == "kt":
                    h = step[1]
                    act.wait_ge(tr_full.sem, tr_full.upto(b, use + 1))
                    act.activation(k_nat[:].rearrange("p t c -> p (t c)"), tr[use % 2][:], ACT.Copy).then_inc(k_nat_ready.sem, 1)
                elif kind == "on1":
                    h = step[1]
                    act.wait_ge(o_full.sem, o_full.upto(b, h + 1))
                    for t in range(TT):
                        last = act.activation(o_sq[:, t, :], hb[:, t * P:(t + 1) * P], ACT.Square, accum_out=o_ss[:, t:t + 1])
                    last.then_inc(o_sq_ready.sem, 1)
                elif kind == "yt":
                    h = step[1]
                    act.wait_ge(tr_full.sem, tr_full.upto(b, use + 1))
                    act.activation(yH_hi[h][:], tr[use % 2][:], ACT.Copy, scale=gnw[:, 0:1]).then_inc(yH_hi_ready.sem, 1)
                elif kind == "n1a":
                    square_x(b)
                elif kind == "xT":
                    evacuate_x(b, step[1], use)
                if kind in TR_KINDS:
                    use += 1

    @blk.tensor
    def _(pe):
        def transpose_x(b, k, use, after=None):
            if k == 0:
                pe.wait_ge(xn_ready.sem, xn_ready.upto(b, 1))
            for t in range(TT):
                last = pe.transpose(tr[use % 2][:, t * P:(t + 1) * P], x_in[:, t, k * P:(k + 1) * P], ident[:])
            last.then_inc(tr_full.sem, 1)

        def bank_read(b, use):
            if use >= 2:
                read, index = tr_read[TR_USES[use - 2][0]]
                pe.wait_ge(read.sem, read.upto(b, index(TR_USES[use - 2])))

        pe.sem_inc(pj_full.sem, 1)
        pe.wait_ge(consts_in, 7 * 16)
        pe.wait_ge(pool_set, 1)
        for k in range(KT):
            if k >= 2:
                pe.wait_ge(hT_ready.sem, hT_ready.upto(-1, k - 1))
            transpose_x(-1, k, len(TR_USES) - KT + k)

        with pe.Fori(0, NB) as b:
            use = 0
            pe.wait_ge(hT_ready.sem, hT_ready.upto(b, 0))
            for step in STEPS:
                kind = step[0]
                if kind == "proj":
                    n, g = step[1:]
                    name, at, s = chunk_name(n), GROUPS_TO[n] + g, n % 2
                    if g == 0:
                        pe.wait_ge(w_lo_ready.sem, w_lo_ready.upto(b, n))
                    read, index = pj_read[at - 2]
                    pe.wait_ge(read.sem, read.upto(b, index) if at >= 2 else res_done.upto(b, 0))
                    if name in FIRST_HEAD:
                        cols = slice(g * P, (g + 1) * P)
                        last = three_passes(pe, pj[at % 2][:],
                                            (lambda k: w_hi[s][:, k, cols], lambda k: w_lo[s][:, k, cols]),
                                            (lambda k: hT_hi[:, k, :], lambda k: hT_lo[:, k, :]))
                    else:
                        rows = slice(g * P, (g + 1) * P)
                        if name[:2] == "WO":
                            if n == len(CHUNKS) and g == 0:
                                pe.wait_ge(yA_ready.sem, yA_ready.upto(b, TT))
                                pe.wait_ge(yH_ready.sem, yH_ready.upto(b, HG - 1))
                            still = (lambda k: yA_hi[:, k, rows] if k < HG else yH_hi[k - HG][:, rows],
                                     lambda k: yA_lo[:, k, rows] if k < HG else yH_lo[k - HG][:, rows])
                        else:
                            still = (lambda k: hT_hi[:, k, rows], lambda k: hT_lo[:, k, rows])
                        last_head = (lambda: pe.wait_ge(yH_ready.sem, yH_ready.upto(b, HG))) if (name, g) == ("WO0", 0) else None
                        last = three_passes(pe, pj[at % 2][:, 0:WC], still,
                                            (lambda k: w_hi[s][:, k, :], lambda k: w_lo[s][:, k, :]), last_head)
                    last.then_inc(pj_full.sem, 1)
                elif kind == "qT":
                    j = step[1]
                    if j == 0:
                        pe.wait_ge(qk_ready.sem, qk_ready.upto(b, TT))
                    bank_read(b, use)
                    for t in range(TT):
                        last = pe.transpose(tr[use % 2][:, t * P:(t + 1) * P], qk[:, t, 2 * j:2 * j + 2, :].rearrange("p s d -> p (s d)"), ident[:])
                    last.then_inc(tr_full.sem, 1)
                elif kind == "kT":
                    for t in range(TT):
                        last = pe.transpose(sc[0][:, t * P:(t + 1) * P], qk[:, t, N_Q:SLOTS, :].rearrange("p s d -> p (s d)"), ident[:])
                    last.then_inc(kT_full.sem, 1)
                elif kind == "sc":
                    t = step[1]
                    if t == 0:
                        pe.wait_ge(kT_ready.sem, kT_ready.upto(b, 1))
                        pe.wait_ge(v_even_ready.sem, v_even_ready.upto(b, 1))
                    for kv in range(N_KV):
                        rows = slice(kv * HD, (kv + 1) * HD)
                        if t > 0:
                            pe.wait_ge(exp_ready.sem, exp_ready.upto(b, 2 * (t - 1) + kv + 1))
                        for cc in range(2):
                            keys = kT if cc else kT_even
                            for jj in range(2):
                                i = 2 * cc + jj
                                first = t == 0 and cc == 0
                                last = pe.matmul(sc[kv][:, i * P:(i + 1) * P], qT[rows, 2 * t + cc, 2 * jj:2 * jj + 2, :].rearrange("p j q -> p (j q)"),
                                                 keys[rows, t, :], start=True, stop=not first)
                                if first:
                                    last = pe.matmul(sc[kv][:, i * P:(i + 1) * P], ones_row[:], penalty[:], start=False, stop=True)
                        last.then_inc(sc_full.sem, 1)
                elif kind == "pt":
                    u = step[1]
                    pe.wait_ge(prob_ready.sem, prob_ready.upto(b, u + 1))
                    bank_read(b, use)
                    for i in range(4):
                        last = pe.transpose(tr[use % 2][:, i * P:(i + 1) * P], prob[u % 2][:, i, :], ident[:])
                    last.then_inc(tr_full.sem, 1)
                elif kind == "pv":
                    t = step[1]
                    pe.wait_ge(probT_ready.sem, probT_ready.upto(b, 2 * t + 2))
                    pe.wait_ge(yA_ready.sem, yA_ready.upto(b, t))
                    for cc in range(2):
                        v = v_nat if cc else v_even
                        for kv in range(N_KV):
                            last = pe.matmul(pvb[kv * HD:(kv + 1) * HD, cc * 256:(cc + 1) * 256], v[:, t, kv * HD:(kv + 1) * HD],
                                             probT[kv][:, 2 * cc:2 * cc + 2, :].rearrange("p i c -> p (i c)"), start=True, stop=True)
                    last.then_inc(pv_full.sem, 1)
                elif kind == "att":
                    h = step[1]
                    pe.wait_ge(gates_ready.sem, gates_ready.upto(b, h + 1))
                    pe.wait_ge(hb_read.sem, hb_read.upto(b, h))
                    for t in range(TT):
                        last = pe.matmul(hb[:, t * P:(t + 1) * P], f_gate[h][:, t * P:(t + 1) * P],
                                         q_in[h % 2][:, t * P:(t + 1) * P], start=True, stop=True)
                    last.then_inc(att_full.sem, 1)
                elif kind == "kt":
                    h = step[1]
                    pe.wait_ge(gates_ready.sem, gates_ready.upto(b, h + 1))
                    bank_read(b, use)
                    for t in range(TT):
                        last = pe.transpose(tr[use % 2][:, t * P:(t + 1) * P], k_end[h % 2][:, t * P:(t + 1) * P], ident[:])
                    last.then_inc(tr_full.sem, 1)
                elif kind == "ds":
                    h, par = step[1:]
                    if par == 0:
                        pe.wait_ge(k_nat_ready.sem, k_nat_ready.upto(b, h + 1))
                        pe.wait_ge(i_ready.sem, i_ready.upto(b, TT if h < 2 else 2 * TT))
                    bank_read(b, use)
                    rows = slice(par * CHUNK, (par + 1) * CHUNK)
                    for t in range(TT):
                        last = pe.matmul(tr[use % 2][:, t * P:(t + 1) * P], k_nat[rows, t, :], i_nat[rows, t, h * P:(h + 1) * P], start=True, stop=True)
                    last.then_inc(tr_full.sem, 1)
                elif kind == "o":
                    h = step[1]
                    pe.wait_ge(att_ready.sem, att_ready.upto(b, h + 1))
                    pe.wait_ge(state_ready.sem, state_ready.upto(b, h + 1))
                    for t in range(TT):
                        cols = slice(t * P, (t + 1) * P)
                        pe.matmul(hb[:, cols], att_m[:, t, :], i_nat[:, t, h * P:(h + 1) * P], start=True, stop=True)
                        for cc in range(2):
                            at = t * P + cc * CHUNK
                            last = pe.matmul(hb[cc * CHUNK:(cc + 1) * CHUNK, cols], q_h[h][:, at:at + CHUNK], state[:, 2 * t + cc, :],
                                             start=False, stop=True, skip_group_check=True)
                    last.then_inc(o_full.sem, 1)
                elif kind == "yt":
                    h = step[1]
                    pe.wait_ge(y_nat_ready.sem, y_nat_ready.upto(b, h + 1))
                    bank_read(b, use)
                    for t in range(TT):
                        last = pe.transpose(tr[use % 2][:, t * P:(t + 1) * P], y_nat[:, t, :], ident[:])
                    last.then_inc(tr_full.sem, 1)
                elif kind == "xT":
                    bank_read(b, use)
                    transpose_x(b, step[1], use)
                if kind in TR_KINDS:
                    use += 1

    @blk.vector
    def _(dve):
        def split(b, n):
            s = n % 2
            cols = P if n % NW in HALF_CHUNKS else WC
            dve.wait_ge(w_hi_ready.sem, w_hi_ready.upto(b, n))
            dve.tensor_tensor(w_lo[s][:, :, 0:cols], w_stage[s][:, :, 0:cols], w_hi[s][:, :, 0:cols].bitcast(F32), ALU.subtract).then_inc(w_lo_ready.sem, 1)

        def mean_square_x(b):
            dve.wait_ge(ss_ready.sem, ss_ready.upto(b, 1))
            dve.tensor_scalar(ss[:], ss[:], 1.0 / D, EPS, ALU.mult, ALU.add).then_inc(ms_ready.sem, 1)

        def scale_x(b):
            dve.wait_ge(x_rs_ready.sem, x_rs_ready.upto(b, 1))
            for t in range(TT):
                last = dve.tensor_scalar(x_in[:, t, :], x_in[:, t, :], x_rs[:, t:t + 1], None, ALU.mult)
            last.then_inc(xn_ready.sem, 1)

        def low_part(out, ps, weight, hi, ready):
            dve.scalar_tensor_tensor(out=out, in0=ps, scalar=weight, in1=hi.bitcast(F32), op0=ALU.mult, op1=ALU.subtract).then_inc(ready.sem, 1)

        def evacuate_x(b, k, use):
            dve.wait_ge(h_hi_ready.sem, h_hi_ready.upto(b, k + 1))
            low_part(hT_lo[:, k, :], tr[use % 2][:], n1w[:, k:k + 1], hT_hi[:, k, :], hT_ready)

        for s in (yA_ready, gates_ready, hb_read, res_done):
            dve.sem_inc(s.sem, 1)
        dve.wait_ge(consts_in, 7 * 16)
        dve.wait_ge(pool_set, 1)
        dve.tensor_tensor(lb_e[:, 0, :], lb_in[:, 0, :], lb_in[:, 1, :], ALU.max)
        dve.drain()
        dve.tensor_tensor(lb_e[:, 2, :], lb_in[:, 0, :], lb_e[:, 0, :], ALU.subtract)
        dve.tensor_tensor(lb_e[:, 3, :], lb_in[:, 1, :], lb_e[:, 0, :], ALU.subtract).then_inc(dve_set, 1)
        dve.wait_ge(act_set, 1)
        dve.tensor_tensor(lb_e[:, 1, :], lb_e[:, 0, :], lb_e[:, 1, :], ALU.add)
        dve.drain()
        dve.reciprocal(lb_e[:, 2, :], lb_e[:, 1, :])
        dve.drain()
        dve.tensor_tensor(lb[:], lb_e[:, 0, :], lb_e[:, 2, :], ALU.mult)
        dve.drain()
        dve.tensor_scalar(one_less_lb[:], lb[:], -1.0, 1.0, ALU.mult, ALU.add)
        split(0, 0)
        mean_square_x(-1)
        scale_x(-1)
        for k in range(KT):
            evacuate_x(-1, k, len(TR_USES) - KT + k)

        with dve.Fori(0, NB) as b:
            use = 0
            for step in STEPS:
                kind = step[0]
                if kind == "split":
                    split(b, step[1])
                elif kind == "proj" and chunk_name(step[1])[:2] == "WO":
                    n, g = step[1:]
                    c = n - len(CHUNKS)
                    if g == 0:
                        dve.wait_ge(xr_loaded[c % 2], b * 32 + 16 * (c // 2 + 1))
                    dve.wait_ge(pj_full.sem, pj_full.upto(b, GROUPS_TO[n] + g + 1))
                    dve.tensor_tensor(x_res[c % 2][:, g, :], x_res[c % 2][:, g, :], pj[(GROUPS_TO[n] + g) % 2][:, 0:WC], ALU.add).then_inc(res_done.sem, 1)
                elif kind == "qn1":
                    t = step[1]
                    dve.drain()
                    dve.wait_ge(qa_ready.sem, qa_ready.upto(b, TT + t + 1))
                    dve.tensor_tensor(qk_sq[:], qk[:, t, :, :], qk[:, t, :, :], ALU.mult)
                    dve.drain()
                    dve.tensor_reduce(q_ss[:, t, :], qk_sq[:], AX.X, ALU.add)
                    dve.drain()
                    dve.tensor_scalar(q_ss[:, t, :], q_ss[:, t, :], 1.0 / HD, EPS, ALU.mult, ALU.add).then_inc(q_ms_ready.sem, 1)
                elif kind == "qn2":
                    t = step[1]
                    q = qk[:, t, :, :]
                    dve.drain()
                    if t == 0:
                        dve.wait_ge(rope_loaded, b * 16 + 16)
                    dve.wait_ge(q_rs_ready.sem, q_rs_ready.upto(b, t + 1))
                    dve.tensor_tensor(q, q, q_rs[:, t, :, None].broadcast_to([P, SLOTS, HD]), ALU.mult)
                    dve.drain()
                    dve.tensor_tensor(q[:, 0:N_Q], q[:, 0:N_Q], qk_weight[:, 0:1, :].broadcast_to([P, N_Q, HD]), ALU.mult)
                    dve.tensor_tensor(q[:, N_Q:SLOTS], q[:, N_Q:SLOTS], qk_weight[:, 1:2, :].broadcast_to([P, N_KV, HD]), ALU.mult)
                    dve.drain()
                    half = ROPE // 2
                    cosines = rope[:, t:t + 1, 0:ROPE].broadcast_to([P, SLOTS, ROPE])
                    minus_sin = rope[:, t:t + 1, ROPE:ROPE + half].broadcast_to([P, SLOTS, half])
                    sin = rope[:, t:t + 1, ROPE + half:2 * ROPE].broadcast_to([P, SLOTS, half])
                    dve.tensor_tensor(rope_u[:], q[:, :, 0:ROPE], cosines, ALU.mult)
                    dve.tensor_tensor(rope_v[:, :, 0:half], q[:, :, half:ROPE], minus_sin, ALU.mult)
                    dve.tensor_tensor(rope_v[:, :, half:ROPE], q[:, :, 0:half], sin, ALU.mult)
                    dve.drain()
                    dve.tensor_tensor(q[:, :, 0:ROPE], rope_u[:], rope_v[:], ALU.add).then_inc(qk_ready.sem, 1)
                elif kind == "ha":
                    h = step[1]
                    dve.wait_ge(f_ready.sem, f_ready.upto(b, h + 1))
                    dve.tensor_scalar(f_gate[h][:], f_gate[h][:], one_less_lb[:, h:h + 1], lb[:, h:h + 1], ALU.mult, ALU.add).then_inc(fg_ready.sem, 1)
                elif kind == "hb":
                    h, s = step[1], step[1] % 2
                    dve.wait_ge(lf_ready.sem, lf_ready.upto(b, h + 1))
                    dve.tensor_scalar(f_gate[h][:], f_gate[h][:], -1.0, 1.0, ALU.mult, ALU.add)
                    dve.tensor_tensor_scan(t_b[:], not_start[:], t_a[:], 0.0, ALU.mult, ALU.add)
                    dve.drain()
                    chunks = t_b[:].rearrange("p (c s) -> p c s", s=CHUNK)
                    dve.tensor_tensor(t_a[:].rearrange("p (c s) -> p c s", s=CHUNK), chunks,
                                      chunks[:, :, CHUNK // 2:CHUNK // 2 + 1].broadcast_to([P, NC, CHUNK]), ALU.subtract)
                    if h >= 2:
                        dve.wait_ge(k_nat_ready.sem, k_nat_ready.upto(b, h - 1))
                    dve.tensor_tensor(k_end[s][:].rearrange("p (c s) -> p c s", s=CHUNK),
                                      chunks[:, :, CHUNK - 1:CHUNK].broadcast_to([P, NC, CHUNK]), chunks, ALU.subtract).then_inc(b_ready.sem, 1)
                elif kind == "hc":
                    h, s = step[1], step[1] % 2
                    dve.wait_ge(e_ready.sem, e_ready.upto(b, h + 1))
                    dve.tensor_tensor(q_in[s][:], q_in[s][:], q_h[h][:], ALU.mult)
                    dve.tensor_tensor(k_end[s][:], k_end[s][:], f_gate[h][:], ALU.mult)
                    dve.drain()
                    dve.tensor_tensor(f_gate[h][:], f_gate[h][:], t_a[:], ALU.mult)
                    dve.tensor_tensor(q_h[h][:], q_h[h][:], t_b[:], ALU.mult).then_inc(gates_ready.sem, 1)
                elif kind == "sm1":
                    u, s, kv = step[1], step[1] % 2, step[1] % 2
                    dve.wait_ge(sc_full.sem, sc_full.upto(b, u + 1))
                    dve.tensor_reduce(top[:, s, :], sc[kv][:].rearrange("p (i c) -> p i c", c=P), AX.X, ALU.max)
                    dve.drain()
                    dve.scalar_tensor_tensor(out=top[:, s, :], in0=top[:, s, :], scalar=HD ** -0.5, in1=sink[:, kv, :], op0=ALU.mult, op1=ALU.max)
                    dve.drain()
                    dve.tensor_scalar(neg_top[:, s, :], top[:, s, :], -1.0, None, ALU.mult)
                    dve.tensor_tensor(sink_less[:, s, :], sink[:, kv, :], top[:, s, :], ALU.subtract).then_inc(sink_less_ready.sem, 1)
                elif kind == "sm2":
                    u, s = step[1], step[1] % 2
                    dve.wait_ge(exp_ready.sem, exp_ready.upto(b, u + 1))
                    dve.tensor_tensor(denom[:, s, :], denom[:, s, :], sink_e[:, s, :], ALU.add)
                    dve.drain()
                    dve.reciprocal(denom[:, s, :], denom[:, s, :])
                    dve.drain()
                    dve.tensor_tensor(prob[s][:], prob[s][:], denom[:, s, :, None].broadcast_to([P, 4, P]), ALU.mult).then_inc(prob_ready.sem, 1)
                elif kind == "pv":
                    t = step[1]
                    dve.wait_ge(yA_hi_ready.sem, yA_hi_ready.upto(b, t + 1))
                    split_cols = "p j (c q) -> p j c q"
                    dve.tensor_tensor(yA_lo[:, :, t * P:(t + 1) * P].rearrange(split_cols, c=2),
                                      pvb[:].rearrange("p (c j q) -> p j c q", c=2, j=4),
                                      yA_hi[:, :, t * P:(t + 1) * P].rearrange(split_cols, c=2).bitcast(F32), ALU.subtract).then_inc(yA_ready.sem, 1)
                elif kind == "att":
                    h = step[1]
                    dve.wait_ge(att_full.sem, att_full.upto(b, h + 1))
                    dve.sem_inc(dve_waited, 1)
                    dve.copy_predicated(att_m[:], causal[:].broadcast_to([P, TT, P]), hb[:].rearrange("p (t c) -> p t c", c=P)).then_inc(att_ready.sem, 1)
                elif kind == "ds" and step[2] == 1:
                    h = step[1]
                    dve.wait_ge(tr_full.sem, tr_full.upto(b, use + 1))
                    dve.tensor_copy(state[:, 0, :], carry[:, h, :])
                    for c in range(NC):
                        dve.drain()
                        ps = tr[(use - 1 + c % 2) % 2][:, (c // 2) * P:(c // 2 + 1) * P]
                        last = dve.scalar_tensor_tensor(out=state[:, c + 1, :] if c < NC - 1 else carry[:, h, :], in0=state[:, c, :],
                                                        scalar=decay[:, h, c:c + 1], in1=ps, op0=ALU.mult, op1=ALU.add)
                    last.then_inc(state_ready.sem, 1)
                elif kind == "on1":
                    h = step[1]
                    dve.wait_ge(o_sq_ready.sem, o_sq_ready.upto(b, h + 1))
                    dve.tensor_scalar(o_ss[:], o_ss[:], 1.0 / P, EPS, ALU.mult, ALU.add).then_inc(o_ms_ready.sem, 1)
                elif kind == "on2":
                    h = step[1]
                    dve.wait_ge(o_rs_ready.sem, o_rs_ready.upto(b, h + 1))
                    dve.tensor_tensor(y_nat[:], hb[:].rearrange("p (t c) -> p t c", c=P), o_rs[:, :, None].broadcast_to([P, TT, P]), ALU.mult).then_inc(hb_read.sem, 1)
                elif kind == "on3":
                    h = step[1]
                    dve.drain()
                    dve.wait_ge(g_ready.sem, g_ready.upto(b, TT if h < 2 else 2 * TT))
                    dve.tensor_tensor(y_nat[:], y_nat[:], g_nat[:, :, h * P:(h + 1) * P], ALU.mult).then_inc(y_nat_ready.sem, 1)
                elif kind == "yt":
                    h = step[1]
                    dve.wait_ge(yH_hi_ready.sem, yH_hi_ready.upto(b, h + 1))
                    low_part(yH_lo[h][:], tr[use % 2][:], gnw[:, 0:1], yH_hi[h][:], yH_ready)
                elif kind == "n1a":
                    mean_square_x(b)
                elif kind == "n1b":
                    scale_x(b)
                elif kind == "xT":
                    evacuate_x(b, step[1], use)
                if kind in TR_KINDS:
                    use += 1


def build_phase_b(nc, ctx, dram, x_mid, out):
    def sem(name):
        return ctx.enter_context(nc.semaphore(name))

    def signal(name, per_pass, ahead=0):
        return Signal(nc, ctx, name, per_pass, ahead)

    put = Places(nc).put
    ident = put("b_ident", [P, P], F32)
    n2w = put("b_n2w", [P, D], F32)
    neg_half = put("b_neg_half", [P, 4], F32)
    h_hi = put("b_h_hi", [P, KT, TH], F32R)
    h_lo = put("b_h_lo", [P, KT, TH], F32R)
    acc = put("b_acc", [P, HT, D], F32)
    gu_stage = [put(f"b_gu_stage{s}", [P, KT, 2 * P], F32) for s in range(2)]
    gu_hi = [put(f"b_gu_hi{s}", [P, KT, 2 * P], F32R) for s in range(2)]
    gu_lo = [put(f"b_gu_lo{s}", [P, KT, 2 * P], F32R) for s in range(2)]
    dn_stage = [put(f"b_dn_stage{s}", [P, D], F32) for s in range(2)]
    dn_hi = [put(f"b_dn_hi{s}", [P, D], F32R) for s in range(2)]
    dn_lo = [put(f"b_dn_lo{s}", [P, D], F32R) for s in range(2)]
    a_hi = [put(f"b_a_hi{s}", [P, TH], F32R) for s in range(2)]
    a_lo = [put(f"b_a_lo{s}", [P, TH], F32R) for s in range(2)]
    silu = [put(f"b_silu{s}", [P, 512], F32) for s in range(2)]
    a_full = [put(f"b_a_full{s}", [P, 512], F32) for s in range(2)]
    xn = [put(f"b_xn{s}", [P, D], F32) for s in range(2)]
    ss = put("b_ss", [P, HT], F32)
    rs = put("b_rs", [P, HT], F32)

    gu = [ctx.enter_context(nc.psum_tensor(f"b_gu{s}", [P, 512], F32)) for s in range(4)]
    wide = [ctx.enter_context(nc.psum_tensor(f"b_wide{s}", [P, D], F32)) for s in range(2)]

    consts_in, consts_set, pool_waited = sem("b_consts_in"), sem("b_consts_set"), sem("b_pool_waited")
    gu_loaded = [sem(f"gu_loaded{s}") for s in range(2)]
    dn_loaded = [sem(f"dn_loaded{s}") for s in range(2)]
    acc_loaded = [sem(f"acc_loaded{s}") for s in range(2)]
    stored = sem("stored")
    gu_hi_ready = signal("gu_hi_ready", FT)
    gu_lo_ready = signal("gu_lo_ready", FT, 2)
    dn_hi_ready = signal("dn_hi_ready", FT)
    dn_lo_ready = signal("dn_lo_ready", FT, 2)
    ss_ready = signal("b_ss_ready", 2)
    ms_ready = signal("b_ms_ready", 2)
    rs_ready = signal("b_rs_ready", 2)
    xn_ready = signal("b_xn_ready", HT)
    xT_full = signal("b_xT_full", HT)
    h_hi_ready = signal("b_h_hi_ready", HT)
    h_ready = signal("b_h_ready", HT)
    gu_full = signal("gu_full", 4 * FT, 5)
    silu_ready = signal("silu_ready", 2 * FT, 2)
    a_full_ready = signal("a_full_ready", 2 * FT, 2)
    a_hi_ready = signal("a_hi_ready", 2 * FT)
    a_ready = signal("a_ready", 2 * FT)
    dn_full = signal("dn_full", HT * FT, 17)
    acc_done = signal("acc_done", HT * FT, 2)

    def tiles(eng, whole):
        whole(0, 0, down=False)
        with eng.Fori(0, (FT - 2) // 2) as i:
            whole(2 * i + 1, 1)
            whole(2 * i + 2, 0)
        whole(FT - 1, 1)

    blk = ctx.enter_context(nc.Block())

    @blk.sync
    def _(sp):
        sp.dma_start(ident[:], dram["ident"]).then_inc(consts_in, 16)
        sp.dma_start(n2w[:], dram["n2w"]).then_inc(consts_in, 16)
        with sp.Fori(0, 2) as half:
            with sp.Fori(0, FT // 2) as i:
                for s in range(2):
                    sp.wait_ge(gu_lo_ready.sem, half * FT + (2 * i + (s + 1)))
                    sp.dma_start(gu_stage[s][:], dram["w_gu"][bass.ds(2 * i + s, 1)].rearrange("o p k n -> p (o k) n")).then_inc(gu_loaded[s], 16)
                    sp.wait_ge(dn_lo_ready.sem, half * FT + (2 * i + (s + 1)))
                    sp.dma_start(dn_stage[s][:], dram["w_dn"][bass.ds(2 * i + s, 1)].rearrange("o p n -> p (o n)")).then_inc(dn_loaded[s], 16)

    mid = x_mid.rearrange("(h q t p) d -> h q p t d", h=2, q=2, p=P)
    out_v = out.rearrange("(h q t p) d -> h q p t d", h=2, q=2, p=P)

    @blk.gpsimd
    def _(pool):
        pool.memset(neg_half[:], -0.5).then_inc(consts_set, 1)
        pool.wait_ge(consts_set, 1)
        with pool.Fori(0, 2) as half:
            for q in range(2):
                pool.dma_start(acc[:, 4 * q:4 * q + 4, :], mid[bass.ds(half, 1), q].rearrange("o p t d -> p (o t) d")).then_inc(acc_loaded[q], 16)
            for q in range(2):
                pool.drain()
                pool.wait_ge(ms_ready.sem, ms_ready.upto(half, q + 1))
                pool.tensor_tensor(rs[:, 4 * q:4 * q + 4], ss[:, 4 * q:4 * q + 4], neg_half[:], ALU.pow).then_inc(rs_ready.sem, 1)
            for q in range(2):
                pool.wait_ge(acc_done.sem, acc_done.upto(half, HT * (FT - 1) + 4 * q + 4))
                pool.sem_inc(pool_waited, 1)
                pool.dma_start(out_v[bass.ds(half, 1), q].rearrange("o p t d -> p (o t) d"), acc[:, 4 * q:4 * q + 4, :]).then_inc(stored, 16)
            pool.wait_ge(stored, half * 32 + 32)

    @blk.scalar
    def _(act):
        with act.Fori(0, 2) as half:
            def split_gu(j, s):
                act.wait_ge(gu_loaded[s], half * (8 * FT) + (j - s) * 8 + 16)
                act.wait_ge(gu_full.sem, half * (4 * FT) + (j * 4 + 1))
                act.activation(gu_hi[s][:], gu_stage[s][:], ACT.Copy).then_inc(gu_hi_ready.sem, 1)

            def split_dn(j, s):
                act.wait_ge(dn_loaded[s], half * (8 * FT) + (j - s) * 8 + 16)
                act.wait_ge(dn_full.sem, half * (HT * FT) + (j * HT + 1))
                act.activation(dn_hi[s][:], dn_stage[s][:], ACT.Copy).then_inc(dn_hi_ready.sem, 1)

            for t in range(HT):
                if t % 4 == 0:
                    act.wait_ge(acc_loaded[t // 4], half * 16 + 16)
                if t % 4 == 0 and t:
                    pass
                last = act.activation(silu[0][:].bitcast(BF16), acc[:, t, :], ACT.Square, accum_out=ss[:, t:t + 1])
                if t % 4 == 3:
                    last.then_inc(ss_ready.sem, 1)
                act.drain()
            split_gu(0, 0)
            for t in range(HT):
                act.wait_ge(xT_full.sem, xT_full.upto(half, t + 1))
                act.activation(h_hi[:, :, t * P:(t + 1) * P], wide[t % 2][:].rearrange("p (k c) -> p k c", c=P), ACT.Copy).then_inc(h_hi_ready.sem, 1)

            def whole(j, s, down=True):
                static_last = isinstance(j, int) and j == FT - 1
                if not static_last:
                    split_gu(j + 1, 1 - s)
                for tb in range(2):
                    act.wait_ge(gu_full.sem, gu_full.upto(half, 0) + (j * 4 + (2 * tb + 1)))
                    act.wait_ge(a_full_ready.sem, a_full_ready.upto(half, 0) + (j * 2 + (tb - 1)))
                    act.activation(silu[tb][:], gu[2 * tb][:], ACT.Silu).then_inc(silu_ready.sem, 1)
                    if tb == 0:
                        split_dn(j, s)
                    act.wait_ge(a_full_ready.sem, a_full_ready.upto(half, 0) + (j * 2 + (tb + 1)))
                    act.activation(a_hi[s][:, tb * 512:(tb + 1) * 512], a_full[tb][:], ACT.Copy).then_inc(a_hi_ready.sem, 1)

            tiles(act, whole)

    @blk.tensor
    def _(pe):
        pe.sem_inc(gu_full.sem, 5)
        pe.sem_inc(dn_full.sem, 17)
        pe.wait_ge(consts_in, 32)
        with pe.Fori(0, 2) as half:
            for t in range(HT):
                pe.wait_ge(xn_ready.sem, xn_ready.upto(half, t + 1))
                if t >= 2:
                    pe.wait_ge(h_ready.sem, h_ready.upto(half, t - 1))
                else:
                    pe.wait_ge(acc_done.sem, acc_done.upto(half, 0))
                for k in range(KT):
                    last = pe.transpose(wide[t % 2][:, k * P:(k + 1) * P], xn[t % 2][:, k * P:(k + 1) * P], ident[:])
                last.then_inc(xT_full.sem, 1)
            pe.wait_ge(h_ready.sem, h_ready.upto(half, HT))

            def down(j, s, t):
                if t == 0:
                    pe.wait_ge(a_ready.sem, half * (2 * FT) + (j * 2 + 2))
                    pe.wait_ge(dn_lo_ready.sem, half * FT + (j + 3))
                pe.wait_ge(acc_done.sem, half * (HT * FT) + (j * HT + (t + 1)))
                rows = slice(t * P, (t + 1) * P)
                for n in range(2):
                    cols = slice(n * 512, (n + 1) * 512)
                    pe.matmul(wide[t % 2][:, cols], a_hi[s][:, rows], dn_hi[s][:, cols], start=True, stop=False)
                    pe.matmul(wide[t % 2][:, cols], a_hi[s][:, rows], dn_lo[s][:, cols], start=False, stop=False)
                    last = pe.matmul(wide[t % 2][:, cols], a_lo[s][:, rows], dn_hi[s][:, cols], start=False, stop=True)
                last.then_inc(dn_full.sem, 1)

            def whole(j, s, down_before=True, **kw):
                with_down = kw.get("down", True)
                pe.wait_ge(gu_lo_ready.sem, half * FT + (j + 3))
                for g in range(4):
                    tb, up = g // 2, g % 2
                    read = a_full_ready if up else silu_ready
                    pe.wait_ge(read.sem, half * (2 * FT) + (j * 2 + (tb + 1)))
                    cols = slice(up * P, (up + 1) * P)
                    toks = slice(tb * 512, (tb + 1) * 512)
                    last = three_passes(pe, gu[g][:],
                                        (lambda k: gu_hi[s][:, k, cols], lambda k: gu_lo[s][:, k, cols]),
                                        (lambda k: h_hi[:, k, toks], lambda k: h_lo[:, k, toks]))
                    last.then_inc(gu_full.sem, 1)
                    if with_down:
                        down(j - 1, 1 - s, 2 * g)
                        down(j - 1, 1 - s, 2 * g + 1)

            tiles(pe, whole)
            for t in range(HT):
                down(FT - 1, (FT - 1) % 2, t)

    @blk.vector
    def _(dve):
        for s, n in ((gu_lo_ready, 2), (dn_lo_ready, 2), (acc_done, 2), (silu_ready, 2), (a_full_ready, 2)):
            dve.sem_inc(s.sem, n)
        dve.wait_ge(consts_in, 32)
        with dve.Fori(0, 2) as half:
            def low(out, full, hi, ready):
                dve.tensor_tensor(out, full, hi.bitcast(F32), ALU.subtract).then_inc(ready.sem, 1)

            def split_gu(j, s):
                dve.wait_ge(gu_hi_ready.sem, half * FT + (j + 1))
                low(gu_lo[s][:], gu_stage[s][:], gu_hi[s][:], gu_lo_ready)

            def split_dn(j, s):
                dve.wait_ge(dn_hi_ready.sem, half * FT + (j + 1))
                low(dn_lo[s][:], dn_stage[s][:], dn_hi[s][:], dn_lo_ready)

            def scaled(t):
                dve.scalar_tensor_tensor(out=xn[t % 2][:], in0=acc[:, t, :], scalar=rs[:, t:t + 1], in1=n2w[:], op0=ALU.mult, op1=ALU.mult).then_inc(xn_ready.sem, 1)

            def h_low(t):
                dve.wait_ge(h_hi_ready.sem, h_hi_ready.upto(half, t + 1))
                low(h_lo[:, :, t * P:(t + 1) * P], wide[t % 2][:].rearrange("p (k c) -> p k c", c=P), h_hi[:, :, t * P:(t + 1) * P], h_ready)

            for q in range(2):
                dve.wait_ge(ss_ready.sem, ss_ready.upto(half, q + 1))
                dve.tensor_scalar(ss[:, 4 * q:4 * q + 4], ss[:, 4 * q:4 * q + 4], 1.0 / D, EPS, ALU.mult, ALU.add).then_inc(ms_ready.sem, 1)
            split_gu(0, 0)
            for t in range(HT):
                if t % 4 == 0:
                    dve.wait_ge(rs_ready.sem, rs_ready.upto(half, t // 4 + 1))
                scaled(t)
                if t >= 1:
                    h_low(t - 1)
            h_low(HT - 1)

            def add(j, t):
                dve.wait_ge(dn_full.sem, half * (HT * FT) + (j * HT + (t + 18)))
                dve.tensor_tensor(acc[:, t, :], acc[:, t, :], wide[t % 2][:], ALU.add).then_inc(acc_done.sem, 1)

            def whole(j, s, down=True):
                if not (isinstance(j, int) and j == FT - 1):
                    split_gu(j + 1, 1 - s)
                for tb in range(2):
                    if down:
                        add(j - 1, 4 * tb)
                        add(j - 1, 4 * tb + 1)
                    dve.wait_ge(gu_full.sem, half * (4 * FT) + (j * 4 + (2 * tb + 2 + 5)))
                    dve.wait_ge(silu_ready.sem, half * (2 * FT) + (j * 2 + (tb + 3)))
                    dve.tensor_tensor(a_full[tb][:], silu[tb][:], gu[2 * tb + 1][:], ALU.mult).then_inc(a_full_ready.sem, 1)
                    if tb == 0:
                        split_dn(j, s)
                    if down:
                        add(j - 1, 4 * tb + 2)
                    dve.wait_ge(a_hi_ready.sem, half * (2 * FT) + (j * 2 + (tb + 1)))
                    low(a_lo[s][:, tb * 512:(tb + 1) * 512], a_full[tb][:], a_hi[s][:, tb * 512:(tb + 1) * 512], a_ready)
                    if down:
                        add(j - 1, 4 * tb + 3)

            tiles(dve, whole)
            for t in range(HT):
                add(FT - 1, t)


def build(nc, dram, out):
    x_mid = nc.dram_tensor("x_mid", [SEQ, D], F32, kind="Internal").ap()
    with ExitStack() as ctx:
        build_phase_a(nc, ctx, dram, x_mid)
    with ExitStack() as ctx:
        build_phase_b(nc, ctx, dram, x_mid, out)


def rope_table():
    half = ROPE // 2
    inv = np.float32(500000.0) ** (-np.arange(half, dtype=np.float32) * np.float32(2.0) / np.float32(ROPE))
    angle = np.arange(SEQ, dtype=np.float32)[:, None] * inv[None, :].astype(np.float32)
    c, s = np.cos(angle).astype(np.float32), np.sin(angle).astype(np.float32)
    table = np.concatenate([c, c, -s, s], axis=1).reshape(NB, TT, P, 4 * half).transpose(0, 2, 1, 3)
    return np.ascontiguousarray(np.concatenate([table, table[:1]]))


def laid_out(x, w_in, w_out, norm1_w, norm2_w, q_norm_w, k_norm_w, attn_sinks, hgrn_lb_logits, hgrn_gnorm_w,
             w_gate_up, w_down):
    f = lambda a: np.asarray(a)
    x, w_in, w_out, w_gate_up, w_down = f(x)[0], f(w_in)[0], f(w_out)[0], f(w_gate_up)[0], f(w_down)[0]
    by_k = lambda w: w.reshape(KT, P, -1).transpose(1, 0, 2)
    heads = w_out[:N_Q * HD].reshape(2, 4, HD, D)
    rows = np.concatenate([heads.transpose(1, 0, 2, 3).reshape(N_Q * HD, D), w_out[N_Q * HD:]])
    whole = [by_k(w_in[:, c:c + n]) for _, c, n in CHUNKS if n == WC] + [by_k(rows[:, c:c + WC]) for c in range(0, D, WC)]
    sinks = f(attn_sinks)[0].reshape(N_KV, 1, 2, 2, 1)
    sinks = np.broadcast_to(sinks, (N_KV, 2, 2, 2, HD)).transpose(3, 4, 0, 1, 2).reshape(P, N_KV, 4)
    s = np.arange(P)
    causal = (s[:, None] // CHUNK == s[None, :] // CHUNK) & (s[:, None] <= s[None, :])
    qk_weight = np.stack([f(q_norm_w)[0], f(k_norm_w)[0]])
    return {
        "x_pad": np.concatenate([x, x[:TB]]).reshape(NB + 1, TB, D),
        "w_half": np.stack([by_k(w_in[:, c:c + n]) for _, c, n in CHUNKS if n < WC]),
        "w_whole": np.stack(whole),
        "ident": np.eye(P, dtype=np.float32),
        "causal": causal[:, None, :].astype(np.uint32),
        "qk_weight": np.broadcast_to(qk_weight, (P, 2, HD)),
        "sink": sinks,
        "n1w": f(norm1_w)[0].reshape(KT, P).T,
        "n2w": np.broadcast_to(f(norm2_w)[0], (P, D)),
        "gnw": f(hgrn_gnorm_w)[0].reshape(P, 1),
        "lb": f(hgrn_lb_logits).reshape(2, HG, P).transpose(2, 0, 1),
        "rope": rope_table(),
        "w_gu": np.stack([np.concatenate([by_k(w_gate_up[:, j * P:(j + 1) * P]), by_k(w_gate_up[:, D_FF + j * P:D_FF + (j + 1) * P])], axis=2)
                          for j in range(FT)]),
        "w_dn": w_down.reshape(FT, P, D),
    }


def kernel(**inputs):
    import concourse.bacc as bacc
    from concourse.bass_utils import run_bass_kernel_spmd

    nc = bacc.Bacc("TRN2", target_bir_lowering=False, num_devices=1)
    arrays = {k: np.ascontiguousarray(a) for k, a in laid_out(**inputs).items()}
    dram = {k: nc.dram_tensor(k, a.shape, mybir.dt.from_np(a.dtype), kind="ExternalInput").ap() for k, a in arrays.items()}
    out = nc.dram_tensor("y", (SEQ, D), F32, kind="ExternalOutput").ap()
    build(nc, dram, out)
    r = run_bass_kernel_spmd(nc, [arrays], core_ids=[0])
    return r.results[0]["y"].reshape(1, SEQ, D)
```

```python
from contextlib import ExitStack

import numpy as np

import concourse.bass as bass
from concourse import mybir

F32 = mybir.dt.float32
F32R = mybir.dt.float32r
BF16 = mybir.dt.bfloat16
U32 = mybir.dt.uint32
ALU = mybir.AluOpType
ACT = mybir.ActivationFunctionType
AX = mybir.AxisListType

P = 128
SEQ, D = 2048, 1024
KT = D // P
CHUNK = 64
HD = 64
N_Q, N_KV = 8, 2
SLOTS = N_Q + N_KV
ROPE = HD // 4
HG = 4
D_FF = 2816
FT = D_FF // P
EPS = 1e-6
NEG = -1e30

TB = 512
NB = SEQ // TB
TT = TB // P
NC = TB // CHUNK
WC = 256
TH = 1024
HT = TH // P
XN = 3

CHUNKS = [("KV", 512, 256), ("QA0", 0, 256), ("QA1", 256, 256), ("F0", 1280, 128), ("F1", 1408, 128),
          ("Q01", 768, 256), ("I01", 1792, 256), ("G01", 2304, 256), ("F23", 1536, 256), ("Q23", 1024, 256),
          ("I23", 2048, 256), ("G23", 2560, 256)]
NW = len(CHUNKS) + D // WC
FIRST_HEAD = {"F0": 0, "F1": 1, "F23": 2, "Q01": 0, "Q23": 2}
HALF_CHUNKS = [n for n, c in enumerate(CHUNKS) if c[2] < WC]
WHOLE_CHUNKS = [n for n in range(NW) if n not in HALF_CHUNKS]


def chunk_name(n):
    return CHUNKS[n][0] if n < len(CHUNKS) else f"WO{n - len(CHUNKS)}"


def chunk_groups(n):
    name = chunk_name(n)
    return CHUNKS[n][2] // P if name in FIRST_HEAD else TT


GROUPS_TO = [sum(chunk_groups(m) for m in range(n)) for n in range(NW + 1)]
N_GROUPS = GROUPS_TO[NW]
CHUNK_AT = {chunk_name(n): n for n in range(NW)}


def block_steps():
    at = {}

    def after(name, group, *steps):
        at.setdefault((name, group), []).extend(steps)

    after("KV", 3, ("vmix",))
    after("QA1", 0, ("qn1", 0))
    after("QA1", 1, ("qn1", 1))
    after("QA1", 2, ("qn1", 2))
    after("QA1", 3, ("qn2", 0))
    after("F0", 0, ("qn1", 3), ("qn2", 1))
    after("F1", 0, ("qn2", 2), ("qn2", 3))
    after("Q01", 0, ("qT", 0), ("qT", 1), ("qT", 2), ("qT", 3), ("kT",))
    after("Q01", 1, ("sc", 0), ("sm1", 0), ("sm1", 1))
    after("I01", 0, ("ha", 0))
    after("I01", 1, ("sm2", 0), ("sm2", 1), ("sc", 1))
    after("I01", 2, ("pt", 0), ("pt", 1), ("sm1", 2), ("sm1", 3), ("hb", 0))
    after("I01", 3, ("sm2", 2), ("sm2", 3), ("pv", 0), ("sc", 2))
    after("G01", 0, ("pt", 2), ("pt", 3), ("sm1", 4), ("sm1", 5), ("xload",), ("hc", 0), ("ha", 1))
    after("G01", 1, ("sm2", 4), ("sm2", 5), ("pv", 1), ("sc", 3), ("split", CHUNK_AT["F23"]))
    after("G01", 2, ("pt", 4), ("pt", 5), ("att", 0), ("kt", 0), ("sm1", 6), ("sm1", 7), ("hb", 1))
    after("G01", 3, ("ds", 0, 0), ("ds", 0, 1), ("sm2", 6), ("sm2", 7), ("pv", 2), ("hc", 1))
    after("F23", 0, ("pt", 6), ("pt", 7))
    after("F23", 1, ("pv", 3), ("o", 0), ("on1", 0), ("kt", 1), ("ha", 2), ("sq", 0))
    after("Q23", 0, ("on2", 0), ("on3", 0), ("split", CHUNK_AT["I23"]), ("ds", 1, 0), ("ds", 1, 1), ("hb", 2), ("att", 1), ("sq", 1))
    after("Q23", 1, ("yt", 0), ("hc", 2), ("o", 1), ("on1", 1))
    after("I23", 0, ("on2", 1), ("on3", 1), ("ha", 3))
    after("I23", 1, ("yt", 1), ("att", 2), ("kt", 2), ("sq", 2))
    after("I23", 2, ("sq", 3))
    after("I23", 3, ("hb", 3),)
    after("G23", 0, ("ds", 2, 0), ("ds", 2, 1), ("hc", 3), ("n1a",))
    after("G23", 1, ("o", 2), ("on1", 2), ("kt", 3), ("n1b",))
    after("G23", 2, ("on2", 2), ("ds", 3, 0), ("ds", 3, 1), ("att", 3))
    after("G23", 3, ("on3", 2), ("o", 3), ("on1", 3), ("yt", 2), ("on2", 3), ("on3", 3))
    after("WO0", 0, ("xT", 0))
    after("WO0", 1, ("xT", 1))
    after("WO0", 2, ("xT", 2))
    after("WO1", 0, ("xT", 3))
    after("WO1", 2, ("xT", 4))
    after("WO2", 0, ("xT", 5))
    after("WO2", 2, ("xT", 6))
    after("WO3", 0, ("xT", 7))
    placed = [step[1] for group in at.values() for step in group if step[0] == "split"]
    steps = []
    for n in range(NW):
        early = chunk_groups(n) < TT or chunk_name(n) == "WO0"
        for g in range(chunk_groups(n)):
            if g == 0 and early and n + 1 not in placed:
                steps.append(("split", n + 1))
            if (chunk_name(n), g) == ("WO0", 0):
                steps.append(("yt", 3))
            steps.append(("proj", n, g))
            steps += at.pop((chunk_name(n), g), [])
            if g == 0 and not early and n + 1 not in placed:
                steps.append(("split", n + 1))
    assert not at, at
    return steps


STEPS = block_steps()
LAST_YT_AT = 3
TR_KINDS = ("qT", "pt", "kt", "ds", "yt", "xT")
TR_USES = [s for s in STEPS if s[0] in TR_KINDS]
assert len(TR_USES) % 2 == 0


class Signal:

    def __init__(self, nc, ctx, name, per_pass, ahead=0):
        self.sem = ctx.enter_context(nc.semaphore(name))
        self.per_pass, self.ahead = per_pass, ahead

    def upto(self, n_pass, k):
        return n_pass * self.per_pass + (k + self.ahead)


class Places:

    def __init__(self, nc, at=0):
        self.nc, self.at = nc, at or (nc.sbuf_base + 63) // 64 * 64

    def put(self, name, shape, dt, at=None):
        size = int(np.prod(shape[1:])) * (2 if dt == BF16 else 4)
        offset = self.at if at is None else at
        if at is None:
            self.at += (size + 31) // 32 * 32
            assert self.at <= self.nc.sbuf_usable_end, (name, self.at)
        return self.nc.alloc_sbuf_tensor_at(name, list(shape), dt, offset=offset)


class Kept:

    def __init__(self, nc):
        mem = Places(nc)
        self.ident = mem.put("ident", [P, P], F32)
        self.mid_ms = mem.put("mid_ms", [P, NB * TT], F32)
        self.end = mem.at


def three_passes(pe, out, stationary, moving, tiles=range(KT), before=None):
    for k in tiles:
        if before is not None:
            before(k)
        pe.matmul(out, stationary[0](k), moving[0](k), start=(k == 0), stop=False)
        pe.matmul(out, stationary[0](k), moving[1](k), start=False, stop=False)
        last = pe.matmul(out, stationary[1](k), moving[0](k), start=False, stop=(k == KT - 1))
    return last


def build_phase_a(nc, ctx, dram, x_mid, kept):
    def sem(name):
        return ctx.enter_context(nc.semaphore(name))

    def signal(name, per_pass, ahead=0):
        return Signal(nc, ctx, name, per_pass, ahead)

    ident, mid_ms = kept.ident, kept.mid_ms
    mem = Places(nc, kept.end)
    put = mem.put
    causal = put("a_causal", [P, 1, P], U32)
    qk_weight = put("a_qk_weight", [P, 2, HD], F32)
    sink = put("a_sink", [P, N_KV, 4], F32)
    n1w = put("a_n1w", [P, KT], F32)
    gnw = put("a_gnw", [P, 1], F32)
    lb_in = put("a_lb_in", [P, 2, HG], F32)
    lb_e = put("a_lb_e", [P, 4, HG], F32)
    lb = put("a_lb", [P, HG], F32)
    one_less_lb = put("a_one_less_lb", [P, HG], F32)
    neg_half = put("a_neg_half", [P, SLOTS], F32)
    ones_row = put("a_ones_row", [1, P], F32)
    penalty = put("a_penalty", [1, P], F32)
    not_start = put("a_not_start", [P, TB], BF16)
    rope = put("a_rope", [P, TT, 4 * ROPE // 2], F32)
    w_stage = [put(f"a_w_stage{s}", [P, KT, WC], F32) for s in range(2)]
    w_hi = [put(f"a_w_hi{s}", [P, KT, WC], F32R) for s in range(2)]
    w_lo = [put(f"a_w_lo{s}", [P, KT, WC], F32R) for s in range(2)]
    hT_hi = put("a_hT_hi", [P, KT, TB], F32R)
    hT_lo = put("a_hT_lo", [P, KT, TB], F32R)
    yA_hi = put("a_yA_hi", [P, HG, TB], F32R)
    yA_lo = put("a_yA_lo", [P, HG, TB], F32R)
    arena = mem.at
    x_in = put("a_x_in", [P, TT, D], F32)
    qk = put("a_qk", [P, TT, SLOTS, HD], F32, at=arena)
    qk_sq = put("a_qk_sq", [P, SLOTS, HD], F32, at=arena + TT * SLOTS * HD * 4)
    rope_u = put("a_rope_u", [P, SLOTS, ROPE], F32, at=arena + TT * SLOTS * HD * 4)
    rope_v = put("a_rope_v", [P, SLOTS, ROPE], F32, at=arena + TT * SLOTS * HD * 4 + SLOTS * ROPE * 4)
    x_res = [put(f"a_x_res{s}", [P, TT, WC], F32) for s in range(2)]
    qT = put("a_qT", [P, NC, 4, CHUNK], F32)
    kT = put("a_kT", [P, TT, P], F32)
    kT_even = put("a_kT_even", [P, TT, P], F32)
    v_nat = put("a_v_nat", [P, TT, P], F32)
    v_even = put("a_v_even", [P, TT + 1, P], F32)
    i_nat = put("a_i_nat", [P, TT, HG * P], F32)
    g_nat = put("a_g_nat", [P, TT, HG * P], F32)
    f_at, f_gate, q_h, yH_hi, yH_lo = [], [], [], [], []
    for h in range(HG):
        f_at.append(mem.at)
        f_gate.append(put(f"a_f_gate{h}", [P, TB], F32))
        yH_hi.append(put(f"a_yH_hi{h}", [P, TB], F32R, at=f_at[h]))
        q_at = mem.at
        q_h.append(put(f"a_q_h{h}", [P, TB], F32))
        yH_lo.append(put(f"a_yH_lo{h}", [P, TB], F32R, at=q_at))
    q_in = [put(f"a_q_in{s}", [P, TB], F32) for s in range(2)]
    k_end = [put(f"a_k_end{s}", [P, TB], F32) for s in range(2)]
    t_a = put("a_t_a", [P, TB], F32)
    t_b = put("a_t_b", [P, TB], F32)
    decay = put("a_decay", [P, HG, NC], F32)
    prob_at = mem.at
    prob = [put(f"a_prob{s}", [P, 4, P], F32) for s in range(2)]
    probT = [put(f"a_probT{s}", [P, 4, P], F32) for s in range(2)]
    att_m = put("a_att_m", [P, TT, P], F32)
    k_nat = put("a_k_nat", [P, TT, P], F32)
    state = put("a_state", [P, NC, P], F32)
    carry = put("a_carry", [P, HG, P], F32)
    y_nat = put("a_y_nat", [P, TT, P], F32)
    junk = put("a_junk", [P, D], BF16, at=prob_at)
    o_sq = put("a_o_sq", [P, TT, P], BF16)
    ss = put("a_ss", [P, TT], F32)
    x_rs = put("a_x_rs", [P, TT], F32)
    q_ss = put("a_q_ss", [P, TT, SLOTS], F32)
    q_rs = put("a_q_rs", [P, TT, SLOTS], F32)
    o_ss = put("a_o_ss", [P, TT], F32)
    o_rs = put("a_o_rs", [P, TT], F32)
    top = put("a_top", [P, 2, 4], F32)
    neg_top = put("a_neg_top", [P, 2, 4], F32)
    sink_less = put("a_sink_less", [P, 2, 4], F32)
    sink_e = put("a_sink_e", [P, 2, 4], F32)
    denom = put("a_denom", [P, 2, 4], F32)
    mid_ss = put("a_mid_ss", [P, TT, 4], F32)
    mid_sum = put("a_mid_sum", [P, TT], F32)
    mid_old = put("a_mid_old", [P, (NB - 1) * TT], F32)

    def bank(name):
        return ctx.enter_context(nc.psum_tensor(name, [P, 512], F32))

    pj = [bank(f"a_pj{s}") for s in range(2)]
    tr = [bank(f"a_tr{s}") for s in range(2)]
    sc = [bank(f"a_sc{s}") for s in range(2)]
    pvb = bank("a_pv")
    hb = bank("a_hb")

    consts_in = sem("consts_in")
    w_loaded = [sem(f"w_loaded{s}") for s in range(2)]
    x_loaded, rope_loaded = sem("x_loaded"), sem("rope_loaded")
    xr_loaded = [sem(f"xr_loaded{s}") for s in range(2)]
    xr_stored = [sem(f"xr_stored{s}") for s in range(2)]
    w_hi_ready = signal("w_hi_ready", NW, 1)
    w_lo_ready = signal("w_lo_ready", NW, 1)
    pj_full = signal("pj_full", N_GROUPS, 1)
    tr_full = signal("tr_full", len(TR_USES), KT)
    first_x_loaded = [sem(f"first_x_loaded{t}") for t in range(TT)]
    first_ss_ready, first_ms_ready, first_rs_ready = sem("first_ss_ready"), sem("first_ms_ready"), sem("first_rs_ready")
    ss_ready = signal("ss_ready", 1)
    ms_ready = signal("ms_ready", 1)
    x_rs_ready = signal("x_rs_ready", 1)
    xn_ready = signal("xn_ready", 1, 1)
    h_hi_ready = signal("h_hi_ready", KT, KT)
    hT_ready = signal("hT_ready", KT, KT)
    f_ready = signal("f_ready", HG)
    q_ready = signal("q_ready", HG)
    g_ready = signal("g_ready", 2 * TT)
    kv_ready = signal("kv_ready", TT)
    qa_ready = signal("qa_ready", 2 * TT)
    i_ready = signal("i_ready", 2 * TT)
    v_even_ready = signal("v_even_ready", 1)
    q_ms_ready = signal("q_ms_ready", TT)
    q_rs_ready = signal("q_rs_ready", TT)
    qk_ready = signal("qk_ready", TT)
    kT_full = signal("kT_full", 1)
    qT_ready = signal("qT_ready", 4)
    kT_ready = signal("kT_ready", 1)
    sc_full = signal("sc_full", 8)
    sink_less_ready = signal("sink_less_ready", 8)
    exp_ready = signal("exp_ready", 8)
    prob_ready = signal("prob_ready", 8)
    probT_ready = signal("probT_ready", 8)
    pv_full = signal("pv_full", TT)
    yA_hi_ready = signal("yA_hi_ready", TT)
    yA_ready = signal("yA_ready", TT, 1)
    fg_ready = signal("fg_ready", HG)
    lf_ready = signal("lf_ready", HG)
    b_ready = signal("b_ready", HG)
    e_ready = signal("e_ready", HG)
    gates_ready = signal("gates_ready", HG, 1)
    att_full = signal("att_full", HG)
    att_ready = signal("att_ready", HG)
    k_nat_ready = signal("k_nat_ready", HG)
    state_ready = signal("state_ready", HG)
    o_full = signal("o_full", HG)
    o_sq_ready = signal("o_sq_ready", HG)
    o_ms_ready = signal("o_ms_ready", HG)
    o_rs_ready = signal("o_rs_ready", HG)
    hb_read = signal("hb_read", HG, 1)
    y_nat_ready = signal("y_nat_ready", HG)
    yH_hi_ready = signal("yH_hi_ready", HG)
    yH_ready = signal("yH_ready", HG)
    res_done = signal("res_done", 4 * TT, 1)
    mid_squared = signal("mid_squared", 4 * TT)
    mid_ready = signal("mid_ready", 1, 1)
    pool_waited, dve_waited = sem("pool_waited"), sem("dve_waited")
    pool_set, dve_set, act_set = sem("pool_set"), sem("dve_set"), sem("act_set")

    tr_read = {"qT": (qT_ready, lambda s: s[1] + 1), "pt": (probT_ready, lambda s: s[1] + 1),
               "kt": (k_nat_ready, lambda s: s[1] + 1), "ds": (state_ready, lambda s: s[1] + 1),
               "yt": (yH_ready, lambda s: s[1] + 1), "xT": (hT_ready, lambda s: s[1] + 1)}
    pj_read = []
    counts = {}
    for n in range(NW):
        kind = chunk_name(n)[:2] if chunk_name(n)[:2] in ("KV", "QA", "WO") else chunk_name(n)[0]
        for g in range(chunk_groups(n)):
            counts[kind] = counts.get(kind, 0) + 1
            s = {"F": f_ready, "Q": q_ready, "G": g_ready, "KV": kv_ready, "QA": qa_ready, "I": i_ready,
                 "WO": res_done}[kind]
            pj_read.append((s, counts[kind]))

    blk = ctx.enter_context(nc.Block())

    @blk.sync
    def _(sp):
        def load(n):
            m = n % NW
            if m in HALF_CHUNKS:
                sp.dma_start(w_stage[n % 2][:, :, 0:P], dram["w_half"][HALF_CHUNKS.index(m)]).then_inc(w_loaded[n % 2], 16)
            else:
                sp.dma_start(w_stage[n % 2][:, :, :], dram["w_whole"][WHOLE_CHUNKS.index(m)]).then_inc(w_loaded[n % 2], 16)

        first = dram["x_pad"][0].rearrange("(t p) d -> p t d", p=P)
        for t in range(TT):
            sp.dma_start(x_in[:, t, :], first[:, t, :]).then_inc(first_x_loaded[t], 16)
        load(0)
        for name, tile in (("ident", ident), ("causal", causal), ("qk_weight", qk_weight), ("sink", sink),
                           ("n1w", n1w), ("gnw", gnw), ("lb", lb_in)):
            sp.dma_start(tile[:], dram[name]).then_inc(consts_in, 16)
        with sp.Fori(0, NB) as b:
            for n in range(1, NW + 1):
                sp.wait_ge(w_lo_ready.sem, w_lo_ready.upto(b, max(n - 2, 0)))
                load(n)

    @blk.gpsimd
    def _(pool):
        def wait(sem, value):
            pool.wait_ge(sem, value)
            pool.sem_inc(pool_waited, 1)

        def load_rope(b):
            pool.dma_start(rope[:], dram["rope"][bass.ds(b, 1)].rearrange("o p t c -> p (o t) c")).then_inc(rope_loaded, 16)

        def load_block(b):
            pool.dma_start(x_in[:], dram["x_pad"][bass.ds(b, 1)].rearrange("o (t p) d -> p (o t) d", p=P)).then_inc(x_loaded, 16)
            load_rope(b)

        load_rope(0)
        pool.memset(neg_half[:], -0.5)
        pool.memset(ones_row[:], 1.0)
        pool.memset(penalty[:, 0:CHUNK], 0.0)
        pool.memset(penalty[:, CHUNK:P], NEG)
        pool.memset(kT[:], 0.0)
        pool.memset(v_even[:], 0.0)
        pool.memset(carry[:], 0.0)
        pool.memset(att_m[:], 0.0)
        pool.memset(mid_ms[:], 0.0)
        pool.memset(not_start[:], 1.0)
        pool.drain()
        pool.memset(not_start[:].rearrange("p (c s) -> p c s", s=CHUNK)[:, :, 0:1], 0.0).then_inc(pool_set, 1)

        def power(out, in_, width, ready, done, value, shape=None):
            pool.drain()
            pool.wait_ge(ready.sem, value)
            pool.tensor_tensor(out, in_, neg_half[:, 0:width], ALU.pow).then_inc(done.sem, 1)

        pool.drain()
        for t in range(TT):
            pool.wait_ge(first_ms_ready, t + 1)
            pool.tensor_tensor(x_rs[:, t:t + 1], ss[:, t:t + 1], neg_half[:, 0:1], ALU.pow).then_inc(first_rs_ready, 1)
        x_cols = dram["x_pad"].rearrange("b (t p) (c n) -> b p t c n", p=P, n=WC)
        mid_cols = x_mid.rearrange("(b t p) (c n) -> b p t c n", b=NB, p=P, n=WC)
        with pool.Fori(0, NB) as b:
            def load_res(c, b=b):
                pool.dma_start(x_res[c % 2][:], x_cols[bass.ds(b, 1), :, :, c, :].rearrange("o p t n -> p (o t) n")).then_inc(xr_loaded[c % 2], 16)

            def store_res(c, b=b):
                wait(mid_squared.sem, mid_squared.upto(b, TT * (c + 1)))
                pool.dma_start(mid_cols[bass.ds(b, 1), :, :, c, :].rearrange("o p t n -> p (o t) n"), x_res[c % 2][:]).then_inc(xr_stored[c % 2], 16)

            for step in STEPS:
                kind = step[0]
                if kind == "vmix":
                    wait(kv_ready.sem, kv_ready.upto(b, TT))
                    pool.drain()
                    pool.tensor_copy(v_even[CHUNK:P, 0, :], v_even[CHUNK:P, TT, :])
                    pool.drain()
                    pool.tensor_copy(v_even[0:CHUNK, 0:TT, :], v_nat[0:CHUNK, :, :])
                    pool.drain()
                    pool.tensor_copy(v_even[CHUNK:P, 1:TT + 1, :], v_nat[CHUNK:P, :, :]).then_inc(v_even_ready.sem, 1)
                elif kind == "qn1":
                    t = step[1]
                    power(q_rs[:, t, :], q_ss[:, t, :], SLOTS, q_ms_ready, q_rs_ready, q_ms_ready.upto(b, t + 1))
                elif kind == "sc" and step[1] == 1:
                    wait(sc_full.sem, sc_full.upto(b, 2))
                    pool.drain()
                    pool.memset(penalty[:, CHUNK:P], 0.0)
                elif kind == "xload":
                    wait(kT_full.sem, kT_full.upto(b, 1))
                    load_block(b + 1)
                    load_res(0)
                    load_res(1)
                elif kind == "on1":
                    h = step[1]
                    power(o_rs[:], o_ss[:], TT, o_ms_ready, o_rs_ready, o_ms_ready.upto(b, h + 1))
                elif kind == "n1a":
                    power(x_rs[:], ss[:], TT, ms_ready, x_rs_ready, ms_ready.upto(b, 1))
                elif kind == "proj" and chunk_name(step[1]).startswith("WO") and step[2] == TT - 1:
                    c = step[1] - len(CHUNKS)
                    store_res(c)
                    wait(xr_stored[c % 2], b * 32 + 16 * (c // 2 + 1))
                    if c < 2:
                        load_res(c + 2)

    @blk.scalar
    def _(act):
        def split(b, n):
            s = n % 2
            loaded = b * (16 * NW // 2) + 16 * ((n + 1) // 2 + (1 - s))
            act.wait_ge(w_loaded[s], loaded)
            if n >= 1:
                act.wait_ge(pj_full.sem, pj_full.upto(b, GROUPS_TO[max(n - 1, 0)]))
            cols = P if n % NW in HALF_CHUNKS else WC
            act.activation(w_hi[s][:, :, 0:cols], w_stage[s][:, :, 0:cols], ACT.Copy).then_inc(w_hi_ready.sem, 1)

        def square_x(b, t):
            act.drain()
            if t == 0:
                act.wait_ge(x_loaded, b * 16 + 16)
            last = act.activation(junk[:], x_in[:, t, :], ACT.Square, accum_out=ss[:, t:t + 1])
            if t == TT - 1:
                last.then_inc(ss_ready.sem, 1)

        def evacuate_x(b, k, use):
            act.wait_ge(tr_full.sem, tr_full.upto(b, use + 1))
            act.activation(hT_hi[:, k, :], tr[use % 2][:], ACT.Copy, scale=n1w[:, k:k + 1]).then_inc(h_hi_ready.sem, 1)

        for t in range(TT):
            act.wait_ge(first_x_loaded[t], 16)
            act.activation(junk[:], x_in[:, t, :], ACT.Square, accum_out=ss[:, t:t + 1]).then_inc(first_ss_ready, 1)
            act.drain()
        split(0, 0)
        act.wait_ge(consts_in, 7 * 16)
        for k in range(KT):
            evacuate_x(-1, k, len(TR_USES) - KT + k)
        act.wait_ge(dve_set, 1)
        act.activation(lb_e[:, 0:2, :], lb_e[:, 2:4, :], ACT.Exp).then_inc(act_set, 1)

        with act.Fori(0, NB) as b:
            use = 0
            table = [None]

            def use_exp_table():
                if table[0] != "exp":
                    act.preload_act_table_set("natural_log_exp_and_others")
                table[0] = "exp"

            for step in STEPS:
                kind = step[0]
                if kind == "proj" and chunk_name(step[1])[0] in "FQG" and chunk_name(step[1])[:2] != "QA":
                    table[0] = "other"
                if kind == "split":
                    split(b, step[1])
                elif kind == "proj":
                    n, g = step[1:]
                    name, ps = chunk_name(n), pj[(GROUPS_TO[n] + g) % 2]
                    if name.startswith("WO"):
                        c = n - len(CHUNKS)
                        if g == 0:
                            act.drain()
                        act.wait_ge(res_done.sem, res_done.upto(b, TT * c + g + 1))
                        act.activation(junk[:, g * WC:(g + 1) * WC], x_res[c % 2][:, g, :], ACT.Square,
                                       accum_out=mid_ss[:, g, c:c + 1]).then_inc(mid_squared.sem, 1)
                        continue
                    act.wait_ge(pj_full.sem, pj_full.upto(b, GROUPS_TO[n] + g + 1))
                    if name[0] == "F":
                        act.activation(f_gate[FIRST_HEAD[name] + g][:], ps[:], ACT.Sigmoid).then_inc(f_ready.sem, 1)
                    elif name in FIRST_HEAD:
                        act.activation(q_h[FIRST_HEAD[name] + g][:], ps[:], ACT.Silu).then_inc(q_ready.sem, 1)
                    elif name[0] == "G":
                        c0 = WC * (name == "G23")
                        act.activation(g_nat[:, g, c0:c0 + WC], ps[:, 0:WC], ACT.Silu).then_inc(g_ready.sem, 1)
                    elif name == "KV":
                        act.activation(qk[:, g, N_Q:SLOTS, :], ps[:, 0:P].rearrange("p (s d) -> p s d", d=HD), ACT.Copy)
                        act.activation(v_nat[:, g, :], ps[:, P:2 * P], ACT.Copy).then_inc(kv_ready.sem, 1)
                    elif name[:2] == "QA":
                        half = int(name[2])
                        act.activation(qk[:, g, half:N_Q:2, :], ps[:, 0:WC].rearrange("p (s d) -> p s d", d=HD), ACT.Copy).then_inc(qa_ready.sem, 1)
                    else:
                        c0 = WC * (name == "I23")
                        act.activation(i_nat[:, g, c0:c0 + WC], ps[:, 0:WC], ACT.Copy).then_inc(i_ready.sem, 1)
                elif kind == "ha":
                    h = step[1]
                    use_exp_table()
                    act.wait_ge(fg_ready.sem, fg_ready.upto(b, h + 1))
                    act.wait_ge(gates_ready.sem, gates_ready.upto(b, h))
                    act.activation(t_a[:], f_gate[h][:], ACT.Ln).then_inc(lf_ready.sem, 1)
                elif kind == "hb":
                    h, s = step[1], step[1] % 2
                    use_exp_table()
                    act.wait_ge(b_ready.sem, b_ready.upto(b, h + 1))
                    act.activation(q_in[s][:], t_a[:], ACT.Exp)
                    act.activation(k_end[s][:], k_end[s][:], ACT.Exp)
                    act.activation(decay[:, h, :], t_b[:].rearrange("p (c s) -> p c s", s=CHUNK)[:, :, CHUNK - 1], ACT.Exp)
                    act.drain()
                    act.activation(t_a[:], t_a[:], ACT.Exp, scale=-1.0)
                    act.activation(t_b[:], t_b[:], ACT.Exp).then_inc(e_ready.sem, 1)
                elif kind == "qT":
                    j = step[1]
                    act.wait_ge(tr_full.sem, tr_full.upto(b, use + 1))
                    act.activation(qT[:, :, j, :], tr[use % 2][:].rearrange("p (c q) -> p c q", q=CHUNK), ACT.Copy).then_inc(qT_ready.sem, 1)
                elif kind == "kT":
                    act.wait_ge(kT_full.sem, kT_full.upto(b, 1))
                    ps = sc[0][:].rearrange("p (t c) -> p t c", c=P)
                    act.activation(kT_even[:, 0, CHUNK:P], kT[:, TT - 1, CHUNK:P], ACT.Copy)
                    act.drain()
                    act.activation(kT[:], ps, ACT.Copy)
                    act.activation(kT_even[:, :, 0:CHUNK], ps[:, :, 0:CHUNK], ACT.Copy)
                    act.activation(kT_even[:, 1:TT, CHUNK:P], ps[:, 0:TT - 1, CHUNK:P], ACT.Copy).then_inc(kT_ready.sem, 1)
                elif kind == "sm1":
                    u, s, kv = step[1], step[1] % 2, step[1] % 2
                    use_exp_table()
                    act.wait_ge(sink_less_ready.sem, sink_less_ready.upto(b, u + 1))
                    act.activation(sink_e[:, s, :], sink_less[:, s, :], ACT.Exp)
                    for i in range(4):
                        last = act.activation(prob[s][:, i, :], sc[kv][:, i * P:(i + 1) * P], ACT.Exp,
                                              bias=neg_top[:, s, i:i + 1], scale=HD ** -0.5, accum_out=denom[:, s, i:i + 1])
                    last.then_inc(exp_ready.sem, 1)
                elif kind == "pt":
                    u = step[1]
                    act.wait_ge(tr_full.sem, tr_full.upto(b, use + 1))
                    act.activation(probT[u % 2][:].rearrange("p i c -> p (i c)"), tr[use % 2][:], ACT.Copy).then_inc(probT_ready.sem, 1)
                elif kind == "pv":
                    t = step[1]
                    act.wait_ge(pv_full.sem, pv_full.upto(b, t + 1))
                    act.activation(yA_hi[:, :, t * P:(t + 1) * P].rearrange("p j (c q) -> p j c q", c=2),
                                   pvb[:].rearrange("p (c j q) -> p j c q", c=2, j=4), ACT.Copy).then_inc(yA_hi_ready.sem, 1)
                elif kind == "kt":
                    h = step[1]
                    act.wait_ge(tr_full.sem, tr_full.upto(b, use + 1))
                    act.activation(k_nat[:].rearrange("p t c -> p (t c)"), tr[use % 2][:], ACT.Copy).then_inc(k_nat_ready.sem, 1)
                elif kind == "on1":
                    h = step[1]
                    act.wait_ge(o_full.sem, o_full.upto(b, h + 1))
                    for t in range(TT):
                        last = act.activation(o_sq[:, t, :], hb[:, t * P:(t + 1) * P], ACT.Square, accum_out=o_ss[:, t:t + 1])
                    last.then_inc(o_sq_ready.sem, 1)
                elif kind == "yt":
                    h = step[1]
                    act.wait_ge(tr_full.sem, tr_full.upto(b, use + 1))
                    act.activation(yH_hi[h][:], tr[use % 2][:], ACT.Copy, scale=gnw[:, 0:1]).then_inc(yH_hi_ready.sem, 1)
                elif kind == "sq":
                    square_x(b, step[1])
                elif kind == "xT":
                    evacuate_x(b, step[1], use)
                if kind in TR_KINDS:
                    use += 1

    @blk.tensor
    def _(pe):
        def transpose_x(b, k, use, after=None):
            if k == 0:
                pe.wait_ge(xn_ready.sem, xn_ready.upto(b, 1))
            for t in range(TT):
                last = pe.transpose(tr[use % 2][:, t * P:(t + 1) * P], x_in[:, t, k * P:(k + 1) * P], ident[:])
            last.then_inc(tr_full.sem, 1)

        def bank_read(b, use):
            if use >= 2:
                read, index = tr_read[TR_USES[use - 2][0]]
                pe.wait_ge(read.sem, read.upto(b, index(TR_USES[use - 2])))

        def transpose_y(b, h, use):
            pe.wait_ge(y_nat_ready.sem, y_nat_ready.upto(b, h + 1))
            bank_read(b, use)
            for t in range(TT):
                last = pe.transpose(tr[use % 2][:, t * P:(t + 1) * P], y_nat[:, t, :], ident[:])
            last.then_inc(tr_full.sem, 1)

        pe.sem_inc(pj_full.sem, 1)
        pe.wait_ge(consts_in, 7 * 16)
        pe.wait_ge(pool_set, 1)
        for k in range(KT):
            if k >= 2:
                pe.wait_ge(hT_ready.sem, hT_ready.upto(-1, k - 1))
            transpose_x(-1, k, len(TR_USES) - KT + k)

        with pe.Fori(0, NB) as b:
            use = 0
            for step in STEPS:
                kind = step[0]
                if kind == "proj":
                    n, g = step[1:]
                    name, at, s = chunk_name(n), GROUPS_TO[n] + g, n % 2
                    if g == 0:
                        pe.wait_ge(w_lo_ready.sem, w_lo_ready.upto(b, n))
                    if (name, g) != ("WO0", 1):
                        read, index = pj_read[at - 2]
                        pe.wait_ge(read.sem, read.upto(b, index) if at >= 2 else res_done.upto(b, 0))
                    if name in FIRST_HEAD:
                        cols = slice(g * P, (g + 1) * P)
                        last = three_passes(pe, pj[at % 2][:],
                                            (lambda k: w_hi[s][:, k, cols], lambda k: w_lo[s][:, k, cols]),
                                            (lambda k: hT_hi[:, k, :], lambda k: hT_lo[:, k, :]))
                    else:
                        rows = slice(g * P, (g + 1) * P)
                        if name[:2] == "WO":
                            if n == len(CHUNKS) and g == 0:
                                pe.wait_ge(yA_ready.sem, yA_ready.upto(b, TT))
                                pe.wait_ge(yH_ready.sem, yH_ready.upto(b, HG - 2))
                            still = (lambda k: yA_hi[:, k, rows] if k < HG else yH_hi[k - HG][:, rows],
                                     lambda k: yA_lo[:, k, rows] if k < HG else yH_lo[k - HG][:, rows])
                        else:
                            still = (lambda k: hT_hi[:, k, rows], lambda k: hT_lo[:, k, rows])
                        moving = (lambda k: w_hi[s][:, k, :], lambda k: w_lo[s][:, k, :])
                        if (name, g) == ("WO0", 0):
                            three_passes(pe, pj[at % 2][:, 0:WC], still, moving, range(KT - 2))
                            pe.wait_ge(yH_ready.sem, yH_ready.upto(b, HG - 1))
                            three_passes(pe, pj[at % 2][:, 0:WC], still, moving, range(KT - 2, KT - 1))
                            read, index = pj_read[at - 1]
                            pe.wait_ge(read.sem, read.upto(b, index))
                            other_rows = slice(P, 2 * P)
                            other = (lambda k: yA_hi[:, k, other_rows] if k < HG else yH_hi[k - HG][:, other_rows],
                                     lambda k: yA_lo[:, k, other_rows] if k < HG else yH_lo[k - HG][:, other_rows])
                            three_passes(pe, pj[(at + 1) % 2][:, 0:WC], other, moving, range(LAST_YT_AT))
                            transpose_y(b, HG - 1, TR_USES.index(("yt", HG - 1)))
                            three_passes(pe, pj[(at + 1) % 2][:, 0:WC], other, moving, range(LAST_YT_AT, KT - 1))
                            pe.wait_ge(yH_ready.sem, yH_ready.upto(b, HG))
                        left = range(KT - 1, KT) if (name, g) in (("WO0", 0), ("WO0", 1)) else range(KT)
                        arrived = (lambda k: pe.wait_ge(hT_ready.sem, hT_ready.upto(b - 1, k + 1))) if at == 0 else None
                        last = three_passes(pe, pj[at % 2][:, 0:WC], still, moving, left, arrived)
                    last.then_inc(pj_full.sem, 1)
                elif kind == "qT":
                    j = step[1]
                    if j == 0:
                        pe.wait_ge(qk_ready.sem, qk_ready.upto(b, TT))
                    bank_read(b, use)
                    for t in range(TT):
                        last = pe.transpose(tr[use % 2][:, t * P:(t + 1) * P], qk[:, t, 2 * j:2 * j + 2, :].rearrange("p s d -> p (s d)"), ident[:])
                    last.then_inc(tr_full.sem, 1)
                elif kind == "kT":
                    for t in range(TT):
                        last = pe.transpose(sc[0][:, t * P:(t + 1) * P], qk[:, t, N_Q:SLOTS, :].rearrange("p s d -> p (s d)"), ident[:])
                    last.then_inc(kT_full.sem, 1)
                elif kind == "sc":
                    t = step[1]
                    if t == 0:
                        pe.wait_ge(kT_ready.sem, kT_ready.upto(b, 1))
                        pe.wait_ge(v_even_ready.sem, v_even_ready.upto(b, 1))
                    for kv in range(N_KV):
                        rows = slice(kv * HD, (kv + 1) * HD)
                        if t > 0:
                            pe.wait_ge(exp_ready.sem, exp_ready.upto(b, 2 * (t - 1) + kv + 1))
                        for cc in range(2):
                            keys = kT if cc else kT_even
                            for jj in range(2):
                                i = 2 * cc + jj
                                first = t == 0 and cc == 0
                                last = pe.matmul(sc[kv][:, i * P:(i + 1) * P], qT[rows, 2 * t + cc, 2 * jj:2 * jj + 2, :].rearrange("p j q -> p (j q)"),
                                                 keys[rows, t, :], start=True, stop=not first)
                                if first:
                                    last = pe.matmul(sc[kv][:, i * P:(i + 1) * P], ones_row[:], penalty[:], start=False, stop=True)
                        last.then_inc(sc_full.sem, 1)
                elif kind == "pt":
                    u = step[1]
                    pe.wait_ge(prob_ready.sem, prob_ready.upto(b, u + 1))
                    bank_read(b, use)
                    for i in range(4):
                        last = pe.transpose(tr[use % 2][:, i * P:(i + 1) * P], prob[u % 2][:, i, :], ident[:])
                    last.then_inc(tr_full.sem, 1)
                elif kind == "pv":
                    t = step[1]
                    pe.wait_ge(probT_ready.sem, probT_ready.upto(b, 2 * t + 2))
                    pe.wait_ge(yA_ready.sem, yA_ready.upto(b, t))
                    for cc in range(2):
                        v = v_nat if cc else v_even
                        for kv in range(N_KV):
                            last = pe.matmul(pvb[kv * HD:(kv + 1) * HD, cc * 256:(cc + 1) * 256], v[:, t, kv * HD:(kv + 1) * HD],
                                             probT[kv][:, 2 * cc:2 * cc + 2, :].rearrange("p i c -> p (i c)"), start=True, stop=True)
                    last.then_inc(pv_full.sem, 1)
                elif kind == "att":
                    h = step[1]
                    pe.wait_ge(gates_ready.sem, gates_ready.upto(b, h + 1))
                    pe.wait_ge(hb_read.sem, hb_read.upto(b, h))
                    for t in range(TT):
                        last = pe.matmul(hb[:, t * P:(t + 1) * P], f_gate[h][:, t * P:(t + 1) * P],
                                         q_in[h % 2][:, t * P:(t + 1) * P], start=True, stop=True)
                    last.then_inc(att_full.sem, 1)
                elif kind == "kt":
                    h = step[1]
                    pe.wait_ge(gates_ready.sem, gates_ready.upto(b, h + 1))
                    bank_read(b, use)
                    for t in range(TT):
                        last = pe.transpose(tr[use % 2][:, t * P:(t + 1) * P], k_end[h % 2][:, t * P:(t + 1) * P], ident[:])
                    last.then_inc(tr_full.sem, 1)
                elif kind == "ds":
                    h, par = step[1:]
                    if par == 0:
                        pe.wait_ge(k_nat_ready.sem, k_nat_ready.upto(b, h + 1))
                        pe.wait_ge(i_ready.sem, i_ready.upto(b, TT if h < 2 else 2 * TT))
                    bank_read(b, use)
                    rows = slice(par * CHUNK, (par + 1) * CHUNK)
                    for t in range(TT):
                        last = pe.matmul(tr[use % 2][:, t * P:(t + 1) * P], k_nat[rows, t, :], i_nat[rows, t, h * P:(h + 1) * P], start=True, stop=True)
                    last.then_inc(tr_full.sem, 1)
                elif kind == "o":
                    h = step[1]
                    pe.wait_ge(att_ready.sem, att_ready.upto(b, h + 1))
                    pe.wait_ge(state_ready.sem, state_ready.upto(b, h + 1))
                    for t in range(TT):
                        cols = slice(t * P, (t + 1) * P)
                        pe.matmul(hb[:, cols], att_m[:, t, :], i_nat[:, t, h * P:(h + 1) * P], start=True, stop=True)
                        for cc in range(2):
                            at = t * P + cc * CHUNK
                            last = pe.matmul(hb[cc * CHUNK:(cc + 1) * CHUNK, cols], q_h[h][:, at:at + CHUNK], state[:, 2 * t + cc, :],
                                             start=False, stop=True, skip_group_check=True)
                    last.then_inc(o_full.sem, 1)
                elif kind == "yt" and step[1] < HG - 1:
                    transpose_y(b, step[1], use)
                elif kind == "xT":
                    bank_read(b, use)
                    transpose_x(b, step[1], use)
                if kind in TR_KINDS:
                    use += 1

    @blk.vector
    def _(dve):
        def split(b, n):
            s = n % 2
            cols = P if n % NW in HALF_CHUNKS else WC
            dve.wait_ge(w_hi_ready.sem, w_hi_ready.upto(b, n))
            dve.tensor_tensor(w_lo[s][:, :, 0:cols], w_stage[s][:, :, 0:cols], w_hi[s][:, :, 0:cols].bitcast(F32), ALU.subtract).then_inc(w_lo_ready.sem, 1)

        def mean_square_x(b):
            dve.wait_ge(ss_ready.sem, ss_ready.upto(b, 1))
            dve.tensor_scalar(ss[:], ss[:], 1.0 / D, EPS, ALU.mult, ALU.add).then_inc(ms_ready.sem, 1)

        def scale_x(b):
            dve.wait_ge(x_rs_ready.sem, x_rs_ready.upto(b, 1))
            for t in range(TT):
                last = dve.tensor_scalar(x_in[:, t, :], x_in[:, t, :], x_rs[:, t:t + 1], None, ALU.mult)
            last.then_inc(xn_ready.sem, 1)

        def low_part(out, ps, weight, hi, ready):
            dve.scalar_tensor_tensor(out=out, in0=ps, scalar=weight, in1=hi.bitcast(F32), op0=ALU.mult, op1=ALU.subtract).then_inc(ready.sem, 1)

        def evacuate_x(b, k, use):
            dve.wait_ge(h_hi_ready.sem, h_hi_ready.upto(b, k + 1))
            low_part(hT_lo[:, k, :], tr[use % 2][:], n1w[:, k:k + 1], hT_hi[:, k, :], hT_ready)

        for s in (yA_ready, gates_ready, hb_read, res_done):
            dve.sem_inc(s.sem, 1)
        for t in range(TT + 1):
            if t < TT:
                dve.wait_ge(first_ss_ready, t + 1)
                dve.tensor_scalar(ss[:, t:t + 1], ss[:, t:t + 1], 1.0 / D, EPS, ALU.mult, ALU.add).then_inc(first_ms_ready, 1)
            if t > 0:
                dve.wait_ge(first_rs_ready, t)
                last = dve.tensor_scalar(x_in[:, t - 1, :], x_in[:, t - 1, :], x_rs[:, t - 1:t], None, ALU.mult)
        last.then_inc(xn_ready.sem, 1)
        split(0, 0)
        dve.wait_ge(consts_in, 7 * 16)
        dve.wait_ge(pool_set, 1)
        for k in range(KT):
            evacuate_x(-1, k, len(TR_USES) - KT + k)
        dve.tensor_tensor(lb_e[:, 0, :], lb_in[:, 0, :], lb_in[:, 1, :], ALU.max)
        dve.drain()
        dve.tensor_tensor(lb_e[:, 2, :], lb_in[:, 0, :], lb_e[:, 0, :], ALU.subtract)
        dve.tensor_tensor(lb_e[:, 3, :], lb_in[:, 1, :], lb_e[:, 0, :], ALU.subtract).then_inc(dve_set, 1)
        dve.wait_ge(act_set, 1)
        dve.tensor_tensor(lb_e[:, 1, :], lb_e[:, 0, :], lb_e[:, 1, :], ALU.add)
        dve.drain()
        dve.reciprocal(lb_e[:, 2, :], lb_e[:, 1, :])
        dve.drain()
        dve.tensor_tensor(lb[:], lb_e[:, 0, :], lb_e[:, 2, :], ALU.mult)
        dve.drain()
        dve.tensor_scalar(one_less_lb[:], lb[:], -1.0, 1.0, ALU.mult, ALU.add)

        with dve.Fori(0, NB) as b:
            use = 0
            for step in STEPS:
                kind = step[0]
                if kind == "split":
                    split(b, step[1])
                elif kind == "proj" and chunk_name(step[1])[:2] == "WO":
                    n, g = step[1:]
                    c = n - len(CHUNKS)
                    if g == 0:
                        dve.wait_ge(xr_loaded[c % 2], b * 32 + 16 * (c // 2 + 1))
                    dve.wait_ge(pj_full.sem, pj_full.upto(b, GROUPS_TO[n] + g + 1))
                    dve.tensor_tensor(x_res[c % 2][:, g, :], x_res[c % 2][:, g, :], pj[(GROUPS_TO[n] + g) % 2][:, 0:WC], ALU.add).then_inc(res_done.sem, 1)
                elif kind == "qn1":
                    t = step[1]
                    dve.drain()
                    dve.wait_ge(qa_ready.sem, qa_ready.upto(b, TT + t + 1))
                    dve.tensor_tensor(qk_sq[:], qk[:, t, :, :], qk[:, t, :, :], ALU.mult)
                    dve.drain()
                    dve.tensor_reduce(q_ss[:, t, :], qk_sq[:], AX.X, ALU.add)
                    dve.drain()
                    dve.tensor_scalar(q_ss[:, t, :], q_ss[:, t, :], 1.0 / HD, EPS, ALU.mult, ALU.add).then_inc(q_ms_ready.sem, 1)
                elif kind == "qn2":
                    t = step[1]
                    q = qk[:, t, :, :]
                    dve.drain()
                    if t == 0:
                        dve.wait_ge(rope_loaded, b * 16 + 16)
                    dve.wait_ge(q_rs_ready.sem, q_rs_ready.upto(b, t + 1))
                    dve.tensor_tensor(q, q, q_rs[:, t, :, None].broadcast_to([P, SLOTS, HD]), ALU.mult)
                    dve.drain()
                    dve.tensor_tensor(q[:, 0:N_Q], q[:, 0:N_Q], qk_weight[:, 0:1, :].broadcast_to([P, N_Q, HD]), ALU.mult)
                    dve.tensor_tensor(q[:, N_Q:SLOTS], q[:, N_Q:SLOTS], qk_weight[:, 1:2, :].broadcast_to([P, N_KV, HD]), ALU.mult)
                    dve.drain()
                    half = ROPE // 2
                    cosines = rope[:, t:t + 1, 0:ROPE].broadcast_to([P, SLOTS, ROPE])
                    minus_sin = rope[:, t:t + 1, ROPE:ROPE + half].broadcast_to([P, SLOTS, half])
                    sin = rope[:, t:t + 1, ROPE + half:2 * ROPE].broadcast_to([P, SLOTS, half])
                    dve.tensor_tensor(rope_u[:], q[:, :, 0:ROPE], cosines, ALU.mult)
                    dve.tensor_tensor(rope_v[:, :, 0:half], q[:, :, half:ROPE], minus_sin, ALU.mult)
                    dve.tensor_tensor(rope_v[:, :, half:ROPE], q[:, :, 0:half], sin, ALU.mult)
                    dve.drain()
                    dve.tensor_tensor(q[:, :, 0:ROPE], rope_u[:], rope_v[:], ALU.add).then_inc(qk_ready.sem, 1)
                elif kind == "ha":
                    h = step[1]
                    dve.wait_ge(f_ready.sem, f_ready.upto(b, h + 1))
                    dve.tensor_scalar(f_gate[h][:], f_gate[h][:], one_less_lb[:, h:h + 1], lb[:, h:h + 1], ALU.mult, ALU.add).then_inc(fg_ready.sem, 1)
                elif kind == "hb":
                    h, s = step[1], step[1] % 2
                    dve.wait_ge(lf_ready.sem, lf_ready.upto(b, h + 1))
                    dve.tensor_scalar(f_gate[h][:], f_gate[h][:], -1.0, 1.0, ALU.mult, ALU.add)
                    dve.tensor_tensor_scan(t_b[:], not_start[:], t_a[:], 0.0, ALU.mult, ALU.add)
                    dve.drain()
                    chunks = t_b[:].rearrange("p (c s) -> p c s", s=CHUNK)
                    dve.tensor_tensor(t_a[:].rearrange("p (c s) -> p c s", s=CHUNK), chunks,
                                      chunks[:, :, CHUNK // 2:CHUNK // 2 + 1].broadcast_to([P, NC, CHUNK]), ALU.subtract)
                    if h >= 2:
                        dve.wait_ge(k_nat_ready.sem, k_nat_ready.upto(b, h - 1))
                    dve.tensor_tensor(k_end[s][:].rearrange("p (c s) -> p c s", s=CHUNK),
                                      chunks[:, :, CHUNK - 1:CHUNK].broadcast_to([P, NC, CHUNK]), chunks, ALU.subtract).then_inc(b_ready.sem, 1)
                elif kind == "hc":
                    h, s = step[1], step[1] % 2
                    dve.wait_ge(e_ready.sem, e_ready.upto(b, h + 1))
                    dve.tensor_tensor(q_in[s][:], q_in[s][:], q_h[h][:], ALU.mult)
                    dve.tensor_tensor(k_end[s][:], k_end[s][:], f_gate[h][:], ALU.mult)
                    dve.drain()
                    dve.tensor_tensor(f_gate[h][:], f_gate[h][:], t_a[:], ALU.mult)
                    dve.tensor_tensor(q_h[h][:], q_h[h][:], t_b[:], ALU.mult).then_inc(gates_ready.sem, 1)
                elif kind == "sm1":
                    u, s, kv = step[1], step[1] % 2, step[1] % 2
                    dve.wait_ge(sc_full.sem, sc_full.upto(b, u + 1))
                    dve.tensor_reduce(top[:, s, :], sc[kv][:].rearrange("p (i c) -> p i c", c=P), AX.X, ALU.max)
                    dve.drain()
                    dve.scalar_tensor_tensor(out=top[:, s, :], in0=top[:, s, :], scalar=HD ** -0.5, in1=sink[:, kv, :], op0=ALU.mult, op1=ALU.max)
                    dve.drain()
                    dve.tensor_scalar(neg_top[:, s, :], top[:, s, :], -1.0, None, ALU.mult)
                    dve.tensor_tensor(sink_less[:, s, :], sink[:, kv, :], top[:, s, :], ALU.subtract).then_inc(sink_less_ready.sem, 1)
                elif kind == "sm2":
                    u, s = step[1], step[1] % 2
                    dve.wait_ge(exp_ready.sem, exp_ready.upto(b, u + 1))
                    dve.tensor_tensor(denom[:, s, :], denom[:, s, :], sink_e[:, s, :], ALU.add)
                    dve.drain()
                    dve.reciprocal(denom[:, s, :], denom[:, s, :])
                    dve.drain()
                    dve.tensor_tensor(prob[s][:], prob[s][:], denom[:, s, :, None].broadcast_to([P, 4, P]), ALU.mult).then_inc(prob_ready.sem, 1)
                elif kind == "pv":
                    t = step[1]
                    dve.wait_ge(yA_hi_ready.sem, yA_hi_ready.upto(b, t + 1))
                    split_cols = "p j (c q) -> p j c q"
                    dve.tensor_tensor(yA_lo[:, :, t * P:(t + 1) * P].rearrange(split_cols, c=2),
                                      pvb[:].rearrange("p (c j q) -> p j c q", c=2, j=4),
                                      yA_hi[:, :, t * P:(t + 1) * P].rearrange(split_cols, c=2).bitcast(F32), ALU.subtract).then_inc(yA_ready.sem, 1)
                elif kind == "att":
                    h = step[1]
                    dve.wait_ge(att_full.sem, att_full.upto(b, h + 1))
                    dve.sem_inc(dve_waited, 1)
                    dve.copy_predicated(att_m[:], causal[:].broadcast_to([P, TT, P]), hb[:].rearrange("p (t c) -> p t c", c=P)).then_inc(att_ready.sem, 1)
                elif kind == "ds" and step[2] == 1:
                    h = step[1]
                    dve.wait_ge(tr_full.sem, tr_full.upto(b, use + 1))
                    dve.tensor_copy(state[:, 0, :], carry[:, h, :])
                    for c in range(NC):
                        dve.drain()
                        ps = tr[(use - 1 + c % 2) % 2][:, (c // 2) * P:(c // 2 + 1) * P]
                        last = dve.scalar_tensor_tensor(out=state[:, c + 1, :] if c < NC - 1 else carry[:, h, :], in0=state[:, c, :],
                                                        scalar=decay[:, h, c:c + 1], in1=ps, op0=ALU.mult, op1=ALU.add)
                    last.then_inc(state_ready.sem, 1)
                elif kind == "on1":
                    h = step[1]
                    dve.wait_ge(o_sq_ready.sem, o_sq_ready.upto(b, h + 1))
                    dve.tensor_scalar(o_ss[:], o_ss[:], 1.0 / P, EPS, ALU.mult, ALU.add).then_inc(o_ms_ready.sem, 1)
                elif kind == "on2":
                    h = step[1]
                    dve.wait_ge(o_rs_ready.sem, o_rs_ready.upto(b, h + 1))
                    dve.tensor_tensor(y_nat[:], hb[:].rearrange("p (t c) -> p t c", c=P), o_rs[:, :, None].broadcast_to([P, TT, P]), ALU.mult).then_inc(hb_read.sem, 1)
                elif kind == "on3":
                    h = step[1]
                    dve.drain()
                    dve.wait_ge(g_ready.sem, g_ready.upto(b, TT if h < 2 else 2 * TT))
                    dve.tensor_tensor(y_nat[:], y_nat[:], g_nat[:, :, h * P:(h + 1) * P], ALU.mult).then_inc(y_nat_ready.sem, 1)
                elif kind == "yt":
                    h = step[1]
                    dve.wait_ge(yH_hi_ready.sem, yH_hi_ready.upto(b, h + 1))
                    low_part(yH_lo[h][:], tr[use % 2][:], gnw[:, 0:1], yH_hi[h][:], yH_ready)
                elif kind == "n1a":
                    mean_square_x(b)
                elif kind == "n1b":
                    scale_x(b)
                elif kind == "xT":
                    evacuate_x(b, step[1], use)
                if kind in TR_KINDS:
                    use += 1
            dve.tensor_copy(mid_old[:], mid_ms[:, TT:])
            dve.wait_ge(mid_squared.sem, mid_squared.upto(b, 4 * TT))
            dve.tensor_reduce(mid_sum[:], mid_ss[:], AX.X, ALU.add)
            dve.drain()
            dve.tensor_copy(mid_ms[:, 0:(NB - 1) * TT], mid_old[:])
            dve.tensor_scalar(mid_ms[:, (NB - 1) * TT:], mid_sum[:], 1.0 / D, EPS, ALU.mult, ALU.add).then_inc(mid_ready.sem, 1)


def build_phase_b(nc, ctx, dram, x_mid, out, kept):
    def sem(name):
        return ctx.enter_context(nc.semaphore(name))

    def signal(name, per_pass, ahead=0):
        return Signal(nc, ctx, name, per_pass, ahead)

    ident, mid_ms = kept.ident, kept.mid_ms
    put = Places(nc, kept.end).put
    n2w = put("b_n2w", [P, D], F32)
    neg_half = put("b_neg_half", [P, HT], F32)
    rs = put("b_rs", [P, NB * TT], F32)
    h_hi = put("b_h_hi", [P, KT, TH], F32R)
    h_lo = put("b_h_lo", [P, KT, TH], F32R)
    acc = put("b_acc", [P, HT, D], F32)
    gu_stage = [put(f"b_gu_stage{s}", [P, KT, 2 * P], F32) for s in range(2)]
    gu_hi = [put(f"b_gu_hi{s}", [P, KT, 2 * P], F32R) for s in range(2)]
    gu_lo = [put(f"b_gu_lo{s}", [P, KT, 2 * P], F32R) for s in range(2)]
    dn_stage = [put(f"b_dn_stage{s}", [P, D], F32) for s in range(2)]
    dn_hi = [put(f"b_dn_hi{s}", [P, D], F32R) for s in range(2)]
    dn_lo = [put(f"b_dn_lo{s}", [P, D], F32R) for s in range(2)]
    a_hi = [put(f"b_a_hi{s}", [P, TH], F32R) for s in range(2)]
    a_lo = [put(f"b_a_lo{s}", [P, TH], F32R) for s in range(2)]
    silu = [put(f"b_silu{s}", [P, 512], F32) for s in range(2)]
    a_full = silu
    xn = [put(f"b_xn{s}", [P, D], F32) for s in range(XN)]

    gate_up = [ctx.enter_context(nc.psum_tensor(f"b_gate_up{s}", [P, D], F32)) for s in range(2)]
    gu = [gate_up[g // 2][:, (g % 2) * 512:(g % 2 + 1) * 512] for g in range(4)]
    wide = [ctx.enter_context(nc.psum_tensor(f"b_wide{s}", [P, D], F32)) for s in range(2)]

    n2w_in, consts_set, pool_waited = sem("b_n2w_in"), sem("b_consts_set"), sem("b_pool_waited")
    rs_ready = sem("b_rs_ready")
    gu_loaded = [sem(f"gu_loaded{s}") for s in range(2)]
    dn_loaded = [sem(f"dn_loaded{s}") for s in range(2)]
    xn_loaded = [sem(f"xn_loaded{s}") for s in range(XN)]
    acc_loaded = [sem(f"acc_loaded{s}") for s in range(2)]
    stored = [sem(f"stored{s}") for s in range(2)]
    gu_hi_ready = signal("gu_hi_ready", FT)
    gu_lo_ready = signal("gu_lo_ready", FT, 2)
    dn_hi_ready = signal("dn_hi_ready", FT)
    dn_lo_ready = signal("dn_lo_ready", FT, 2)
    xn_ready = signal("b_xn_ready", HT)
    xT_full = signal("b_xT_full", HT)
    h_hi_ready = signal("b_h_hi_ready", HT)
    h_ready = signal("b_h_ready", HT)
    gu_full = signal("gu_full", 4 * FT, 5)
    silu_ready = signal("silu_ready", 2 * FT, 2)
    a_full_ready = signal("a_full_ready", 2 * FT, 2)
    a_hi_ready = signal("a_hi_ready", 2 * FT)
    a_ready = signal("a_ready", 2 * FT, 2)
    dn_full = signal("dn_full", HT * FT, 17)
    acc_done = signal("acc_done", HT * FT, 2)

    def middle_tiles(eng, whole):
        with eng.Fori(0, (FT - 2) // 2) as i:
            whole(2 * i + 1, 1)
            whole(2 * i + 2, 0)

    def xT_bank(half, t):
        if t < 4:
            return gate_up[t % 2][:]
        return gate_up[1][:] if half else wide[t % 2][:]

    def before_in_xT_bank(half, t):
        if half == 0:
            return t - 2 if t % 4 >= 2 else None
        return t - 1 if t >= 4 else t - 2 if t >= 2 else None

    mid = x_mid.rearrange("(h t p) d -> h p t d", h=2, p=P)
    out_v = out.rearrange("(h t p) d -> h p t d", h=2, p=P)

    def xn_slot(half, t):
        return (half * HT + t) % XN

    def load_xn(eng, half, t):
        s = xn_slot(half, t)
        eng.dma_start(xn[s][:], mid[half, :, t, :]).then_inc(xn_loaded[s], 16)

    blk = ctx.enter_context(nc.Block())

    @blk.sync
    def _(sp):
        load_xn(sp, 0, 0)
        sp.dma_start(n2w[:], dram["n2w"]).then_inc(n2w_in, 16)
        for t in range(1, XN):
            load_xn(sp, 0, t)
        def load_weights(half, j, s):
            sp.wait_ge(gu_lo_ready.sem, half * FT + (j + 1))
            sp.dma_start(gu_stage[s][:], dram["w_gu"][bass.ds(j, 1)].rearrange("o p k n -> p (o k) n")).then_inc(gu_loaded[s], 16)
            sp.wait_ge(dn_lo_ready.sem, half * FT + (j + 1))
            sp.dma_start(dn_stage[s][:], dram["w_dn"][bass.ds(j, 1)].rearrange("o p n -> p (o n)")).then_inc(dn_loaded[s], 16)

        for half in range(2):
            if half:
                for t in range(XN):
                    sp.wait_ge(xT_full.sem, xT_full.upto(half, t + 1 - XN))
                    load_xn(sp, half, t)
            load_weights(half, 0, 0)
            if half:
                load_weights(half, 1, 1)
            for t in range(XN, HT):
                sp.wait_ge(xT_full.sem, xT_full.upto(half, t - XN + 1))
                load_xn(sp, half, t)
                if half == 0 and t == XN + 1:
                    load_weights(half, 1, 1)
            with sp.Fori(1, FT // 2) as i:
                for s in range(2):
                    load_weights(half, 2 * i + s, s)

    @blk.gpsimd
    def _(pool):
        pool.memset(neg_half[:], -0.5).then_inc(consts_set, 1)
        pool.wait_ge(consts_set, 1)
        for first, last in ((0, 2), (2, HT), (HT, 2 * HT)):
            pool.tensor_tensor(rs[:, first:last], mid_ms[:, first:last], neg_half[:, 0:last - first], ALU.pow).then_inc(rs_ready, 1)

        def load_acc(half, q):
            if half:
                pool.wait_ge(stored[q], 64 * half)
            pool.dma_start(acc[:, 4 * q:4 * q + 4, :], mid[half, :, 4 * q:4 * q + 4, :]).then_inc(acc_loaded[q], 16)

        def store(half, t):
            pool.wait_ge(acc_done.sem, acc_done.upto(half, HT * (FT - 1) + t + 1))
            pool.dma_start(out_v[half, :, t, :], acc[:, t, :]).then_inc(stored[t // 4], 16)

        for half in range(2):
            for t in range(HT):
                if half:
                    store(half - 1, t)
                if half and t == HT // 2:
                    load_acc(half, 0)
            if half == 0:
                pool.wait_ge(xT_full.sem, xT_full.upto(half, HT))
                load_acc(half, 0)
            load_acc(half, 1)
        for t in range(HT):
            store(1, t)
        for q in range(2):
            pool.wait_ge(stored[q], 128)

    @blk.scalar
    def _(act):
        for half in range(2):
            def split_gu(j, s):
                act.wait_ge(gu_loaded[s], half * (8 * FT) + (j - s) * 8 + 16)
                act.wait_ge(gu_full.sem, half * (4 * FT) + (j * 4 + 1))
                act.activation(gu_hi[s][:], gu_stage[s][:], ACT.Copy).then_inc(gu_hi_ready.sem, 1)

            def split_dn(j, s):
                act.wait_ge(dn_loaded[s], half * (8 * FT) + (j - s) * 8 + 16)
                act.wait_ge(dn_full.sem, half * (HT * FT) + (j * HT + 1))
                act.activation(dn_hi[s][:], dn_stage[s][:], ACT.Copy).then_inc(dn_hi_ready.sem, 1)

            def h_high(t):
                act.wait_ge(xT_full.sem, xT_full.upto(half, t + 1))
                act.activation(h_hi[:, :, t * P:(t + 1) * P], xT_bank(half, t).rearrange("p (k c) -> p k c", c=P), ACT.Copy).then_inc(h_hi_ready.sem, 1)

            def gate_silu(j, tb):
                act.wait_ge(gu_full.sem, gu_full.upto(half, 0) + (j * 4 + (2 * tb + 1)))
                act.wait_ge(a_ready.sem, half * (2 * FT) + (j * 2 + (tb + 1)))
                act.activation(silu[tb][:], gu[2 * tb], ACT.Silu).then_inc(silu_ready.sem, 1)

            def a_high(j, s, tb):
                act.wait_ge(a_full_ready.sem, a_full_ready.upto(half, 0) + (j * 2 + (tb + 1)))
                act.activation(a_hi[s][:, tb * 512:(tb + 1) * 512], a_full[tb][:], ACT.Copy).then_inc(a_hi_ready.sem, 1)

            def whole(j, s):
                if not (isinstance(j, int) and half * FT + j == 2 * FT - 1):
                    split_gu(j + 1, 1 - s)
                for tb in range(2):
                    gate_silu(j, tb)
                    if tb == 0:
                        split_dn(j, s)
                    a_high(j, s, tb)

            for t in range(5):
                h_high(t)
                if half == 0 and t == 1:
                    split_gu(0, 0)
            split_gu(1, 1)
            h_high(5)
            gate_silu(0, 0)
            h_high(6)
            h_high(7)
            split_dn(0, 0)
            a_high(0, 0, 0)
            gate_silu(0, 1)
            a_high(0, 0, 1)
            middle_tiles(act, whole)
            whole(FT - 1, 1)

    @blk.tensor
    def _(pe):
        pe.sem_inc(gu_full.sem, 5)
        pe.sem_inc(dn_full.sem, 17)
        for half in range(2):
            def transpose_x(t):
                pe.wait_ge(xn_ready.sem, xn_ready.upto(half, t + 1))
                if before_in_xT_bank(half, t) is not None:
                    pe.wait_ge(h_ready.sem, h_ready.upto(half, before_in_xT_bank(half, t) + 1))
                elif half:
                    pe.wait_ge(a_full_ready.sem, a_full_ready.upto(half, t - 1))
                for k in range(KT):
                    last = pe.transpose(xT_bank(half, t)[:, k * P:(k + 1) * P], xn[xn_slot(half, t)][:, k * P:(k + 1) * P], ident[:])
                last.then_inc(xT_full.sem, 1)

            def down(of_half, j, s, t):
                if t % 4 == 0:
                    pe.wait_ge(a_ready.sem, of_half * (2 * FT) + (j * 2 + (t // 4 + 3)))
                if t == 0:
                    pe.wait_ge(dn_lo_ready.sem, of_half * FT + (j + 3))
                pe.wait_ge(acc_done.sem, of_half * (HT * FT) + (j * HT + (t + 1)))
                rows = slice(t * P, (t + 1) * P)
                for n in range(2):
                    cols = slice(n * 512, (n + 1) * 512)
                    pe.matmul(wide[t % 2][:, cols], a_hi[s][:, rows], dn_hi[s][:, cols], start=True, stop=False)
                    pe.matmul(wide[t % 2][:, cols], a_hi[s][:, rows], dn_lo[s][:, cols], start=False, stop=False)
                    last = pe.matmul(wide[t % 2][:, cols], a_lo[s][:, rows], dn_hi[s][:, cols], start=False, stop=True)
                last.then_inc(dn_full.sem, 1)

            def gate_or_up(j, s, g):
                if g == 0:
                    pe.wait_ge(gu_lo_ready.sem, half * FT + (j + 3))
                tb, up = g // 2, g % 2
                read = a_full_ready if up else silu_ready
                pe.wait_ge(read.sem, half * (2 * FT) + (j * 2 + (tb + 1)))
                cols = slice(up * P, (up + 1) * P)
                toks = slice(tb * 512, (tb + 1) * 512)
                last = three_passes(pe, gu[g],
                                    (lambda k: gu_hi[s][:, k, cols], lambda k: gu_lo[s][:, k, cols]),
                                    (lambda k: h_hi[:, k, toks], lambda k: h_lo[:, k, toks]))
                last.then_inc(gu_full.sem, 1)

            def whole(j, s):
                for g in range(4):
                    gate_or_up(j, s, g)
                    for t in (2 * g, 2 * g + 1):
                        down(half, j - 1, 1 - s, t)

            for t in range(HT):
                transpose_x(t)
                if half:
                    down(half - 1, FT - 1, 1, t)
                if t in (4, 5):
                    if t == 4:
                        pe.wait_ge(h_ready.sem, h_ready.upto(half, 4))
                    gate_or_up(0, 0, t - 4)
            pe.wait_ge(h_ready.sem, h_ready.upto(half, HT))
            gate_or_up(0, 0, 2)
            gate_or_up(0, 0, 3)
            middle_tiles(pe, whole)
            whole(FT - 1, 1)
        for t in range(HT):
            down(1, FT - 1, 1, t)

    @blk.vector
    def _(dve):
        for s, n in ((gu_lo_ready, 2), (dn_lo_ready, 2), (acc_done, 2), (silu_ready, 2), (a_full_ready, 2), (a_ready, 2)):
            dve.sem_inc(s.sem, n)
        dve.wait_ge(n2w_in, 16)
        for half in range(2):
            def low(out, full, hi, ready):
                dve.tensor_tensor(out, full, hi.bitcast(F32), ALU.subtract).then_inc(ready.sem, 1)

            def split_gu(j, s):
                dve.wait_ge(gu_hi_ready.sem, half * FT + (j + 1))
                low(gu_lo[s][:], gu_stage[s][:], gu_hi[s][:], gu_lo_ready)

            def split_dn(j, s):
                dve.wait_ge(dn_hi_ready.sem, half * FT + (j + 1))
                low(dn_lo[s][:], dn_stage[s][:], dn_hi[s][:], dn_lo_ready)

            def scaled(of_half, t):
                if of_half == 0 and t in (0, 2) or of_half and t == 0:
                    dve.wait_ge(rs_ready, 3 if of_half else 1 + t // 2)
                at, slot = of_half * HT + t, xn_slot(of_half, t)
                dve.wait_ge(xn_loaded[slot], 16 * (at // XN + 1))
                dve.scalar_tensor_tensor(out=xn[slot][:], in0=xn[slot][:], scalar=rs[:, at:at + 1], in1=n2w[:], op0=ALU.mult, op1=ALU.mult).then_inc(xn_ready.sem, 1)

            def h_low(t):
                dve.wait_ge(h_hi_ready.sem, h_hi_ready.upto(half, t + 1))
                low(h_lo[:, :, t * P:(t + 1) * P], xT_bank(half, t).rearrange("p (k c) -> p k c", c=P), h_hi[:, :, t * P:(t + 1) * P], h_ready)

            def add(of_half, j, t):
                if t % 4 == 0:
                    dve.wait_ge(acc_loaded[t // 4], 16 * (of_half + 1))
                dve.wait_ge(dn_full.sem, of_half * (HT * FT) + (j * HT + (t + 18)))
                dve.tensor_tensor(acc[:, t, :], acc[:, t, :], wide[t % 2][:], ALU.add).then_inc(acc_done.sem, 1)

            def a_product(j, tb):
                dve.wait_ge(gu_full.sem, half * (4 * FT) + (j * 4 + (2 * tb + 2 + 5)))
                dve.wait_ge(silu_ready.sem, half * (2 * FT) + (j * 2 + (tb + 3)))
                dve.tensor_tensor(a_full[tb][:], silu[tb][:], gu[2 * tb + 1], ALU.mult).then_inc(a_full_ready.sem, 1)

            def a_low(j, s, tb):
                dve.wait_ge(a_hi_ready.sem, half * (2 * FT) + (j * 2 + (tb + 1)))
                low(a_lo[s][:, tb * 512:(tb + 1) * 512], a_full[tb][:], a_hi[s][:, tb * 512:(tb + 1) * 512], a_ready)

            def whole(j, s, at_end=None):
                if not (isinstance(j, int) and half * FT + j == 2 * FT - 1):
                    split_gu(j + 1, 1 - s)
                for tb in range(2):
                    add(half, j - 1, 4 * tb)
                    add(half, j - 1, 4 * tb + 1)
                    a_product(j, tb)
                    if tb == 0:
                        split_dn(j, s)
                    add(half, j - 1, 4 * tb + 2)
                    a_low(j, s, tb)
                    add(half, j - 1, 4 * tb + 3)
                    if tb == 0 and at_end is not None:
                        at_end()

            if half == 0:
                for t in range(XN):
                    scaled(0, t)
            for t in range(HT):
                h_low(t)
                if half:
                    add(half - 1, FT - 1, t)
                if t + XN < HT:
                    scaled(half, t + XN)
                if half == 0 and t == 1:
                    split_gu(0, 0)
                if t == 4:
                    split_gu(1, 1)
                if t == 5:
                    a_product(0, 0)
            split_dn(0, 0)
            a_low(0, 0, 0)
            a_product(0, 1)
            a_low(0, 0, 1)
            middle_tiles(dve, whole)

            def scale_next():
                for t in range(XN):
                    scaled(1, t)

            whole(FT - 1, 1, None if half else scale_next)
        for t in range(HT):
            add(1, FT - 1, t)


def build(nc, dram, out):
    x_mid = nc.dram_tensor("x_mid", [SEQ, D], F32, kind="Internal").ap()
    kept = Kept(nc)
    with ExitStack() as ctx:
        build_phase_a(nc, ctx, dram, x_mid, kept)
    with ExitStack() as ctx:
        build_phase_b(nc, ctx, dram, x_mid, out, kept)


def rope_table():
    half = ROPE // 2
    inv = np.float32(500000.0) ** (-np.arange(half, dtype=np.float32) * np.float32(2.0) / np.float32(ROPE))
    angle = np.arange(SEQ, dtype=np.float32)[:, None] * inv[None, :].astype(np.float32)
    c, s = np.cos(angle).astype(np.float32), np.sin(angle).astype(np.float32)
    table = np.concatenate([c, c, -s, s], axis=1).reshape(NB, TT, P, 4 * half).transpose(0, 2, 1, 3)
    return np.ascontiguousarray(np.concatenate([table, table[:1]]))


def laid_out(x, w_in, w_out, norm1_w, norm2_w, q_norm_w, k_norm_w, attn_sinks, hgrn_lb_logits, hgrn_gnorm_w,
             w_gate_up, w_down):
    f = lambda a: np.asarray(a)
    x, w_in, w_out, w_gate_up, w_down = f(x)[0], f(w_in)[0], f(w_out)[0], f(w_gate_up)[0], f(w_down)[0]
    by_k = lambda w: w.reshape(KT, P, -1).transpose(1, 0, 2)
    heads = w_out[:N_Q * HD].reshape(2, 4, HD, D)
    rows = np.concatenate([heads.transpose(1, 0, 2, 3).reshape(N_Q * HD, D), w_out[N_Q * HD:]])
    whole = [by_k(w_in[:, c:c + n]) for _, c, n in CHUNKS if n == WC] + [by_k(rows[:, c:c + WC]) for c in range(0, D, WC)]
    sinks = f(attn_sinks)[0].reshape(N_KV, 1, 2, 2, 1)
    sinks = np.broadcast_to(sinks, (N_KV, 2, 2, 2, HD)).transpose(3, 4, 0, 1, 2).reshape(P, N_KV, 4)
    s = np.arange(P)
    causal = (s[:, None] // CHUNK == s[None, :] // CHUNK) & (s[:, None] <= s[None, :])
    qk_weight = np.stack([f(q_norm_w)[0], f(k_norm_w)[0]])
    return {
        "x_pad": np.concatenate([x, x[:TB]]).reshape(NB + 1, TB, D),
        "w_half": np.stack([by_k(w_in[:, c:c + n]) for _, c, n in CHUNKS if n < WC]),
        "w_whole": np.stack(whole),
        "ident": np.eye(P, dtype=np.float32),
        "causal": causal[:, None, :].astype(np.uint32),
        "qk_weight": np.broadcast_to(qk_weight, (P, 2, HD)),
        "sink": sinks,
        "n1w": f(norm1_w)[0].reshape(KT, P).T,
        "n2w": np.broadcast_to(f(norm2_w)[0], (P, D)),
        "gnw": f(hgrn_gnorm_w)[0].reshape(P, 1),
        "lb": f(hgrn_lb_logits).reshape(2, HG, P).transpose(2, 0, 1),
        "rope": rope_table(),
        "w_gu": np.stack([np.concatenate([by_k(w_gate_up[:, j * P:(j + 1) * P]), by_k(w_gate_up[:, D_FF + j * P:D_FF + (j + 1) * P])], axis=2)
                          for j in range(FT)]),
        "w_dn": w_down.reshape(FT, P, D),
    }


def kernel(**inputs):
    import concourse.bacc as bacc
    from concourse.bass_utils import run_bass_kernel_spmd

    nc = bacc.Bacc("TRN2", target_bir_lowering=False, num_devices=1)
    arrays = {k: np.ascontiguousarray(a) for k, a in laid_out(**inputs).items()}
    dram = {k: nc.dram_tensor(k, a.shape, mybir.dt.from_np(a.dtype), kind="ExternalInput").ap() for k, a in arrays.items()}
    out = nc.dram_tensor("y", (SEQ, D), F32, kind="ExternalOutput").ap()
    build(nc, dram, out)
    r = run_bass_kernel_spmd(nc, [arrays], core_ids=[0])
    return r.results[0]["y"].reshape(1, SEQ, D)
```

```python
from contextlib import ExitStack

import numpy as np

import concourse.bass as bass
from concourse import mybir

F32 = mybir.dt.float32
F32R = mybir.dt.float32r
BF16 = mybir.dt.bfloat16
U32 = mybir.dt.uint32
ALU = mybir.AluOpType
ACT = mybir.ActivationFunctionType
AX = mybir.AxisListType

P = 128
SEQ, D = 2048, 1024
KT = D // P
CHUNK = 64
HD = 64
N_Q, N_KV = 8, 2
SLOTS = N_Q + N_KV
ROPE = HD // 4
HG = 4
D_FF = 2816
FT = D_FF // P
EPS = 1e-6
NEG = -1e30

TB = 512
NB = SEQ // TB
TT = TB // P
NC = TB // CHUNK
WC = 256
TH = 1024
HT = TH // P
XN = 3

CHUNKS = [("KV", 512, 256), ("QA0", 0, 256), ("QA1", 256, 256), ("F0", 1280, 128), ("F1", 1408, 128),
          ("Q01", 768, 256), ("I01", 1792, 256), ("G01", 2304, 256), ("F23", 1536, 256), ("Q23", 1024, 256),
          ("I23", 2048, 256), ("G23", 2560, 256)]
NW = len(CHUNKS) + D // WC
FIRST_HEAD = {"F0": 0, "F1": 1, "F23": 2, "Q01": 0, "Q23": 2}
HALF_CHUNKS = [n for n, c in enumerate(CHUNKS) if c[2] < WC]
WHOLE_CHUNKS = [n for n in range(NW) if n not in HALF_CHUNKS]


def chunk_name(n):
    return CHUNKS[n][0] if n < len(CHUNKS) else f"WO{n - len(CHUNKS)}"


def chunk_groups(n):
    name = chunk_name(n)
    return CHUNKS[n][2] // P if name in FIRST_HEAD else TT


GROUPS_TO = [sum(chunk_groups(m) for m in range(n)) for n in range(NW + 1)]
N_GROUPS = GROUPS_TO[NW]
CHUNK_AT = {chunk_name(n): n for n in range(NW)}


def block_steps():
    at = {}

    def after(name, group, *steps):
        at.setdefault((name, group), []).extend(steps)

    after("KV", 3, ("vmix",))
    after("QA1", 0, ("qn1", 0))
    after("QA1", 1, ("qn1", 1))
    after("QA1", 2, ("qn1", 2), ("qn2", 0))
    after("QA1", 3, ("qn1", 3))
    after("F0", 0, ("qn2", 1), ("split_hi", CHUNK_AT["Q01"]), ("split_lo", CHUNK_AT["Q01"]), ("qn2", 2))
    after("F1", 0, ("qn2", 3))
    after("Q01", 0, ("qT", 0), ("qT", 1), ("qT", 2), ("qT", 3), ("kT",))
    after("Q01", 1, ("sc", 0), ("sm1", 0), ("sm1", 1))
    after("I01", 0, ("ha", 0))
    after("I01", 1, ("sm2", 0), ("sm2", 1), ("sc", 1))
    after("I01", 2, ("pt", 0), ("pt", 1), ("sm1", 2), ("sm1", 3), ("hb", 0))
    after("I01", 3, ("sm2", 2), ("sm2", 3), ("pv", 0), ("sc", 2))
    after("G01", 0, ("pt", 2), ("pt", 3), ("sm1", 4), ("sm1", 5), ("xload",), ("hc", 0), ("ha", 1))
    after("G01", 1, ("sm2", 4), ("sm2", 5), ("pv", 1), ("sc", 3), ("split_hi", CHUNK_AT["F23"]), ("split_lo", CHUNK_AT["F23"]))
    after("G01", 2, ("pt", 4), ("pt", 5), ("att", 0), ("kt", 0), ("sm1", 6), ("sm1", 7), ("hb", 1))
    after("G01", 3, ("ds", 0, 0), ("ds", 0, 1), ("sm2", 6), ("sm2", 7), ("pv", 2), ("hc", 1))
    after("F23", 0, ("pt", 6), ("pt", 7))
    after("F23", 1, ("pv", 3), ("o", 0), ("on1", 0), ("kt", 1), ("ha", 2), ("sq", 0))
    after("Q23", 0, ("on2", 0), ("on3", 0), ("hb", 2), ("split_lo", CHUNK_AT["I23"]), ("ds", 1, 0), ("ds", 1, 1), ("att", 1))
    after("Q23", 1, ("yt", 0), ("hc", 2), ("sq", 1))
    after("I23", 0, ("o", 1), ("on1", 1), ("ha", 3))
    after("I23", 1, ("on2", 1), ("on3", 1), ("split_lo", CHUNK_AT["G23"]), ("kt", 2), ("sq", 2))
    after("I23", 2, ("yt", 1), ("att", 2), ("sq", 3))
    after("I23", 3, ("hb", 3),)
    after("G23", 0, ("ds", 2, 0), ("ds", 2, 1), ("hc", 3), ("n1a",))
    after("G23", 1, ("o", 2), ("on1", 2), ("kt", 3), ("n1b", 0), ("n1b", 1))
    after("G23", 2, ("on2", 2), ("ds", 3, 0), ("ds", 3, 1), ("att", 3))
    after("G23", 3, ("on3", 2), ("o", 3), ("on1", 3), ("yt", 2), ("n1b", 2), ("on2", 3), ("on3", 3), ("n1b", 3))
    for n in range(CHUNK_AT["WO0"], NW):
        after(chunk_name(n), 1, ("split_lo", n + 1))
    after("WO0", 0, ("xT", 0))
    after("WO0", 1, ("xT", 1))
    after("WO0", 2, ("xT", 2))
    after("WO1", 0, ("xT", 3))
    after("WO1", 2, ("xT", 4))
    after("WO2", 0, ("xT", 5))
    after("WO2", 2, ("xT", 6))
    after("WO3", 0, ("xT", 7))
    placed = [step for group in at.values() for step in group if step[0].startswith("split")]
    steps = []
    for n in range(NW):
        first_steps = [part for part in (("split_hi", n + 1), ("split_lo", n + 1)) if part not in placed]
        for g in range(chunk_groups(n)):
            if (chunk_name(n), g) == ("WO0", 0):
                first_steps.append(("yt", HG - 1))
            if g == 0 and (chunk_groups(n) < TT or chunk_name(n) == "WO0"):
                steps += first_steps
            steps.append(("proj", n, g))
            steps += at.pop((chunk_name(n), g), [])
            if g == 0 and not (chunk_groups(n) < TT or chunk_name(n) == "WO0"):
                steps += first_steps
    assert not at, at
    return steps


STEPS = block_steps()
LAST_YT_AT = 3
TR_KINDS = ("qT", "pt", "kt", "ds", "yt", "xT")
TR_USES = [s for s in STEPS if s[0] in TR_KINDS]
assert len(TR_USES) % 2 == 0


class Signal:

    def __init__(self, nc, ctx, name, per_pass, ahead=0):
        self.sem = ctx.enter_context(nc.semaphore(name))
        self.per_pass, self.ahead = per_pass, ahead

    def upto(self, n_pass, k):
        return n_pass * self.per_pass + (k + self.ahead)


class Places:

    def __init__(self, nc, at=0):
        self.nc, self.at = nc, at or (nc.sbuf_base + 63) // 64 * 64

    def put(self, name, shape, dt, at=None):
        size = int(np.prod(shape[1:])) * (2 if dt == BF16 else 4)
        offset = self.at if at is None else at
        if at is None:
            self.at += (size + 31) // 32 * 32
            assert self.at <= self.nc.sbuf_usable_end, (name, self.at)
        return self.nc.alloc_sbuf_tensor_at(name, list(shape), dt, offset=offset)


class Kept:

    def __init__(self, nc, ctx):
        mem = Places(nc)
        self.ident = mem.put("ident", [P, P], F32)
        self.mid_ms = mem.put("mid_ms", [P, NB * TT], F32)
        self.w_stage, self.xn = [], []
        for s in range(2):
            at = mem.at
            self.w_stage.append(mem.put(f"a_w_stage{s}", [P, KT, WC], F32))
            tiles = [2] if s == 0 else [0, 1]
            self.xn += [(t, mem.nc.alloc_sbuf_tensor_at(f"b_xn{t}", [P, D], F32, offset=at + i * D * 4)) for i, t in enumerate(tiles)]
            if s == 0:
                self.n2w = mem.nc.alloc_sbuf_tensor_at("b_n2w", [P, D], F32, offset=at + D * 4)
        self.xn = [tile for _, tile in sorted(self.xn, key=lambda pair: pair[0])]
        self.end = mem.at
        self.xn_loaded = [ctx.enter_context(nc.semaphore(f"xn_loaded{t}")) for t in range(XN)]
        self.n2w_in = ctx.enter_context(nc.semaphore("n2w_in"))


def three_passes(pe, out, stationary, moving, tiles=range(KT), before=None):
    for k in tiles:
        if before is not None:
            before(k)
        pe.matmul(out, stationary[0](k), moving[0](k), start=(k == 0), stop=False)
        pe.matmul(out, stationary[0](k), moving[1](k), start=False, stop=False)
        last = pe.matmul(out, stationary[1](k), moving[0](k), start=False, stop=(k == KT - 1))
    return last


def build_phase_a(nc, ctx, dram, x_mid, kept):
    def sem(name):
        return ctx.enter_context(nc.semaphore(name))

    def signal(name, per_pass, ahead=0):
        return Signal(nc, ctx, name, per_pass, ahead)

    ident, mid_ms = kept.ident, kept.mid_ms
    mem = Places(nc, kept.end)
    put = mem.put
    causal = put("a_causal", [P, 1, P], U32)
    qk_weight = put("a_qk_weight", [P, 2, ROPE], F32)
    qk_weight_T = put("a_qk_weight_T", [P, 2], F32)
    sink = put("a_sink", [P, N_KV, 4], F32)
    n1w = put("a_n1w", [P, KT], F32)
    gnw = put("a_gnw", [P, 1], F32)
    lb_in = put("a_lb_in", [P, 2, HG], F32)
    lb_e = put("a_lb_e", [P, 4, HG], F32)
    lb = put("a_lb", [P, HG], F32)
    one_less_lb = put("a_one_less_lb", [P, HG], F32)
    neg_half = put("a_neg_half", [P, SLOTS], F32)
    ones_row = put("a_ones_row", [1, P], F32)
    penalty = put("a_penalty", [1, P], F32)
    not_start = put("a_not_start", [P, TB], BF16)
    rope = put("a_rope", [P, TT, 4 * ROPE // 2], F32)
    w_stage = kept.w_stage
    w_hi = [put(f"a_w_hi{s}", [P, KT, WC], F32R) for s in range(2)]
    w_lo = [put(f"a_w_lo{s}", [P, KT, WC], F32R) for s in range(2)]
    hT_hi = put("a_hT_hi", [P, KT, TB], F32R)
    hT_lo = put("a_hT_lo", [P, KT, TB], F32R)
    yA_hi = put("a_yA_hi", [P, HG, TB], F32R)
    yA_lo = put("a_yA_lo", [P, HG, TB], F32R)
    arena = mem.at
    x_in = put("a_x_in", [P, TT, D], F32)
    qk = put("a_qk", [P, TT, SLOTS, HD], F32, at=arena)
    qk_sq = put("a_qk_sq", [P, SLOTS, HD], F32, at=arena + TT * SLOTS * HD * 4)
    rope_u = put("a_rope_u", [P, SLOTS, ROPE], F32, at=arena + (TT + 1) * SLOTS * HD * 4)
    rope_v = put("a_rope_v", [P, SLOTS, ROPE], F32, at=arena + (TT + 1) * SLOTS * HD * 4 + SLOTS * ROPE * 4)
    x_res = [put(f"a_x_res{s}", [P, TT, WC], F32) for s in range(2)]
    qT = put("a_qT", [P, NC, 4, CHUNK], F32)
    kT = put("a_kT", [P, TT, P], F32)
    kT_even = put("a_kT_even", [P, TT, P], F32)
    v_nat = put("a_v_nat", [P, TT, P], F32)
    v_even = put("a_v_even", [P, TT + 1, P], F32)
    i_nat = put("a_i_nat", [P, TT, HG * P], F32)
    g_nat = put("a_g_nat", [P, TT, HG * P], F32)
    f_at, f_gate, q_h, yH_hi, yH_lo = [], [], [], [], []
    for h in range(HG):
        f_at.append(mem.at)
        f_gate.append(put(f"a_f_gate{h}", [P, TB], F32))
        yH_hi.append(put(f"a_yH_hi{h}", [P, TB], F32R, at=f_at[h]))
        q_at = mem.at
        q_h.append(put(f"a_q_h{h}", [P, TB], F32))
        yH_lo.append(put(f"a_yH_lo{h}", [P, TB], F32R, at=q_at))
    q_in = [put(f"a_q_in{s}", [P, TB], F32) for s in range(2)]
    k_end = [put(f"a_k_end{s}", [P, TB], F32) for s in range(2)]
    t_a = put("a_t_a", [P, TB], F32)
    t_b = put("a_t_b", [P, TB], F32)
    decay = put("a_decay", [P, HG, NC], F32)
    prob_at = mem.at
    prob = [put(f"a_prob{s}", [P, 4, P], F32) for s in range(2)]
    probT = [put(f"a_probT{s}", [P, 4, P], F32) for s in range(2)]
    att_m = put("a_att_m", [P, TT, P], F32)
    k_nat = put("a_k_nat", [P, TT, P], F32)
    state = put("a_state", [P, NC, P], F32)
    carry = put("a_carry", [P, HG, P], F32)
    y_nat = put("a_y_nat", [P, TT, P], F32)
    junk = put("a_junk", [P, D], BF16, at=prob_at)
    o_sq = put("a_o_sq", [P, TT, P], BF16)
    ss = put("a_ss", [P, TT], F32)
    x_rs = put("a_x_rs", [P, TT], F32)
    q_ss = put("a_q_ss", [P, TT, SLOTS], F32)
    q_rs = put("a_q_rs", [P, TT, SLOTS], F32)
    o_ss = put("a_o_ss", [P, TT], F32)
    o_rs = put("a_o_rs", [P, TT], F32)
    top = put("a_top", [P, 2, 4], F32)
    neg_top = put("a_neg_top", [P, 2, 4], F32)
    sink_less = put("a_sink_less", [P, 2, 4], F32)
    sink_e = put("a_sink_e", [P, 2, 4], F32)
    denom = put("a_denom", [P, 2, 4], F32)
    mid_ss = put("a_mid_ss", [P, TT, 4], F32)
    mid_sum = put("a_mid_sum", [P, TT], F32)
    mid_old = put("a_mid_old", [P, (NB - 1) * TT], F32)

    def bank(name):
        return ctx.enter_context(nc.psum_tensor(name, [P, 512], F32))

    pj = [bank(f"a_pj{s}") for s in range(2)]
    tr = [bank(f"a_tr{s}") for s in range(2)]
    sc = [bank(f"a_sc{s}") for s in range(2)]
    pvb = bank("a_pv")
    hb = bank("a_hb")
    first_banks = tr + sc + [pvb, hb]

    consts_in = sem("consts_in")
    w_loaded = [sem(f"w_loaded{s}") for s in range(2)]
    x_loaded, rope_loaded = sem("x_loaded"), sem("rope_loaded")
    xr_loaded = [sem(f"xr_loaded{s}") for s in range(2)]
    xr_stored = [sem(f"xr_stored{s}") for s in range(2)]
    w_hi_ready = signal("w_hi_ready", NW, 1)
    w_lo_ready = signal("w_lo_ready", NW, 1)
    pj_full = signal("pj_full", N_GROUPS, 1)
    tr_full = signal("tr_full", len(TR_USES), KT)
    first_x_loaded = [sem(f"first_x_loaded{t}") for t in range(TT)]
    first_ss_ready, first_ms_ready, first_rs_ready = sem("first_ss_ready"), sem("first_ms_ready"), sem("first_rs_ready")
    ss_ready = signal("ss_ready", 1)
    ms_ready = signal("ms_ready", 1)
    x_rs_ready = signal("x_rs_ready", 1)
    xn_ready = signal("xn_ready", 1, 1)
    h_hi_ready = signal("h_hi_ready", KT, KT)
    hT_ready = signal("hT_ready", KT, KT)
    f_ready = signal("f_ready", HG)
    q_ready = signal("q_ready", HG)
    g_ready = signal("g_ready", 2 * TT)
    kv_ready = signal("kv_ready", TT)
    qa_ready = signal("qa_ready", 2 * TT)
    i_ready = signal("i_ready", 2 * TT)
    v_even_ready = signal("v_even_ready", 1)
    q_sq_ready = signal("q_sq_ready", TT)
    q_ms_ready = signal("q_ms_ready", TT)
    q_rs_ready = signal("q_rs_ready", TT)
    qk_ready = signal("qk_ready", TT)
    kT_full = signal("kT_full", 1)
    qT_ready = signal("qT_ready", 4)
    kT_ready = signal("kT_ready", 1)
    sc_full = signal("sc_full", 8)
    sink_less_ready = signal("sink_less_ready", 8)
    exp_ready = signal("exp_ready", 8)
    prob_ready = signal("prob_ready", 8)
    probT_ready = signal("probT_ready", 8)
    pv_full = signal("pv_full", TT)
    yA_hi_ready = signal("yA_hi_ready", TT)
    yA_ready = signal("yA_ready", TT, 1)
    fg_ready = signal("fg_ready", HG)
    lf_ready = signal("lf_ready", HG)
    b_ready = signal("b_ready", HG)
    e_ready = signal("e_ready", HG)
    gates_ready = signal("gates_ready", HG, 1)
    att_full = signal("att_full", HG)
    att_ready = signal("att_ready", HG)
    k_nat_ready = signal("k_nat_ready", HG)
    state_ready = signal("state_ready", HG)
    o_full = signal("o_full", HG)
    o_sq_ready = signal("o_sq_ready", HG)
    o_ms_ready = signal("o_ms_ready", HG)
    o_rs_ready = signal("o_rs_ready", HG)
    hb_read = signal("hb_read", HG, 1)
    y_nat_ready = signal("y_nat_ready", HG)
    yH_hi_ready = signal("yH_hi_ready", HG)
    yH_ready = signal("yH_ready", HG)
    res_done = signal("res_done", 4 * TT, 1)
    mid_squared = signal("mid_squared", 4 * TT)
    mid_ready = signal("mid_ready", 1, 1)
    pool_waited, dve_waited = sem("pool_waited"), sem("dve_waited")
    pool_set, dve_set, act_set = sem("pool_set"), sem("dve_set"), sem("act_set")

    tr_read = {"qT": (qT_ready, lambda s: s[1] + 1), "pt": (probT_ready, lambda s: s[1] + 1),
               "kt": (k_nat_ready, lambda s: s[1] + 1), "ds": (state_ready, lambda s: s[1] + 1),
               "yt": (yH_ready, lambda s: s[1] + 1), "xT": (hT_ready, lambda s: s[1] + 1)}
    pj_read = []
    counts = {}
    for n in range(NW):
        kind = chunk_name(n)[:2] if chunk_name(n)[:2] in ("KV", "QA", "WO") else chunk_name(n)[0]
        for g in range(chunk_groups(n)):
            counts[kind] = counts.get(kind, 0) + 1
            s = {"F": f_ready, "Q": q_ready, "G": g_ready, "KV": kv_ready, "QA": qa_ready, "I": i_ready,
                 "WO": res_done}[kind]
            pj_read.append((s, counts[kind]))

    blk = ctx.enter_context(nc.Block())

    @blk.sync
    def _(sp):
        def load(n):
            m = n % NW
            if m in HALF_CHUNKS:
                sp.dma_start(w_stage[n % 2][:, :, 0:P], dram["w_half"][HALF_CHUNKS.index(m)]).then_inc(w_loaded[n % 2], 16)
            else:
                sp.dma_start(w_stage[n % 2][:, :, :], dram["w_whole"][WHOLE_CHUNKS.index(m)]).then_inc(w_loaded[n % 2], 16)

        first = dram["x_pad"][0].rearrange("(t p) d -> p t d", p=P)
        for t in range(TT):
            sp.dma_start(x_in[:, t, :], first[:, t, :]).then_inc(first_x_loaded[t], 16)
        load(0)
        for name, tile in (("ident", ident), ("causal", causal), ("qk_weight", qk_weight), ("qk_weight_T", qk_weight_T), ("sink", sink),
                           ("n1w", n1w), ("gnw", gnw), ("lb", lb_in)):
            sp.dma_start(tile[:], dram[name]).then_inc(consts_in, 16)
        with sp.Fori(0, NB) as b:
            for n in range(1, NW + 1):
                sp.wait_ge(w_lo_ready.sem, w_lo_ready.upto(b, max(n - 2, 0)))
                load(n)
        mid_tiles = x_mid.rearrange("(t p) d -> t p d", p=P)
        sp.wait_ge(w_lo_ready.sem, w_lo_ready.upto(NB - 1, NW - 1))
        for t in range(2):
            sp.dma_start(kept.xn[t][:], mid_tiles[t]).then_inc(kept.xn_loaded[t], 16)
        sp.wait_ge(w_lo_ready.sem, w_lo_ready.upto(NB - 1, NW))
        sp.dma_start(kept.n2w[:], dram["n2w"]).then_inc(kept.n2w_in, 16)
        sp.dma_start(kept.xn[2][:], mid_tiles[2]).then_inc(kept.xn_loaded[2], 16)

    @blk.gpsimd
    def _(pool):
        def wait(sem, value):
            pool.wait_ge(sem, value)
            pool.sem_inc(pool_waited, 1)

        def load_rope(b):
            pool.dma_start(rope[:], dram["rope"][bass.ds(b, 1)].rearrange("o p t c -> p (o t) c")).then_inc(rope_loaded, 16)

        def load_block(b):
            pool.dma_start(x_in[:], dram["x_pad"][bass.ds(b, 1)].rearrange("o (t p) d -> p (o t) d", p=P)).then_inc(x_loaded, 16)
            load_rope(b)

        load_rope(0)
        pool.memset(neg_half[:], -0.5)
        pool.memset(ones_row[:], 1.0)
        pool.memset(penalty[:, 0:CHUNK], 0.0)
        pool.memset(penalty[:, CHUNK:P], NEG)
        pool.memset(kT[:], 0.0)
        pool.memset(v_even[:], 0.0)
        pool.memset(carry[:], 0.0)
        pool.memset(att_m[:], 0.0)
        pool.memset(mid_ms[:], 0.0)
        pool.memset(not_start[:], 1.0)
        pool.drain()
        pool.memset(not_start[:].rearrange("p (c s) -> p c s", s=CHUNK)[:, :, 0:1], 0.0).then_inc(pool_set, 1)

        def power(out, in_, width, ready, done, value, shape=None):
            pool.drain()
            pool.wait_ge(ready.sem, value)
            pool.tensor_tensor(out, in_, neg_half[:, 0:width], ALU.pow).then_inc(done.sem, 1)

        pool.drain()
        for t in range(TT):
            pool.wait_ge(first_ms_ready, t + 1)
            pool.tensor_tensor(x_rs[:, t:t + 1], ss[:, t:t + 1], neg_half[:, 0:1], ALU.pow).then_inc(first_rs_ready, 1)
        x_cols = dram["x_pad"].rearrange("b (t p) (c n) -> b p t c n", p=P, n=WC)
        mid_cols = x_mid.rearrange("(b t p) (c n) -> b p t c n", b=NB, p=P, n=WC)
        with pool.Fori(0, NB) as b:
            def load_res(c, b=b):
                pool.dma_start(x_res[c % 2][:], x_cols[bass.ds(b, 1), :, :, c, :].rearrange("o p t n -> p (o t) n")).then_inc(xr_loaded[c % 2], 16)

            def store_res(c, b=b):
                wait(mid_squared.sem, mid_squared.upto(b, TT * (c + 1)))
                pool.dma_start(mid_cols[bass.ds(b, 1), :, :, c, :].rearrange("o p t n -> p (o t) n"), x_res[c % 2][:]).then_inc(xr_stored[c % 2], 16)

            for step in STEPS:
                kind = step[0]
                if kind == "vmix":
                    wait(kv_ready.sem, kv_ready.upto(b, TT))
                    pool.drain()
                    pool.tensor_copy(v_even[CHUNK:P, 0, :], v_even[CHUNK:P, TT, :])
                    pool.drain()
                    pool.tensor_copy(v_even[0:CHUNK, 0:TT, :], v_nat[0:CHUNK, :, :])
                    pool.drain()
                    pool.tensor_copy(v_even[CHUNK:P, 1:TT + 1, :], v_nat[CHUNK:P, :, :]).then_inc(v_even_ready.sem, 1)
                elif kind == "qn1":
                    t = step[1]
                    power(q_rs[:, t, :], q_ss[:, t, :], SLOTS, q_ms_ready, q_rs_ready, q_ms_ready.upto(b, t + 1))
                elif kind == "sc" and step[1] == 1:
                    wait(sc_full.sem, sc_full.upto(b, 2))
                    pool.drain()
                    pool.memset(penalty[:, CHUNK:P], 0.0)
                elif kind == "xload":
                    wait(kT_full.sem, kT_full.upto(b, 1))
                    load_block(b + 1)
                    load_res(0)
                    load_res(1)
                elif kind == "on1":
                    h = step[1]
                    power(o_rs[:], o_ss[:], TT, o_ms_ready, o_rs_ready, o_ms_ready.upto(b, h + 1))
                elif kind == "n1a":
                    power(x_rs[:], ss[:], TT, ms_ready, x_rs_ready, ms_ready.upto(b, 1))
                elif kind == "proj" and chunk_name(step[1]).startswith("WO") and step[2] == TT - 1:
                    c = step[1] - len(CHUNKS)
                    store_res(c)
                    wait(xr_stored[c % 2], b * 32 + 16 * (c // 2 + 1))
                    if c < 2:
                        load_res(c + 2)

    @blk.scalar
    def _(act):
        def split(b, n):
            s = n % 2
            loaded = b * (16 * NW // 2) + 16 * ((n + 1) // 2 + (1 - s))
            act.wait_ge(w_loaded[s], loaded)
            if n >= 1:
                act.wait_ge(pj_full.sem, pj_full.upto(b, GROUPS_TO[max(n - 1, 0)]))
            cols = P if n % NW in HALF_CHUNKS else WC
            act.activation(w_hi[s][:, :, 0:cols], w_stage[s][:, :, 0:cols], ACT.Copy).then_inc(w_hi_ready.sem, 1)

        def square_x(b, t):
            act.drain()
            if t == 0:
                act.wait_ge(x_loaded, b * 16 + 16)
            last = act.activation(junk[:], x_in[:, t, :], ACT.Square, accum_out=ss[:, t:t + 1])
            if t == TT - 1:
                last.then_inc(ss_ready.sem, 1)

        def evacuate_x(b, k, use, bank):
            act.wait_ge(tr_full.sem, tr_full.upto(b, use + 1))
            act.activation(hT_hi[:, k, :], bank[:], ACT.Copy, scale=n1w[:, k:k + 1]).then_inc(h_hi_ready.sem, 1)

        for t in range(TT):
            act.wait_ge(first_x_loaded[t], 16)
            act.activation(junk[:], x_in[:, t, :], ACT.Square, accum_out=ss[:, t:t + 1]).then_inc(first_ss_ready, 1)
            act.drain()
        split(0, 0)
        act.wait_ge(consts_in, 8 * 16)
        for k in range(KT):
            evacuate_x(-1, k, len(TR_USES) - KT + k, first_banks[k % len(first_banks)])
        act.wait_ge(dve_set, 1)
        act.activation(lb_e[:, 0:2, :], lb_e[:, 2:4, :], ACT.Exp).then_inc(act_set, 1)

        with act.Fori(0, NB) as b:
            use = 0
            table = [None]

            def use_exp_table():
                if table[0] != "exp":
                    act.preload_act_table_set("natural_log_exp_and_others")
                table[0] = "exp"

            for step in STEPS:
                kind = step[0]
                if kind == "proj" and chunk_name(step[1])[0] in "FQG" and chunk_name(step[1])[:2] != "QA":
                    table[0] = "other"
                if kind == "split_hi":
                    split(b, step[1])
                elif kind == "proj":
                    n, g = step[1:]
                    name, ps = chunk_name(n), pj[(GROUPS_TO[n] + g) % 2]
                    if name.startswith("WO"):
                        c = n - len(CHUNKS)
                        if g == 0:
                            act.drain()
                        act.wait_ge(res_done.sem, res_done.upto(b, TT * c + g + 1))
                        act.activation(junk[:, g * WC:(g + 1) * WC], x_res[c % 2][:, g, :], ACT.Square,
                                       accum_out=mid_ss[:, g, c:c + 1]).then_inc(mid_squared.sem, 1)
                        continue
                    act.wait_ge(pj_full.sem, pj_full.upto(b, GROUPS_TO[n] + g + 1))
                    if name[0] == "F":
                        act.activation(f_gate[FIRST_HEAD[name] + g][:], ps[:], ACT.Sigmoid).then_inc(f_ready.sem, 1)
                    elif name in FIRST_HEAD:
                        act.activation(q_h[FIRST_HEAD[name] + g][:], ps[:], ACT.Silu).then_inc(q_ready.sem, 1)
                    elif name[0] == "G":
                        c0 = WC * (name == "G23")
                        act.activation(g_nat[:, g, c0:c0 + WC], ps[:, 0:WC], ACT.Silu).then_inc(g_ready.sem, 1)
                    elif name == "KV":
                        act.activation(qk[:, g, N_Q:SLOTS, :], ps[:, 0:P].rearrange("p (s d) -> p s d", d=HD), ACT.Copy)
                        act.activation(v_nat[:, g, :], ps[:, P:2 * P], ACT.Copy).then_inc(kv_ready.sem, 1)
                    elif name[:2] == "QA":
                        half = int(name[2])
                        act.activation(qk[:, g, half:N_Q:2, :], ps[:, 0:WC].rearrange("p (s d) -> p s d", d=HD), ACT.Copy).then_inc(qa_ready.sem, 1)
                    else:
                        c0 = WC * (name == "I23")
                        act.activation(i_nat[:, g, c0:c0 + WC], ps[:, 0:WC], ACT.Copy).then_inc(i_ready.sem, 1)
                elif kind == "qn1":
                    t = step[1]
                    act.drain()
                    if t > 0:
                        act.wait_ge(q_ms_ready.sem, q_ms_ready.upto(b, t))
                    act.activation(qk_sq[:], qk[:, t, :, :], ACT.Square).then_inc(q_sq_ready.sem, 1)
                elif kind == "ha":
                    h = step[1]
                    use_exp_table()
                    act.wait_ge(fg_ready.sem, fg_ready.upto(b, h + 1))
                    act.wait_ge(gates_ready.sem, gates_ready.upto(b, h))
                    act.activation(t_a[:], f_gate[h][:], ACT.Ln).then_inc(lf_ready.sem, 1)
                elif kind == "hb":
                    h, s = step[1], step[1] % 2
                    use_exp_table()
                    act.wait_ge(b_ready.sem, b_ready.upto(b, h + 1))
                    act.activation(q_in[s][:], t_a[:], ACT.Exp)
                    act.activation(k_end[s][:], k_end[s][:], ACT.Exp)
                    act.activation(decay[:, h, :], t_b[:].rearrange("p (c s) -> p c s", s=CHUNK)[:, :, CHUNK - 1], ACT.Exp)
                    act.drain()
                    act.activation(t_a[:], t_a[:], ACT.Exp, scale=-1.0)
                    act.activation(t_b[:], t_b[:], ACT.Exp).then_inc(e_ready.sem, 1)
                elif kind == "qT":
                    j = step[1]
                    act.wait_ge(tr_full.sem, tr_full.upto(b, use + 1))
                    act.activation(qT[:, :, j, :], tr[use % 2][:].rearrange("p (c q) -> p c q", q=CHUNK), ACT.Copy,
                                   scale=qk_weight_T[:, 0:1]).then_inc(qT_ready.sem, 1)
                elif kind == "kT":
                    act.wait_ge(kT_full.sem, kT_full.upto(b, 1))
                    ps = sc[0][:].rearrange("p (t c) -> p t c", c=P)
                    act.activation(kT_even[:, 0, CHUNK:P], kT[:, TT - 1, CHUNK:P], ACT.Copy)
                    act.drain()
                    k_scale = qk_weight_T[:, 1:2]
                    act.activation(kT[:], ps, ACT.Copy, scale=k_scale)
                    act.activation(kT_even[:, :, 0:CHUNK], ps[:, :, 0:CHUNK], ACT.Copy, scale=k_scale)
                    act.activation(kT_even[:, 1:TT, CHUNK:P], ps[:, 0:TT - 1, CHUNK:P], ACT.Copy, scale=k_scale).then_inc(kT_ready.sem, 1)
                elif kind == "sm1":
                    u, s, kv = step[1], step[1] % 2, step[1] % 2
                    use_exp_table()
                    act.wait_ge(sink_less_ready.sem, sink_less_ready.upto(b, u + 1))
                    act.activation(sink_e[:, s, :], sink_less[:, s, :], ACT.Exp)
                    for i in range(4):
                        last = act.activation(prob[s][:, i, :], sc[kv][:, i * P:(i + 1) * P], ACT.Exp,
                                              bias=neg_top[:, s, i:i + 1], scale=HD ** -0.5, accum_out=denom[:, s, i:i + 1])
                    last.then_inc(exp_ready.sem, 1)
                elif kind == "pt":
                    u = step[1]
                    act.wait_ge(tr_full.sem, tr_full.upto(b, use + 1))
                    act.activation(probT[u % 2][:].rearrange("p i c -> p (i c)"), tr[use % 2][:], ACT.Copy).then_inc(probT_ready.sem, 1)
                elif kind == "pv":
                    t = step[1]
                    act.wait_ge(pv_full.sem, pv_full.upto(b, t + 1))
                    act.activation(yA_hi[:, :, t * P:(t + 1) * P].rearrange("p j (c q) -> p j c q", c=2),
                                   pvb[:].rearrange("p (c j q) -> p j c q", c=2, j=4), ACT.Copy).then_inc(yA_hi_ready.sem, 1)
                elif kind == "kt":
                    h = step[1]
                    act.wait_ge(tr_full.sem, tr_full.upto(b, use + 1))
                    act.activation(k_nat[:].rearrange("p t c -> p (t c)"), tr[use % 2][:], ACT.Copy).then_inc(k_nat_ready.sem, 1)
                elif kind == "on1":
                    h = step[1]
                    act.wait_ge(o_full.sem, o_full.upto(b, h + 1))
                    for t in range(TT):
                        last = act.activation(o_sq[:, t, :], hb[:, t * P:(t + 1) * P], ACT.Square, accum_out=o_ss[:, t:t + 1])
                    last.then_inc(o_sq_ready.sem, 1)
                elif kind == "yt":
                    h = step[1]
                    act.wait_ge(tr_full.sem, tr_full.upto(b, use + 1))
                    act.activation(yH_hi[h][:], tr[use % 2][:], ACT.Copy, scale=gnw[:, 0:1]).then_inc(yH_hi_ready.sem, 1)
                elif kind == "sq":
                    square_x(b, step[1])
                elif kind == "xT":
                    evacuate_x(b, step[1], use, tr[use % 2])
                if kind in TR_KINDS:
                    use += 1

    @blk.tensor
    def _(pe):
        def transpose_x(b, k, use, bank):
            if k == 0:
                pe.wait_ge(xn_ready.sem, xn_ready.upto(b, 1))
            for t in range(TT):
                last = pe.transpose(bank[:, t * P:(t + 1) * P], x_in[:, t, k * P:(k + 1) * P], ident[:])
            last.then_inc(tr_full.sem, 1)

        def bank_read(b, use):
            if use >= 2:
                read, index = tr_read[TR_USES[use - 2][0]]
                pe.wait_ge(read.sem, read.upto(b, index(TR_USES[use - 2])))

        def transpose_y(b, h, use):
            pe.wait_ge(y_nat_ready.sem, y_nat_ready.upto(b, h + 1))
            bank_read(b, use)
            for t in range(TT):
                last = pe.transpose(tr[use % 2][:, t * P:(t + 1) * P], y_nat[:, t, :], ident[:])
            last.then_inc(tr_full.sem, 1)

        pe.sem_inc(pj_full.sem, 1)
        pe.wait_ge(consts_in, 8 * 16)
        pe.wait_ge(pool_set, 1)
        for k in range(KT):
            if k >= len(first_banks):
                pe.wait_ge(hT_ready.sem, hT_ready.upto(-1, k - len(first_banks) + 1))
            transpose_x(-1, k, len(TR_USES) - KT + k, first_banks[k % len(first_banks)])

        with pe.Fori(0, NB) as b:
            use = 0
            for step in STEPS:
                kind = step[0]
                if kind == "proj":
                    n, g = step[1:]
                    name, at, s = chunk_name(n), GROUPS_TO[n] + g, n % 2
                    if g == 0:
                        pe.wait_ge(w_lo_ready.sem, w_lo_ready.upto(b, n))
                    if (name, g) != ("WO0", 1):
                        read, index = pj_read[at - 2]
                        pe.wait_ge(read.sem, read.upto(b, index) if at >= 2 else res_done.upto(b, 0))
                    if name in FIRST_HEAD:
                        cols = slice(g * P, (g + 1) * P)
                        last = three_passes(pe, pj[at % 2][:],
                                            (lambda k: w_hi[s][:, k, cols], lambda k: w_lo[s][:, k, cols]),
                                            (lambda k: hT_hi[:, k, :], lambda k: hT_lo[:, k, :]))
                    else:
                        rows = slice(g * P, (g + 1) * P)
                        if name[:2] == "WO":
                            if n == len(CHUNKS) and g == 0:
                                pe.wait_ge(yA_ready.sem, yA_ready.upto(b, TT))
                                pe.wait_ge(yH_ready.sem, yH_ready.upto(b, HG - 2))
                            still = (lambda k: yA_hi[:, k, rows] if k < HG else yH_hi[k - HG][:, rows],
                                     lambda k: yA_lo[:, k, rows] if k < HG else yH_lo[k - HG][:, rows])
                        else:
                            still = (lambda k: hT_hi[:, k, rows], lambda k: hT_lo[:, k, rows])
                        moving = (lambda k: w_hi[s][:, k, :], lambda k: w_lo[s][:, k, :])
                        if (name, g) == ("WO0", 0):
                            three_passes(pe, pj[at % 2][:, 0:WC], still, moving, range(KT - 2))
                            pe.wait_ge(yH_ready.sem, yH_ready.upto(b, HG - 1))
                            three_passes(pe, pj[at % 2][:, 0:WC], still, moving, range(KT - 2, KT - 1))
                            read, index = pj_read[at - 1]
                            pe.wait_ge(read.sem, read.upto(b, index))
                            other_rows = slice(P, 2 * P)
                            other = (lambda k: yA_hi[:, k, other_rows] if k < HG else yH_hi[k - HG][:, other_rows],
                                     lambda k: yA_lo[:, k, other_rows] if k < HG else yH_lo[k - HG][:, other_rows])
                            three_passes(pe, pj[(at + 1) % 2][:, 0:WC], other, moving, range(LAST_YT_AT))
                            transpose_y(b, HG - 1, TR_USES.index(("yt", HG - 1)))
                            three_passes(pe, pj[(at + 1) % 2][:, 0:WC], other, moving, range(LAST_YT_AT, KT - 1))
                            pe.wait_ge(yH_ready.sem, yH_ready.upto(b, HG))
                        left = range(KT - 1, KT) if (name, g) in (("WO0", 0), ("WO0", 1)) else range(KT)
                        arrived = (lambda k: pe.wait_ge(hT_ready.sem, hT_ready.upto(b - 1, k + 1))) if at == 0 else None
                        last = three_passes(pe, pj[at % 2][:, 0:WC], still, moving, left, arrived)
                    last.then_inc(pj_full.sem, 1)
                elif kind == "qT":
                    j = step[1]
                    if j == 0:
                        pe.wait_ge(qk_ready.sem, qk_ready.upto(b, TT))
                    bank_read(b, use)
                    for t in range(TT):
                        last = pe.transpose(tr[use % 2][:, t * P:(t + 1) * P], qk[:, t, 2 * j:2 * j + 2, :].rearrange("p s d -> p (s d)"), ident[:])
                    last.then_inc(tr_full.sem, 1)
                elif kind == "kT":
                    for t in range(TT):
                        last = pe.transpose(sc[0][:, t * P:(t + 1) * P], qk[:, t, N_Q:SLOTS, :].rearrange("p s d -> p (s d)"), ident[:])
                    last.then_inc(kT_full.sem, 1)
                elif kind == "sc":
                    t = step[1]
                    if t == 0:
                        pe.wait_ge(kT_ready.sem, kT_ready.upto(b, 1))
                        pe.wait_ge(v_even_ready.sem, v_even_ready.upto(b, 1))
                    for kv in range(N_KV):
                        rows = slice(kv * HD, (kv + 1) * HD)
                        if t > 0:
                            pe.wait_ge(exp_ready.sem, exp_ready.upto(b, 2 * (t - 1) + kv + 1))
                        for cc in range(2):
                            keys = kT if cc else kT_even
                            for jj in range(2):
                                i = 2 * cc + jj
                                first = t == 0 and cc == 0
                                last = pe.matmul(sc[kv][:, i * P:(i + 1) * P], qT[rows, 2 * t + cc, 2 * jj:2 * jj + 2, :].rearrange("p j q -> p (j q)"),
                                                 keys[rows, t, :], start=True, stop=not first)
                                if first:
                                    last = pe.matmul(sc[kv][:, i * P:(i + 1) * P], ones_row[:], penalty[:], start=False, stop=True)
                        last.then_inc(sc_full.sem, 1)
                elif kind == "pt":
                    u = step[1]
                    pe.wait_ge(prob_ready.sem, prob_ready.upto(b, u + 1))
                    bank_read(b, use)
                    for i in range(4):
                        last = pe.transpose(tr[use % 2][:, i * P:(i + 1) * P], prob[u % 2][:, i, :], ident[:])
                    last.then_inc(tr_full.sem, 1)
                elif kind == "pv":
                    t = step[1]
                    pe.wait_ge(probT_ready.sem, probT_ready.upto(b, 2 * t + 2))
                    pe.wait_ge(yA_ready.sem, yA_ready.upto(b, t))
                    for cc in range(2):
                        v = v_nat if cc else v_even
                        for kv in range(N_KV):
                            last = pe.matmul(pvb[kv * HD:(kv + 1) * HD, cc * 256:(cc + 1) * 256], v[:, t, kv * HD:(kv + 1) * HD],
                                             probT[kv][:, 2 * cc:2 * cc + 2, :].rearrange("p i c -> p (i c)"), start=True, stop=True)
                    last.then_inc(pv_full.sem, 1)
                elif kind == "att":
                    h = step[1]
                    pe.wait_ge(gates_ready.sem, gates_ready.upto(b, h + 1))
                    pe.wait_ge(hb_read.sem, hb_read.upto(b, h))
                    for t in range(TT):
                        last = pe.matmul(hb[:, t * P:(t + 1) * P], f_gate[h][:, t * P:(t + 1) * P],
                                         q_in[h % 2][:, t * P:(t + 1) * P], start=True, stop=True)
                    last.then_inc(att_full.sem, 1)
                elif kind == "kt":
                    h = step[1]
                    pe.wait_ge(gates_ready.sem, gates_ready.upto(b, h + 1))
                    bank_read(b, use)
                    for t in range(TT):
                        last = pe.transpose(tr[use % 2][:, t * P:(t + 1) * P], k_end[h % 2][:, t * P:(t + 1) * P], ident[:])
                    last.then_inc(tr_full.sem, 1)
                elif kind == "ds":
                    h, par = step[1:]
                    if par == 0:
                        pe.wait_ge(k_nat_ready.sem, k_nat_ready.upto(b, h + 1))
                        pe.wait_ge(i_ready.sem, i_ready.upto(b, TT if h < 2 else 2 * TT))
                    bank_read(b, use)
                    rows = slice(par * CHUNK, (par + 1) * CHUNK)
                    for t in range(TT):
                        last = pe.matmul(tr[use % 2][:, t * P:(t + 1) * P], k_nat[rows, t, :], i_nat[rows, t, h * P:(h + 1) * P], start=True, stop=True)
                    last.then_inc(tr_full.sem, 1)
                elif kind == "o":
                    h = step[1]
                    pe.wait_ge(att_ready.sem, att_ready.upto(b, h + 1))
                    pe.wait_ge(state_ready.sem, state_ready.upto(b, h + 1))
                    for t in range(TT):
                        cols = slice(t * P, (t + 1) * P)
                        pe.matmul(hb[:, cols], att_m[:, t, :], i_nat[:, t, h * P:(h + 1) * P], start=True, stop=True)
                        for cc in range(2):
                            at = t * P + cc * CHUNK
                            last = pe.matmul(hb[cc * CHUNK:(cc + 1) * CHUNK, cols], q_h[h][:, at:at + CHUNK], state[:, 2 * t + cc, :],
                                             start=False, stop=True, skip_group_check=True)
                    last.then_inc(o_full.sem, 1)
                elif kind == "yt" and step[1] < HG - 1:
                    transpose_y(b, step[1], use)
                elif kind == "xT":
                    bank_read(b, use)
                    transpose_x(b, step[1], use, tr[use % 2])
                if kind in TR_KINDS:
                    use += 1

    @blk.vector
    def _(dve):
        def split(b, n):
            s = n % 2
            cols = P if n % NW in HALF_CHUNKS else WC
            dve.wait_ge(w_hi_ready.sem, w_hi_ready.upto(b, n))
            dve.tensor_tensor(w_lo[s][:, :, 0:cols], w_stage[s][:, :, 0:cols], w_hi[s][:, :, 0:cols].bitcast(F32), ALU.subtract).then_inc(w_lo_ready.sem, 1)

        def mean_square_x(b):
            dve.wait_ge(ss_ready.sem, ss_ready.upto(b, 1))
            dve.tensor_scalar(ss[:], ss[:], 1.0 / D, EPS, ALU.mult, ALU.add).then_inc(ms_ready.sem, 1)

        def scale_x(b, t):
            if t == 0:
                dve.wait_ge(x_rs_ready.sem, x_rs_ready.upto(b, 1))
            last = dve.tensor_scalar(x_in[:, t, :], x_in[:, t, :], x_rs[:, t:t + 1], None, ALU.mult)
            if t == TT - 1:
                last.then_inc(xn_ready.sem, 1)

        def low_part(out, ps, weight, hi, ready):
            dve.scalar_tensor_tensor(out=out, in0=ps, scalar=weight, in1=hi.bitcast(F32), op0=ALU.mult, op1=ALU.subtract).then_inc(ready.sem, 1)

        def evacuate_x(b, k, bank):
            dve.wait_ge(h_hi_ready.sem, h_hi_ready.upto(b, k + 1))
            low_part(hT_lo[:, k, :], bank[:], n1w[:, k:k + 1], hT_hi[:, k, :], hT_ready)

        for s in (yA_ready, gates_ready, hb_read, res_done):
            dve.sem_inc(s.sem, 1)
        for t in range(TT + 1):
            if t < TT:
                dve.wait_ge(first_ss_ready, t + 1)
                dve.tensor_scalar(ss[:, t:t + 1], ss[:, t:t + 1], 1.0 / D, EPS, ALU.mult, ALU.add).then_inc(first_ms_ready, 1)
            if t > 0:
                dve.wait_ge(first_rs_ready, t)
                last = dve.tensor_scalar(x_in[:, t - 1, :], x_in[:, t - 1, :], x_rs[:, t - 1:t], None, ALU.mult)
        last.then_inc(xn_ready.sem, 1)
        split(0, 0)
        dve.wait_ge(consts_in, 8 * 16)
        dve.wait_ge(pool_set, 1)
        for k in range(KT):
            evacuate_x(-1, k, first_banks[k % len(first_banks)])
        dve.tensor_tensor(lb_e[:, 0, :], lb_in[:, 0, :], lb_in[:, 1, :], ALU.max)
        dve.drain()
        dve.tensor_tensor(lb_e[:, 2, :], lb_in[:, 0, :], lb_e[:, 0, :], ALU.subtract)
        dve.tensor_tensor(lb_e[:, 3, :], lb_in[:, 1, :], lb_e[:, 0, :], ALU.subtract).then_inc(dve_set, 1)
        dve.wait_ge(act_set, 1)
        dve.tensor_tensor(lb_e[:, 1, :], lb_e[:, 0, :], lb_e[:, 1, :], ALU.add)
        dve.drain()
        dve.reciprocal(lb_e[:, 2, :], lb_e[:, 1, :])
        dve.drain()
        dve.tensor_tensor(lb[:], lb_e[:, 0, :], lb_e[:, 2, :], ALU.mult)
        dve.drain()
        dve.tensor_scalar(one_less_lb[:], lb[:], -1.0, 1.0, ALU.mult, ALU.add)

        with dve.Fori(0, NB) as b:
            use = 0
            for step in STEPS:
                kind = step[0]
                if kind == "split_lo":
                    split(b, step[1])
                elif kind == "proj" and chunk_name(step[1])[:2] == "WO":
                    n, g = step[1:]
                    c = n - len(CHUNKS)
                    if g == 0:
                        dve.wait_ge(xr_loaded[c % 2], b * 32 + 16 * (c // 2 + 1))
                    dve.wait_ge(pj_full.sem, pj_full.upto(b, GROUPS_TO[n] + g + 1))
                    dve.tensor_tensor(x_res[c % 2][:, g, :], x_res[c % 2][:, g, :], pj[(GROUPS_TO[n] + g) % 2][:, 0:WC], ALU.add).then_inc(res_done.sem, 1)
                elif kind == "qn1":
                    t = step[1]
                    dve.wait_ge(q_sq_ready.sem, q_sq_ready.upto(b, t + 1))
                    dve.tensor_reduce(q_ss[:, t, :], qk_sq[:], AX.X, ALU.add)
                    dve.drain()
                    dve.tensor_scalar(q_ss[:, t, :], q_ss[:, t, :], 1.0 / HD, EPS, ALU.mult, ALU.add).then_inc(q_ms_ready.sem, 1)
                elif kind == "qn2":
                    t = step[1]
                    q = qk[:, t, :, :]
                    dve.drain()
                    if t == 0:
                        dve.wait_ge(rope_loaded, b * 16 + 16)
                    dve.wait_ge(q_rs_ready.sem, q_rs_ready.upto(b, t + 1))
                    dve.tensor_tensor(q, q, q_rs[:, t, :, None].broadcast_to([P, SLOTS, HD]), ALU.mult)
                    dve.drain()
                    dve.tensor_tensor(q[:, 0:N_Q, 0:ROPE], q[:, 0:N_Q, 0:ROPE], qk_weight[:, 0:1, :].broadcast_to([P, N_Q, ROPE]), ALU.mult)
                    dve.tensor_tensor(q[:, N_Q:SLOTS, 0:ROPE], q[:, N_Q:SLOTS, 0:ROPE], qk_weight[:, 1:2, :].broadcast_to([P, N_KV, ROPE]), ALU.mult)
                    dve.drain()
                    half = ROPE // 2
                    cosines = rope[:, t:t + 1, 0:ROPE].broadcast_to([P, SLOTS, ROPE])
                    minus_sin = rope[:, t:t + 1, ROPE:ROPE + half].broadcast_to([P, SLOTS, half])
                    sin = rope[:, t:t + 1, ROPE + half:2 * ROPE].broadcast_to([P, SLOTS, half])
                    dve.tensor_tensor(rope_u[:], q[:, :, 0:ROPE], cosines, ALU.mult)
                    dve.tensor_tensor(rope_v[:, :, 0:half], q[:, :, half:ROPE], minus_sin, ALU.mult)
                    dve.tensor_tensor(rope_v[:, :, half:ROPE], q[:, :, 0:half], sin, ALU.mult)
                    dve.drain()
                    dve.tensor_tensor(q[:, :, 0:ROPE], rope_u[:], rope_v[:], ALU.add).then_inc(qk_ready.sem, 1)
                elif kind == "ha":
                    h = step[1]
                    dve.wait_ge(f_ready.sem, f_ready.upto(b, h + 1))
                    dve.tensor_scalar(f_gate[h][:], f_gate[h][:], one_less_lb[:, h:h + 1], lb[:, h:h + 1], ALU.mult, ALU.add).then_inc(fg_ready.sem, 1)
                elif kind == "hb":
                    h, s = step[1], step[1] % 2
                    dve.wait_ge(lf_ready.sem, lf_ready.upto(b, h + 1))
                    dve.tensor_scalar(f_gate[h][:], f_gate[h][:], -1.0, 1.0, ALU.mult, ALU.add)
                    dve.tensor_tensor_scan(t_b[:], not_start[:], t_a[:], 0.0, ALU.mult, ALU.add)
                    dve.drain()
                    chunks = t_b[:].rearrange("p (c s) -> p c s", s=CHUNK)
                    dve.tensor_tensor(t_a[:].rearrange("p (c s) -> p c s", s=CHUNK), chunks,
                                      chunks[:, :, CHUNK // 2:CHUNK // 2 + 1].broadcast_to([P, NC, CHUNK]), ALU.subtract)
                    if h >= 2:
                        dve.wait_ge(k_nat_ready.sem, k_nat_ready.upto(b, h - 1))
                    dve.tensor_tensor(k_end[s][:].rearrange("p (c s) -> p c s", s=CHUNK),
                                      chunks[:, :, CHUNK - 1:CHUNK].broadcast_to([P, NC, CHUNK]), chunks, ALU.subtract).then_inc(b_ready.sem, 1)
                elif kind == "hc":
                    h, s = step[1], step[1] % 2
                    dve.wait_ge(e_ready.sem, e_ready.upto(b, h + 1))
                    dve.tensor_tensor(q_in[s][:], q_in[s][:], q_h[h][:], ALU.mult)
                    dve.tensor_tensor(k_end[s][:], k_end[s][:], f_gate[h][:], ALU.mult)
                    dve.drain()
                    dve.tensor_tensor(f_gate[h][:], f_gate[h][:], t_a[:], ALU.mult)
                    dve.tensor_tensor(q_h[h][:], q_h[h][:], t_b[:], ALU.mult).then_inc(gates_ready.sem, 1)
                elif kind == "sm1":
                    u, s, kv = step[1], step[1] % 2, step[1] % 2
                    dve.wait_ge(sc_full.sem, sc_full.upto(b, u + 1))
                    dve.tensor_reduce(top[:, s, :], sc[kv][:].rearrange("p (i c) -> p i c", c=P), AX.X, ALU.max)
                    dve.drain()
                    dve.scalar_tensor_tensor(out=top[:, s, :], in0=top[:, s, :], scalar=HD ** -0.5, in1=sink[:, kv, :], op0=ALU.mult, op1=ALU.max)
                    dve.drain()
                    dve.tensor_scalar(neg_top[:, s, :], top[:, s, :], -1.0, None, ALU.mult)
                    dve.tensor_tensor(sink_less[:, s, :], sink[:, kv, :], top[:, s, :], ALU.subtract).then_inc(sink_less_ready.sem, 1)
                elif kind == "sm2":
                    u, s = step[1], step[1] % 2
                    dve.wait_ge(exp_ready.sem, exp_ready.upto(b, u + 1))
                    dve.tensor_tensor(denom[:, s, :], denom[:, s, :], sink_e[:, s, :], ALU.add)
                    dve.drain()
                    dve.reciprocal(denom[:, s, :], denom[:, s, :])
                    dve.drain()
                    dve.tensor_tensor(prob[s][:], prob[s][:], denom[:, s, :, None].broadcast_to([P, 4, P]), ALU.mult).then_inc(prob_ready.sem, 1)
                elif kind == "pv":
                    t = step[1]
                    dve.wait_ge(yA_hi_ready.sem, yA_hi_ready.upto(b, t + 1))
                    split_cols = "p j (c q) -> p j c q"
                    dve.tensor_tensor(yA_lo[:, :, t * P:(t + 1) * P].rearrange(split_cols, c=2),
                                      pvb[:].rearrange("p (c j q) -> p j c q", c=2, j=4),
                                      yA_hi[:, :, t * P:(t + 1) * P].rearrange(split_cols, c=2).bitcast(F32), ALU.subtract).then_inc(yA_ready.sem, 1)
                elif kind == "att":
                    h = step[1]
                    dve.wait_ge(att_full.sem, att_full.upto(b, h + 1))
                    dve.sem_inc(dve_waited, 1)
                    dve.copy_predicated(att_m[:], causal[:].broadcast_to([P, TT, P]), hb[:].rearrange("p (t c) -> p t c", c=P)).then_inc(att_ready.sem, 1)
                elif kind == "ds" and step[2] == 1:
                    h = step[1]
                    dve.wait_ge(tr_full.sem, tr_full.upto(b, use + 1))
                    dve.tensor_copy(state[:, 0, :], carry[:, h, :])
                    for c in range(NC):
                        dve.drain()
                        ps = tr[(use - 1 + c % 2) % 2][:, (c // 2) * P:(c // 2 + 1) * P]
                        last = dve.scalar_tensor_tensor(out=state[:, c + 1, :] if c < NC - 1 else carry[:, h, :], in0=state[:, c, :],
                                                        scalar=decay[:, h, c:c + 1], in1=ps, op0=ALU.mult, op1=ALU.add)
                    last.then_inc(state_ready.sem, 1)
                elif kind == "on1":
                    h = step[1]
                    dve.wait_ge(o_sq_ready.sem, o_sq_ready.upto(b, h + 1))
                    dve.tensor_scalar(o_ss[:], o_ss[:], 1.0 / P, EPS, ALU.mult, ALU.add).then_inc(o_ms_ready.sem, 1)
                elif kind == "on2":
                    h = step[1]
                    dve.wait_ge(o_rs_ready.sem, o_rs_ready.upto(b, h + 1))
                    dve.tensor_tensor(y_nat[:], hb[:].rearrange("p (t c) -> p t c", c=P), o_rs[:, :, None].broadcast_to([P, TT, P]), ALU.mult).then_inc(hb_read.sem, 1)
                elif kind == "on3":
                    h = step[1]
                    dve.drain()
                    dve.wait_ge(g_ready.sem, g_ready.upto(b, TT if h < 2 else 2 * TT))
                    dve.tensor_tensor(y_nat[:], y_nat[:], g_nat[:, :, h * P:(h + 1) * P], ALU.mult).then_inc(y_nat_ready.sem, 1)
                elif kind == "yt":
                    h = step[1]
                    dve.wait_ge(yH_hi_ready.sem, yH_hi_ready.upto(b, h + 1))
                    low_part(yH_lo[h][:], tr[use % 2][:], gnw[:, 0:1], yH_hi[h][:], yH_ready)
                elif kind == "n1a":
                    mean_square_x(b)
                elif kind == "n1b":
                    scale_x(b, step[1])
                elif kind == "xT":
                    evacuate_x(b, step[1], tr[use % 2])
                if kind in TR_KINDS:
                    use += 1
            dve.tensor_copy(mid_old[:], mid_ms[:, TT:])
            dve.wait_ge(mid_squared.sem, mid_squared.upto(b, 4 * TT))
            dve.tensor_reduce(mid_sum[:], mid_ss[:], AX.X, ALU.add)
            dve.drain()
            dve.tensor_copy(mid_ms[:, 0:(NB - 1) * TT], mid_old[:])
            dve.tensor_scalar(mid_ms[:, (NB - 1) * TT:], mid_sum[:], 1.0 / D, EPS, ALU.mult, ALU.add).then_inc(mid_ready.sem, 1)


def build_phase_b(nc, ctx, dram, x_mid, out, kept):
    def sem(name):
        return ctx.enter_context(nc.semaphore(name))

    def signal(name, per_pass, ahead=0):
        return Signal(nc, ctx, name, per_pass, ahead)

    ident, mid_ms = kept.ident, kept.mid_ms
    put = Places(nc, kept.end).put
    n2w, xn = kept.n2w, kept.xn
    neg_half = put("b_neg_half", [P, HT], F32)
    rs = put("b_rs", [P, NB * TT], F32)
    h_hi = put("b_h_hi", [P, KT, TH], F32R)
    h_lo = put("b_h_lo", [P, KT, TH], F32R)
    acc = put("b_acc", [P, HT, D], F32)
    gu_stage = [put(f"b_gu_stage{s}", [P, KT, 2 * P], F32) for s in range(2)]
    gu_hi = [put(f"b_gu_hi{s}", [P, KT, 2 * P], F32R) for s in range(2)]
    gu_lo = [put(f"b_gu_lo{s}", [P, KT, 2 * P], F32R) for s in range(2)]
    dn_stage = [put(f"b_dn_stage{s}", [P, D], F32) for s in range(2)]
    dn_hi = [put(f"b_dn_hi{s}", [P, D], F32R) for s in range(2)]
    dn_lo = [put(f"b_dn_lo{s}", [P, D], F32R) for s in range(2)]
    a_hi = [put(f"b_a_hi{s}", [P, TH], F32R) for s in range(2)]
    a_lo = [put(f"b_a_lo{s}", [P, TH], F32R) for s in range(2)]
    silu = [put(f"b_silu{s}", [P, 512], F32) for s in range(2)]
    a_full = silu

    gate_up = [ctx.enter_context(nc.psum_tensor(f"b_gate_up{s}", [P, D], F32)) for s in range(2)]
    gu = [gate_up[g // 2][:, (g % 2) * 512:(g % 2 + 1) * 512] for g in range(4)]
    wide = [ctx.enter_context(nc.psum_tensor(f"b_wide{s}", [P, D], F32)) for s in range(2)]

    n2w_in, xn_loaded, consts_set = kept.n2w_in, kept.xn_loaded, sem("b_consts_set")
    rs_ready = sem("b_rs_ready")
    gu_loaded = [sem(f"gu_loaded{s}") for s in range(2)]
    dn_loaded = [sem(f"dn_loaded{s}") for s in range(2)]
    acc_loaded = [sem(f"acc_loaded{s}") for s in range(2)]
    stored = [sem(f"stored{s}") for s in range(2)]
    gu_hi_ready = signal("gu_hi_ready", FT)
    gu_lo_ready = signal("gu_lo_ready", FT, 2)
    dn_hi_ready = signal("dn_hi_ready", FT)
    dn_lo_ready = signal("dn_lo_ready", FT, 2)
    xn_ready = signal("b_xn_ready", HT)
    xT_full = signal("b_xT_full", HT)
    h_hi_ready = signal("b_h_hi_ready", HT)
    h_ready = signal("b_h_ready", HT)
    gu_full = signal("gu_full", 4 * FT, 5)
    silu_ready = signal("silu_ready", 2 * FT, 2)
    a_full_ready = signal("a_full_ready", 2 * FT, 2)
    a_hi_ready = signal("a_hi_ready", 2 * FT)
    a_ready = signal("a_ready", 2 * FT, 2)
    dn_full = signal("dn_full", HT * FT, 17)
    acc_done = signal("acc_done", HT * FT, 2)

    def middle_tiles(eng, whole):
        with eng.Fori(0, (FT - 2) // 2) as i:
            whole(2 * i + 1, 1)
            whole(2 * i + 2, 0)

    def xT_bank(half, t):
        if half == 0:
            return gate_up[t % 2][:] if t < 4 else wide[t % 2][:]
        return gate_up[t // 4][:]

    def before_in_xT_bank(half, t):
        if half == 0:
            return t - 2 if t % 4 >= 2 else None
        return t - 1 if t % 4 else None

    mid = x_mid.rearrange("(h t p) d -> h p t d", h=2, p=P)
    out_v = out.rearrange("(h t p) d -> h p t d", h=2, p=P)

    def xn_slot(half, t):
        return (half * HT + t) % XN

    def load_xn(eng, half, t):
        s = xn_slot(half, t)
        eng.dma_start(xn[s][:], mid[half, :, t, :]).then_inc(xn_loaded[s], 16)

    blk = ctx.enter_context(nc.Block())

    @blk.sync
    def _(sp):
        def load_gu(half, j, s):
            sp.wait_ge(gu_lo_ready.sem, half * FT + (j + 1))
            sp.dma_start(gu_stage[s][:], dram["w_gu"][bass.ds(j, 1)].rearrange("o p k n -> p (o k) n")).then_inc(gu_loaded[s], 16)

        def load_dn(half, j, s):
            sp.wait_ge(dn_lo_ready.sem, half * FT + (j + 1))
            sp.dma_start(dn_stage[s][:], dram["w_dn"][bass.ds(j, 1)].rearrange("o p n -> p (o n)")).then_inc(dn_loaded[s], 16)

        def load_later_xn(half, *tiles):
            for t in tiles:
                sp.wait_ge(xT_full.sem, xT_full.upto(half, t - XN + 1))
                load_xn(sp, half, t)

        for half in range(2):
            if half == 0:
                load_gu(half, 0, 0)
                load_later_xn(half, 3, 4)
                load_dn(half, 0, 0)
                load_gu(half, 1, 1)
                load_later_xn(half, 5, 6, 7)
                load_dn(half, 1, 1)
                load_later_xn(1, 0, 1, 2)
            else:
                load_gu(half, 0, 0)
                load_dn(half, 0, 0)
                load_later_xn(half, 3)
                load_gu(half, 1, 1)
                load_later_xn(half, 4, 5, 6)
                load_dn(half, 1, 1)
                load_later_xn(half, 7)
            with sp.Fori(1, FT // 2) as i:
                for s in range(2):
                    load_gu(half, 2 * i + s, s)
                    load_dn(half, 2 * i + s, s)

    @blk.gpsimd
    def _(pool):
        pool.memset(neg_half[:], -0.5).then_inc(consts_set, 1)
        pool.wait_ge(consts_set, 1)
        for first, last in ((0, 2), (2, HT), (HT, 2 * HT)):
            pool.tensor_tensor(rs[:, first:last], mid_ms[:, first:last], neg_half[:, 0:last - first], ALU.pow).then_inc(rs_ready, 1)

        def load_acc(half, q):
            if half:
                pool.wait_ge(stored[q], 64 * half)
            pool.dma_start(acc[:, 4 * q:4 * q + 4, :], mid[half, :, 4 * q:4 * q + 4, :]).then_inc(acc_loaded[q], 16)

        def store(half, t):
            pool.wait_ge(acc_done.sem, acc_done.upto(half, HT * (FT - 1) + t + 1))
            pool.dma_start(out_v[half, :, t, :], acc[:, t, :]).then_inc(stored[t // 4], 16)

        for half in range(2):
            for t in range(HT):
                if half:
                    store(half - 1, t)
                if half and t == HT // 2:
                    load_acc(half, 0)
            if half == 0:
                pool.wait_ge(xT_full.sem, xT_full.upto(half, HT))
                load_acc(half, 0)
            load_acc(half, 1)
        for t in range(HT):
            store(1, t)
        for q in range(2):
            pool.wait_ge(stored[q], 128)

    @blk.scalar
    def _(act):
        for half in range(2):
            def split_gu(j, s):
                act.wait_ge(gu_loaded[s], half * (8 * FT) + (j - s) * 8 + 16)
                act.wait_ge(gu_full.sem, half * (4 * FT) + (j * 4 + 1))
                act.activation(gu_hi[s][:], gu_stage[s][:], ACT.Copy).then_inc(gu_hi_ready.sem, 1)

            def split_dn(j, s):
                act.wait_ge(dn_loaded[s], half * (8 * FT) + (j - s) * 8 + 16)
                act.wait_ge(dn_full.sem, half * (HT * FT) + (j * HT + 1))
                act.activation(dn_hi[s][:], dn_stage[s][:], ACT.Copy).then_inc(dn_hi_ready.sem, 1)

            def h_high(t, of_half):
                act.wait_ge(xT_full.sem, xT_full.upto(of_half, t + 1))
                act.activation(h_hi[:, :, t * P:(t + 1) * P], xT_bank(of_half, t).rearrange("p (k c) -> p k c", c=P), ACT.Copy).then_inc(h_hi_ready.sem, 1)

            def gate_silu(j, tb):
                act.wait_ge(gu_full.sem, gu_full.upto(half, 0) + (j * 4 + (2 * tb + 1)))
                act.wait_ge(a_ready.sem, half * (2 * FT) + (j * 2 + (tb + 1)))
                act.activation(silu[tb][:], gu[2 * tb], ACT.Silu).then_inc(silu_ready.sem, 1)

            def a_high(j, s, tb):
                act.wait_ge(a_full_ready.sem, a_full_ready.upto(half, 0) + (j * 2 + (tb + 1)))
                act.activation(a_hi[s][:, tb * 512:(tb + 1) * 512], a_full[tb][:], ACT.Copy).then_inc(a_hi_ready.sem, 1)

            def whole(j, s, inputs=()):
                if not (isinstance(j, int) and half * FT + j == 2 * FT - 1):
                    split_gu(j + 1, 1 - s)
                for tb in range(2):
                    gate_silu(j, tb)
                    if tb == 0:
                        split_dn(j, s)
                    for of_half, t in inputs[:2] if tb else ():
                        h_high(t, of_half)
                    a_high(j, s, tb)
                    for of_half, t in inputs[2:] if tb else ():
                        h_high(t, of_half)

            if half == 0:
                for t in range(6):
                    h_high(t, 0)
                    if t == 2:
                        split_gu(0, 0)
                gate_silu(0, 0)
                h_high(6, 0)
                h_high(7, 0)
                split_gu(1, 1)
                split_dn(0, 0)
                a_high(0, 0, 0)
                gate_silu(0, 1)
                a_high(0, 0, 1)
            else:
                h_high(4, 1)
                split_gu(1, 1)
                h_high(5, 1)
                gate_silu(0, 0)
                h_high(6, 1)
                split_dn(0, 0)
                h_high(7, 1)
                a_high(0, 0, 0)
                gate_silu(0, 1)
                a_high(0, 0, 1)
            middle_tiles(act, whole)
            whole(FT - 1, 1, () if half else [(1, 0), (1, 1), (1, 2), (1, 3)])

    @blk.tensor
    def _(pe):
        pe.sem_inc(gu_full.sem, 5)
        pe.sem_inc(dn_full.sem, 17)
        for half in range(2):
            def transpose_x(half, t):
                pe.wait_ge(xn_ready.sem, xn_ready.upto(half, t + 1))
                if before_in_xT_bank(half, t) is not None:
                    pe.wait_ge(h_ready.sem, h_ready.upto(half, before_in_xT_bank(half, t) + 1))
                elif half:
                    pe.wait_ge(a_full_ready.sem, a_full_ready.upto(half, t // 4 - 1))
                for k in range(KT):
                    last = pe.transpose(xT_bank(half, t)[:, k * P:(k + 1) * P], xn[xn_slot(half, t)][:, k * P:(k + 1) * P], ident[:])
                last.then_inc(xT_full.sem, 1)

            def down(of_half, j, s, t):
                if t % 4 == 0:
                    pe.wait_ge(a_ready.sem, of_half * (2 * FT) + (j * 2 + (t // 4 + 3)))
                if t == 0:
                    pe.wait_ge(dn_lo_ready.sem, of_half * FT + (j + 3))
                pe.wait_ge(acc_done.sem, of_half * (HT * FT) + (j * HT + (t + 1)))
                rows = slice(t * P, (t + 1) * P)
                for n in range(2):
                    cols = slice(n * 512, (n + 1) * 512)
                    pe.matmul(wide[t % 2][:, cols], a_hi[s][:, rows], dn_hi[s][:, cols], start=True, stop=False)
                    pe.matmul(wide[t % 2][:, cols], a_hi[s][:, rows], dn_lo[s][:, cols], start=False, stop=False)
                    last = pe.matmul(wide[t % 2][:, cols], a_lo[s][:, rows], dn_hi[s][:, cols], start=False, stop=True)
                last.then_inc(dn_full.sem, 1)

            def gate_or_up(j, s, g):
                if g == 0:
                    pe.wait_ge(gu_lo_ready.sem, half * FT + (j + 3))
                tb, up = g // 2, g % 2
                read = a_full_ready if up else silu_ready
                pe.wait_ge(read.sem, half * (2 * FT) + (j * 2 + (tb + 1)))
                cols = slice(up * P, (up + 1) * P)
                toks = slice(tb * 512, (tb + 1) * 512)
                last = three_passes(pe, gu[g],
                                    (lambda k: gu_hi[s][:, k, cols], lambda k: gu_lo[s][:, k, cols]),
                                    (lambda k: h_hi[:, k, toks], lambda k: h_lo[:, k, toks]))
                last.then_inc(gu_full.sem, 1)

            def whole(j, s, inputs=()):
                inputs = list(inputs)
                for g in range(4):
                    gate_or_up(j, s, g)
                    if g >= 2 and inputs:
                        transpose_x(*inputs.pop(0))
                    for t in (2 * g, 2 * g + 1):
                        down(half, j - 1, 1 - s, t)
                    if g >= 2 and inputs:
                        transpose_x(*inputs.pop(0))

            if half == 0:
                for t in range(HT):
                    transpose_x(0, t)
                    if t == 3:
                        pe.wait_ge(h_ready.sem, h_ready.upto(0, 4))
                        gate_or_up(0, 0, 0)
                    if t == 5:
                        gate_or_up(0, 0, 1)
                pe.wait_ge(h_ready.sem, h_ready.upto(0, HT))
                gate_or_up(0, 0, 2)
                gate_or_up(0, 0, 3)
            else:
                last_down = lambda t: down(0, FT - 1, 1, t)
                last_down(0)
                transpose_x(1, 4)
                last_down(1)
                pe.wait_ge(h_ready.sem, h_ready.upto(1, 4))
                gate_or_up(0, 0, 0)
                transpose_x(1, 5)
                last_down(2)
                last_down(3)
                transpose_x(1, 6)
                gate_or_up(0, 0, 1)
                transpose_x(1, 7)
                last_down(4)
                last_down(5)
                pe.wait_ge(h_ready.sem, h_ready.upto(1, HT))
                gate_or_up(0, 0, 2)
                last_down(6)
                last_down(7)
                gate_or_up(0, 0, 3)
            middle_tiles(pe, whole)
            whole(FT - 1, 1, () if half else [(1, 0), (1, 1), (1, 2), (1, 3)])
        for t in range(HT):
            down(1, FT - 1, 1, t)

    @blk.vector
    def _(dve):
        for s, n in ((gu_lo_ready, 2), (dn_lo_ready, 2), (acc_done, 2), (silu_ready, 2), (a_full_ready, 2), (a_ready, 2)):
            dve.sem_inc(s.sem, n)
        dve.wait_ge(n2w_in, 16)
        for half in range(2):
            def low(out, full, hi, ready):
                dve.tensor_tensor(out, full, hi.bitcast(F32), ALU.subtract).then_inc(ready.sem, 1)

            def split_gu(j, s):
                dve.wait_ge(gu_hi_ready.sem, half * FT + (j + 1))
                low(gu_lo[s][:], gu_stage[s][:], gu_hi[s][:], gu_lo_ready)

            def split_dn(j, s):
                dve.wait_ge(dn_hi_ready.sem, half * FT + (j + 1))
                low(dn_lo[s][:], dn_stage[s][:], dn_hi[s][:], dn_lo_ready)

            def scaled(of_half, t):
                if of_half == 0 and t in (0, 2) or of_half and t == 0:
                    dve.wait_ge(rs_ready, 3 if of_half else 1 + t // 2)
                at, slot = of_half * HT + t, xn_slot(of_half, t)
                dve.wait_ge(xn_loaded[slot], 16 * (at // XN + 1))
                dve.scalar_tensor_tensor(out=xn[slot][:], in0=xn[slot][:], scalar=rs[:, at:at + 1], in1=n2w[:], op0=ALU.mult, op1=ALU.mult).then_inc(xn_ready.sem, 1)

            def h_low(t, of_half):
                dve.wait_ge(h_hi_ready.sem, h_hi_ready.upto(of_half, t + 1))
                low(h_lo[:, :, t * P:(t + 1) * P], xT_bank(of_half, t).rearrange("p (k c) -> p k c", c=P), h_hi[:, :, t * P:(t + 1) * P], h_ready)

            def add(of_half, j, t):
                if t % 4 == 0:
                    dve.wait_ge(acc_loaded[t // 4], 16 * (of_half + 1))
                dve.wait_ge(dn_full.sem, of_half * (HT * FT) + (j * HT + (t + 18)))
                dve.tensor_tensor(acc[:, t, :], acc[:, t, :], wide[t % 2][:], ALU.add).then_inc(acc_done.sem, 1)

            def a_product(j, tb):
                dve.wait_ge(gu_full.sem, half * (4 * FT) + (j * 4 + (2 * tb + 2 + 5)))
                dve.wait_ge(silu_ready.sem, half * (2 * FT) + (j * 2 + (tb + 3)))
                dve.tensor_tensor(a_full[tb][:], silu[tb][:], gu[2 * tb + 1], ALU.mult).then_inc(a_full_ready.sem, 1)

            def a_low(j, s, tb):
                dve.wait_ge(a_hi_ready.sem, half * (2 * FT) + (j * 2 + (tb + 1)))
                low(a_lo[s][:, tb * 512:(tb + 1) * 512], a_full[tb][:], a_hi[s][:, tb * 512:(tb + 1) * 512], a_ready)

            def take(of_half, t):
                h_low(t, of_half)
                if XN <= t + XN - 1 < HT:
                    scaled(of_half, t + XN - 1)

            def whole(j, s, inputs=()):
                inputs = list(inputs)
                if not (isinstance(j, int) and half * FT + j == 2 * FT - 1):
                    split_gu(j + 1, 1 - s)
                for tb in range(2):
                    for t in range(4 * tb, 4 * tb + 4):
                        if tb and t % 2 == 0 and inputs:
                            take(*inputs.pop(0))
                        add(half, j - 1, t)
                        if t % 4 == 2:
                            a_low(j, s, tb)
                        if tb and t % 2 == 1 and inputs:
                            take(*inputs.pop(0))
                        if t % 4 == 1:
                            a_product(j, tb)
                            if tb == 0:
                                split_dn(j, s)

            if half == 0:
                for t in range(XN):
                    scaled(0, t)
                for t in range(HT):
                    h_low(t, 0)
                    if t == 2:
                        split_gu(0, 0)
                    for later in {1: (3,), 3: (4, 5), 4: (6,), 5: (7,)}.get(t, ()):
                        scaled(0, later)
                    if t == 5:
                        a_product(0, 0)
                split_gu(1, 1)
                split_dn(0, 0)
                a_low(0, 0, 0)
                a_product(0, 1)
                a_low(0, 0, 1)
                for t in range(XN):
                    scaled(1, t)
            else:
                beside = {0: 4, 1: 5, 3: 6}
                for t in range(4):
                    add(0, FT - 1, t)
                    if t == 1:
                        split_gu(1, 1)
                    if t in beside:
                        take(1, beside[t])
                a_product(0, 0)
                split_dn(0, 0)
                take(1, 7)
                a_low(0, 0, 0)
                for t in range(4, HT):
                    add(0, FT - 1, t)
                a_product(0, 1)
                a_low(0, 0, 1)
            middle_tiles(dve, whole)
            whole(FT - 1, 1, () if half else [(1, 0), (1, 1), (1, 2), (1, 3)])
        for t in range(HT):
            add(1, FT - 1, t)


def build(nc, dram, out):
    x_mid = nc.dram_tensor("x_mid", [SEQ, D], F32, kind="Internal").ap()
    with ExitStack() as both:
        kept = Kept(nc, both)
        with ExitStack() as ctx:
            build_phase_a(nc, ctx, dram, x_mid, kept)
        with ExitStack() as ctx:
            build_phase_b(nc, ctx, dram, x_mid, out, kept)


def rope_table():
    half = ROPE // 2
    inv = np.float32(500000.0) ** (-np.arange(half, dtype=np.float32) * np.float32(2.0) / np.float32(ROPE))
    angle = np.arange(SEQ, dtype=np.float32)[:, None] * inv[None, :].astype(np.float32)
    c, s = np.cos(angle).astype(np.float32), np.sin(angle).astype(np.float32)
    table = np.concatenate([c, c, -s, s], axis=1).reshape(NB, TT, P, 4 * half).transpose(0, 2, 1, 3)
    return np.ascontiguousarray(np.concatenate([table, table[:1]]))


def laid_out(x, w_in, w_out, norm1_w, norm2_w, q_norm_w, k_norm_w, attn_sinks, hgrn_lb_logits, hgrn_gnorm_w,
             w_gate_up, w_down):
    f = lambda a: np.asarray(a)
    x, w_in, w_out, w_gate_up, w_down = f(x)[0], f(w_in)[0], f(w_out)[0], f(w_gate_up)[0], f(w_down)[0]
    by_k = lambda w: w.reshape(KT, P, -1).transpose(1, 0, 2)
    heads = w_out[:N_Q * HD].reshape(2, 4, HD, D)
    rows = np.concatenate([heads.transpose(1, 0, 2, 3).reshape(N_Q * HD, D), w_out[N_Q * HD:]])
    whole = [by_k(w_in[:, c:c + n]) for _, c, n in CHUNKS if n == WC] + [by_k(rows[:, c:c + WC]) for c in range(0, D, WC)]
    sinks = f(attn_sinks)[0].reshape(N_KV, 1, 2, 2, 1)
    sinks = np.broadcast_to(sinks, (N_KV, 2, 2, 2, HD)).transpose(3, 4, 0, 1, 2).reshape(P, N_KV, 4)
    s = np.arange(P)
    causal = (s[:, None] // CHUNK == s[None, :] // CHUNK) & (s[:, None] <= s[None, :])
    qk_weight = np.stack([f(q_norm_w)[0], f(k_norm_w)[0]])
    return {
        "x_pad": np.concatenate([x, x[:TB]]).reshape(NB + 1, TB, D),
        "w_half": np.stack([by_k(w_in[:, c:c + n]) for _, c, n in CHUNKS if n < WC]),
        "w_whole": np.stack(whole),
        "ident": np.eye(P, dtype=np.float32),
        "causal": causal[:, None, :].astype(np.uint32),
        "qk_weight": np.broadcast_to(qk_weight[:, :ROPE], (P, 2, ROPE)),
        "qk_weight_T": np.tile(np.concatenate([np.ones((2, ROPE), np.float32), qk_weight[:, ROPE:]], axis=1).T, (2, 1)),
        "sink": sinks,
        "n1w": f(norm1_w)[0].reshape(KT, P).T,
        "n2w": np.broadcast_to(f(norm2_w)[0], (P, D)),
        "gnw": f(hgrn_gnorm_w)[0].reshape(P, 1),
        "lb": f(hgrn_lb_logits).reshape(2, HG, P).transpose(2, 0, 1),
        "rope": rope_table(),
        "w_gu": np.stack([np.concatenate([by_k(w_gate_up[:, j * P:(j + 1) * P]), by_k(w_gate_up[:, D_FF + j * P:D_FF + (j + 1) * P])], axis=2)
                          for j in range(FT)]),
        "w_dn": w_down.reshape(FT, P, D),
    }


def kernel(**inputs):
    import concourse.bacc as bacc
    from concourse.bass_utils import run_bass_kernel_spmd

    nc = bacc.Bacc("TRN2", target_bir_lowering=False, num_devices=1)
    arrays = {k: np.ascontiguousarray(a) for k, a in laid_out(**inputs).items()}
    dram = {k: nc.dram_tensor(k, a.shape, mybir.dt.from_np(a.dtype), kind="ExternalInput").ap() for k, a in arrays.items()}
    out = nc.dram_tensor("y", (SEQ, D), F32, kind="ExternalOutput").ap()
    build(nc, dram, out)
    r = run_bass_kernel_spmd(nc, [arrays], core_ids=[0])
    return r.results[0]["y"].reshape(1, SEQ, D)
```
